# Optimizing a Trainium2 kernel written in Bass

```python
import jax, jax.numpy as jnp
from jax import lax
import numpy as np

D_MODEL = 1024
BATCH = 1
SEQ = 256
DEPTH = 2

CHUNK = 64
HEAD_DIM = 64
N_MIXERS = 4
HEADS_PER_GROUP = 4
GROUP_W = HEADS_PER_GROUP * HEAD_DIM
D_MIX = N_MIXERS * GROUP_W
Q_BLOCK = 128
SWA_KV_HEADS = 2
SWA_WINDOW_CHUNKS = 2
KV_W_SWA = SWA_KV_HEADS * HEAD_DIM
CHUNK_LEFT = 8
REL_CLIP = 128
ALIBI_MAX_BIAS = 8.0
D_FF_DENSE = 2816
N_EXPERTS = 8
TOP_K = 2
D_FF_EXPERT = 3584
RMS_EPS = 1e-6

COL_SIZES = (GROUP_W, GROUP_W, GROUP_W,
             GROUP_W, KV_W_SWA, KV_W_SWA,
             GROUP_W, GROUP_W, GROUP_W,
             GROUP_W, GROUP_W, GROUP_W, HEADS_PER_GROUP)
IN_COLS = sum(COL_SIZES)

kernel_name = "hybrid_chunk_causal_parallel_heads_moe"

def rms_norm(x, g):
    xf = x.astype(jnp.float32)
    y = xf * lax.rsqrt(jnp.mean(xf * xf, axis=-1, keepdims=True) + RMS_EPS)
    return (y * g.astype(jnp.float32)).astype(x.dtype)

def _split_cols(h):
    outs, off = [], 0
    for n in COL_SIZES:
        outs.append(h[..., off:off + n])
        off += n
    return outs

def _heads(t, n):
    return t.reshape(t.shape[0], t.shape[1], n, HEAD_DIM)

def _alibi_slopes(n):
    return jnp.exp2(-ALIBI_MAX_BIAS * jnp.arange(1, n + 1, dtype=jnp.float32) / n)

def _chunk_band(x, n_chunks):
    Bn, S = x.shape[0], x.shape[1]
    nC = S // CHUNK
    xc = x.reshape((Bn, nC, CHUNK) + x.shape[2:])
    pad = jnp.zeros((Bn, n_chunks - 1) + xc.shape[2:], x.dtype)
    xp = jnp.concatenate([pad, xc], axis=1)
    band = jnp.stack([xp[:, i:i + nC] for i in range(n_chunks)], axis=2)
    return band.reshape((Bn, nC, n_chunks * CHUNK) + x.shape[2:])

def _band_valid(nC, n_chunks):
    key_chunk = jnp.arange(nC)[:, None] - (n_chunks - 1) + jnp.arange(n_chunks * CHUNK)[None, :] // CHUNK
    return key_chunk >= 0

def stick_breaking_attention(q, k, v):
    Bn, S, H, d = q.shape
    nb = S // Q_BLOCK
    scale = d ** -0.5
    qb = q.reshape(Bn, nb, Q_BLOCK, H, d).transpose(1, 0, 2, 3, 4)
    s_idx = jnp.arange(S)

    def block(args):
        qi, b = args
        t_idx = b * Q_BLOCK + jnp.arange(Q_BLOCK)
        z = jnp.einsum('bqhd,bshd->bhqs', qi, k).astype(jnp.float32) * scale
        strict = s_idx[None, :] < t_idx[:, None]
        log_1m = jnp.where(strict, jax.nn.log_sigmoid(-z), 0.0)
        suffix = lax.cumsum(log_1m, axis=3, reverse=True) - log_1m
        w = jnp.where(strict, jnp.exp(jax.nn.log_sigmoid(z) + suffix), 0.0)
        return jnp.einsum('bhqs,bshd->bqhd', w.astype(v.dtype), v)

    out = lax.map(block, (qb, jnp.arange(nb)))
    return out.transpose(1, 0, 2, 3, 4).reshape(Bn, S, H, d)

def sliding_window_sink_attention(q, k, v, sinks, slopes):
    Bn, S, Hq, d = q.shape
    Hkv = k.shape[2]
    G = Hq // Hkv
    nC = S // CHUNK
    n = SWA_WINDOW_CHUNKS
    W = n * CHUNK
    qc = q.reshape(Bn, nC, CHUNK, Hkv, G, d)
    kb = _chunk_band(k, n)
    vb = _chunk_band(v, n)
    rel = (n - 1) * CHUNK + jnp.arange(CHUNK)[:, None] - jnp.arange(W)[None, :]
    alibi = (-slopes[:, None, None] * jnp.abs(rel).astype(jnp.float32)[None]).reshape(Hkv, G, CHUNK, W)
    logits = jnp.einsum('bcqhgd,bckhd->bchgqk', qc, kb).astype(jnp.float32) * (d ** -0.5) + alibi
    logits = jnp.where(_band_valid(nC, n)[None, :, None, None, None, :], logits, -jnp.inf)
    sink = jnp.broadcast_to(sinks.astype(jnp.float32).reshape(1, 1, Hkv, G, 1, 1), logits.shape[:-1] + (1,))
    p = jax.nn.softmax(jnp.concatenate([logits, sink], axis=-1), axis=-1)[..., :W]
    out = jnp.einsum('bchgqk,bckhd->bcqhgd', p.astype(v.dtype), vb)
    return out.reshape(Bn, S, Hq, d)

def chunked_relpos_attention(q, k, v, rel_table):
    Bn, S, H, d = q.shape
    nC = S // CHUNK
    n = CHUNK_LEFT + 1
    W = n * CHUNK
    qc = q.reshape(Bn, nC, CHUNK, H, d)
    kb = _chunk_band(k, n)
    vb = _chunk_band(v, n)
    rel = (n - 1) * CHUNK + jnp.arange(CHUNK)[:, None] - jnp.arange(W)[None, :]
    idx = jnp.clip(rel, -REL_CLIP, REL_CLIP) + REL_CLIP
    bias = jnp.take(rel_table, idx, axis=1).astype(jnp.float32)
    logits = jnp.einsum('bcqhd,bckhd->bchqk', qc, kb).astype(jnp.float32) * (d ** -0.5) + bias
    logits = jnp.where(_band_valid(nC, n)[None, :, None, None, :], logits, -jnp.inf)
    p = jax.nn.softmax(logits, axis=-1)
    out = jnp.einsum('bchqk,bckhd->bcqhd', p.astype(v.dtype), vb)
    return out.reshape(Bn, S, H, d)

def forgetting_attention(q, k, v, log_f):
    Bn, S, H, d = q.shape
    nb = S // Q_BLOCK
    scale = d ** -0.5
    c = lax.cumsum(log_f, axis=1).transpose(0, 2, 1)
    qb = q.reshape(Bn, nb, Q_BLOCK, H, d).transpose(1, 0, 2, 3, 4)
    cb = c.reshape(Bn, H, nb, Q_BLOCK).transpose(2, 0, 1, 3)
    s_idx = jnp.arange(S)

    def block(args):
        qi, ci, b = args
        t_idx = b * Q_BLOCK + jnp.arange(Q_BLOCK)
        logits = jnp.einsum('bqhd,bshd->bhqs', qi, k).astype(jnp.float32) * scale
        logits = logits + ci[..., None] - c[:, :, None, :]
        logits = jnp.where(s_idx[None, :] <= t_idx[:, None], logits, -jnp.inf)
        p = jax.nn.softmax(logits, axis=-1)
        return jnp.einsum('bhqs,bshd->bqhd', p.astype(v.dtype), v)

    out = lax.map(block, (qb, cb, jnp.arange(nb)))
    return out.transpose(1, 0, 2, 3, 4).reshape(Bn, S, H, d)

def swiglu(h, w_gate, w_up, w_down):
    return (jax.nn.silu(h @ w_gate) * (h @ w_up)) @ w_down

def moe_swiglu(h, w_router, w_gate, w_up, w_down):
    Bn, S, D = h.shape
    t = h.reshape(-1, D)
    logits = (t @ w_router).astype(jnp.float32)
    top_val, top_idx = lax.top_k(logits, TOP_K)
    top_w = jax.nn.softmax(top_val, axis=-1)
    gates = jnp.sum(jax.nn.one_hot(top_idx, N_EXPERTS, dtype=jnp.float32) * top_w[..., None], axis=1)
    y = jnp.zeros_like(t)
    for e in range(N_EXPERTS):
        y = y + gates[:, e:e + 1].astype(t.dtype) * swiglu(t, w_gate[e], w_up[e], w_down[e])
    return y.reshape(Bn, S, D)

def setup_inputs(seed: int = 0) -> dict:
    key = jax.random.key(seed)
    ks = jax.random.split(key, 20)
    n_dense = (DEPTH + 1) // 2
    n_moe = DEPTH // 2
    nrm = jax.random.normal
    f32 = jnp.float32
    return {
        "x": nrm(ks[0], (BATCH, SEQ, D_MODEL), f32),
        "g_mix": 1.0 + 0.02 * nrm(ks[1], (DEPTH, D_MODEL), f32),
        "w_in": nrm(ks[2], (DEPTH, D_MODEL, IN_COLS), f32) * D_MODEL ** -0.5,
        "b_f": jnp.linspace(2.0, 6.0, HEADS_PER_GROUP, dtype=f32)[None, :] + 0.1 * nrm(ks[3], (DEPTH, HEADS_PER_GROUP), f32),
        "g_q": 1.0 + 0.02 * nrm(ks[4], (DEPTH, 3, HEAD_DIM), f32),
        "g_k": 1.0 + 0.02 * nrm(ks[5], (DEPTH, 3, HEAD_DIM), f32),
        "swa_sinks": 0.5 * nrm(ks[6], (DEPTH, HEADS_PER_GROUP), f32),
        "rel_bias": 0.5 * nrm(ks[7], (DEPTH, HEADS_PER_GROUP, 2 * REL_CLIP + 1), f32),
        "g_out": 1.0 + 0.02 * nrm(ks[8], (DEPTH, N_MIXERS, GROUP_W), f32),
        "w_out": nrm(ks[9], (DEPTH, D_MIX, D_MODEL), f32) * D_MIX ** -0.5,
        "g_ffn": 1.0 + 0.02 * nrm(ks[10], (DEPTH, D_MODEL), f32),
        "w_ff_gate": nrm(ks[11], (n_dense, D_MODEL, D_FF_DENSE), f32) * D_MODEL ** -0.5,
        "w_ff_up": nrm(ks[12], (n_dense, D_MODEL, D_FF_DENSE), f32) * D_MODEL ** -0.5,
        "w_ff_down": nrm(ks[13], (n_dense, D_FF_DENSE, D_MODEL), f32) * D_FF_DENSE ** -0.5,
        "w_router": nrm(ks[14], (n_moe, D_MODEL, N_EXPERTS), f32) * D_MODEL ** -0.5,
        "w_exp_gate": nrm(ks[15], (n_moe, N_EXPERTS, D_MODEL, D_FF_EXPERT), f32) * D_MODEL ** -0.5,
        "w_exp_up": nrm(ks[16], (n_moe, N_EXPERTS, D_MODEL, D_FF_EXPERT), f32) * D_MODEL ** -0.5,
        "w_exp_down": nrm(ks[17], (n_moe, N_EXPERTS, D_FF_EXPERT, D_MODEL), f32) * D_FF_EXPERT ** -0.5,
    }

def reference(x, g_mix, w_in, b_f, g_q, g_k, swa_sinks, rel_bias, g_out, w_out, g_ffn,
              w_ff_gate, w_ff_up, w_ff_down, w_router, w_exp_gate, w_exp_up, w_exp_down):
    H = HEADS_PER_GROUP
    slopes = _alibi_slopes(H)
    for l in range(DEPTH):
        h = rms_norm(x, g_mix[l])
        qa, ka, va, qb, kb, vb, qc, kc, vc, qd, kd, vd, fd = _split_cols(h @ w_in[l])
        oa = stick_breaking_attention(_heads(qa, H), _heads(ka, H), _heads(va, H))
        ob = sliding_window_sink_attention(rms_norm(_heads(qb, H), g_q[l, 0]),
                                           rms_norm(_heads(kb, SWA_KV_HEADS), g_k[l, 0]),
                                           _heads(vb, SWA_KV_HEADS), swa_sinks[l], slopes)
        oc = chunked_relpos_attention(rms_norm(_heads(qc, H), g_q[l, 1]),
                                      rms_norm(_heads(kc, H), g_k[l, 1]),
                                      _heads(vc, H), rel_bias[l])
        log_f = jax.nn.log_sigmoid(fd.astype(jnp.float32) + b_f[l].astype(jnp.float32))
        od = forgetting_attention(rms_norm(_heads(qd, H), g_q[l, 2]),
                                  rms_norm(_heads(kd, H), g_k[l, 2]),
                                  _heads(vd, H), log_f)
        Bn, S = x.shape[0], x.shape[1]
        groups = [rms_norm(o.reshape(Bn, S, GROUP_W), g_out[l, i]) for i, o in enumerate((oa, ob, oc, od))]
        x = x + jnp.concatenate(groups, axis=-1) @ w_out[l]
        h2 = rms_norm(x, g_ffn[l])
        if l % 2 == 0:
            i = l // 2
            x = x + swiglu(h2, w_ff_gate[i], w_ff_up[i], w_ff_down[i])
        else:
            i = l // 2
            x = x + moe_swiglu(h2, w_router[i], w_exp_gate[i], w_exp_up[i], w_exp_down[i])
    return x


_drawn_inputs = setup_inputs


def setup_inputs(seed=0):
    import zlib

    import numpy as np

    out = dict(_drawn_inputs(seed))
    spreads = {}
    factors = {'g_q': 2.763, 'swa_sinks': 4.963}
    for name, (base, spread) in spreads.items():
        noise = np.random.default_rng([zlib.crc32(name.encode()), seed]).standard_normal(out[name].shape)
        drawn = base * np.exp(spread * noise) if base else spread * noise
        out[name] = __import__('jax').numpy.asarray(drawn.astype(out[name].dtype))
    for name, factor in factors.items():
        out[name] = (out[name] * factor).astype(out[name].dtype)
    return out
```

```python
from contextlib import ExitStack

import numpy as np

import concourse.bass as bass
from concourse import mybir

ALU = mybir.AluOpType
ACT = mybir.ActivationFunctionType
AX = mybir.AxisListType
F32 = mybir.dt.float32
I32 = mybir.dt.int32
ds = bass.ds

P = 128
T = 256
NT = T // P
D = 1024
KD = D // P
L = 2
H = 4
HD = 64
GW = H * HD
EPS = 1e-6
SCALE = HD ** -0.5
NEG = -1e30
FD = 2816
FE = 3584
E = 8
CLIP = 128
RB = 2 * CLIP + 1
EXT = 384
SC = 3 * P

ORDER = ["D", "A", "C", "B"]
COL0 = {"A": 0, "B": 768, "C": 1280, "D": 2048}
COLS = {"A": 768, "B": 512, "C": 768, "D": 772}
CAT = {"A": 0, "B": 1, "C": 2, "D": 3}
QK = {"B": 0, "C": 1, "D": 2}
IN_COLS = 2820
WIN = {}
_at = 0
for _g in ORDER:
    WIN[_g] = _at
    _at += KD * COLS[_g]
WIN_END = _at
UNITS = {g: [(0, 512, 0), (0, 512, 1)] + ([] if g == "B" else [(512, COLS[g] - 512, 0), (512, COLS[g] - 512, 1)])
         for g in ORDER}

UNIT = 4096
SETS = [(8, 2, 3), (4, 5, 6), (0, 1, 7)]
FT = 512
NJ = 2

FILLS = [("x", i) for i in range(4)]
for _g in ORDER:
    FILLS += [(_g, "qk", 0), (_g, "qk", 1)]
    if _g != "A":
        FILLS += [(_g, "p", h) for h in range(H)]
    FILLS += [(_g, "o"), (_g, "oT")]
FILLS += [("y", i) for i in range(4)]
FILL = {name: n for n, name in enumerate(FILLS)}
NFILL = len(FILLS)
assert NFILL % 2 == 0
PUNIT = {}
for _g in ORDER:
    for _u in range(len(UNITS[_g])):
        PUNIT[_g, _u] = len(PUNIT)
NPU = len(PUNIT)
NPF = NPU + 2
SUSE = {n: i for i, n in enumerate(["Dsum", "D", "Az", "Aw", "C", "B", "out"])}
NSU = len(SUSE)

C_ID, C_UP, C_NEGLOW = 0, 128, 128 + 257
C_AMASK = C_NEGLOW + 256
C_ANEG, C_CAUSAL, C_BLOCK = C_AMASK + SC, C_AMASK + 2 * SC, C_AMASK + 3 * SC
C_ALIBI = C_AMASK + 4 * SC
C_IOTA = C_ALIBI + H * SC
C_REV = C_IOTA + P
C_ALL = C_REV + E
G_MIX, G_FFN, G_OUT, G_Q, G_K = 0, L * KD, 2 * L * KD, 3 * L * KD, 3 * L * KD + 3 * L
G_ALL = G_K + 3 * L


NORMED = {(g, u): n for n, (g, u) in enumerate((g, u) for g in ORDER if g != "A" for u in range(2))}
SOFT = [g for g in ORDER if g != "A"]
R_DIFF, R_MASK, R_ALL = 14, 15, 24


def shape_constants():
    c = np.zeros((P, C_ALL), np.float32)
    p = np.arange(P)[:, None]
    c[:, C_ID:C_ID + P] = p == np.arange(P)[None]
    c[:, C_UP:C_UP + 257] = p <= np.arange(257)[None] - 1
    c[:, C_NEGLOW:C_NEGLOW + 256] = -(p >= np.arange(256)[None] - P).astype(np.float32)
    col = np.arange(SC)[None]
    s, t = np.where(col < 256, p, p + P), np.where(col < 256, col, col - P)
    c[:, C_AMASK:C_AMASK + SC] = s < t
    c[:, C_ANEG:C_ANEG + SC] = np.where(s < t, 0.0, NEG)
    t, s = np.where(col < P, p, p + P), np.where(col < P, col, col - P)
    c[:, C_CAUSAL:C_CAUSAL + SC] = np.where(s <= t, 0.0, NEG)
    c[:, C_BLOCK:C_BLOCK + SC] = np.where(s // 64 <= t // 64, 0.0, NEG)
    back = t // 64 - s // 64
    for h in range(H):
        slope = 2.0 ** (-8.0 * (h + 1) / H)
        c[:, C_ALIBI + h * SC:C_ALIBI + (h + 1) * SC] = np.where((back >= 0) & (back <= 1), -slope * np.abs(t - s), NEG)
    c[:, C_IOTA:C_IOTA + P] = np.arange(P)[None]
    c[:, C_REV:C_REV + E] = E - np.arange(E)[None]
    return c


def trunk(nc, x_in, g_mix, w_in, b_f, g_q, g_k, swa_sinks, rel_bias, g_out, w_out, g_ffn,
          w_ff_gate, w_ff_up, w_ff_down, w_router, w_exp_gate, w_exp_up, w_exp_down, consts, out):
    with ExitStack() as ctx:
        def sb(name, shape, dt=F32):
            return ctx.enter_context(nc.sbuf_tensor(name, shape, dt))

        def sem(name):
            return ctx.enter_context(nc.semaphore(name))

        ext = nc.dram_tensor("ext_rel_bias", [L, H, EXT], F32).ap()

        wmem = sb("wmem", [P, 9 * UNIT])
        x = sb("x", [P, NT, D])
        xs = sb("xs", [P, NT, D])
        hT = sb("hT", [P, KD, T])
        con = sb("con", [P, C_ALL])
        gT = sb("gT", [P, G_ALL])
        grow = sb("grow", [G_ALL, P])
        qkT = sb("qkT", [P, 2, 4, T])
        vbuf = sb("vbuf", [P, 2, NT, GW])
        stage = sb("stage", [P, NT, 512])
        sq = sb("sq", [P, 512])
        obuf = sb("obuf", [P, NT, GW])
        osq = sb("osq", [P, NT, GW])
        bfr = sb("bfr", [P, L, H])
        sink = sb("sink", [P, L, NT, H])
        nsink = sb("nsink", [P, L, NT, H])
        wr = sb("wr", [P, KD, E])
        mhalf = sb("mhalf", [P, 8])
        ssx = sb("ssx", [P, NT])
        rx0 = sb("rx0", [P, NT])
        rx = sb("rx", [P, NT])
        ssq = sb("ssq", [P, 2, 8])
        rq0 = sb("rq0", [P, 2, 8])
        rq = sb("rq", [P, 2, 8])
        sso = sb("sso", [P, NT])
        ro0 = sb("ro0", [P, NT])
        ro = sb("ro", [P, NT])
        fraw = sb("fraw", [P, NT, H])
        fu = sb("fu", [P, NT, H])
        fa = sb("fa", [P, NT, H])
        fe = sb("fe", [P, NT, H])
        fl = sb("fl", [P, NT, H])
        fr = sb("fr", [P, NT, H])
        fsp = sb("fsp", [P, NT, H])
        nm = sb("nm", [P, NT * H])
        rsum = sb("rsum", [P, NT * H])
        rinv = sb("rinv", [P, NT * H])
        esink = sb("esink", [P, NT * H])
        lg = sb("lg", [P, NT, E])
        lg2 = sb("lg2", [P, NT, E])
        tmp = sb("tmp", [P, NT, E])
        one1 = sb("one1", [P, NT, E])
        one2 = sb("one2", [P, NT, E])
        mask = sb("mask", [P, NT, E])
        gates = sb("gates", [P, NT, E])
        slot = sb("slot", [P, NT, E])
        m1 = sb("m1", [P, NT])
        m2 = sb("m2", [P, NT])
        r1 = sb("r1", [P, NT])
        dm = sb("dm", [P, NT])
        em = sb("em", [P, NT])
        em1 = sb("em1", [P, NT])
        p1 = sb("p1", [P, NT])
        p2 = sb("p2", [P, NT])
        cnt = sb("cnt", [P, E], I32)
        ps = ctx.enter_context(nc.psum_tensor("ps", [P, 8, 512], F32))

        Lbuf = wmem[:, 0:H * SC].rearrange("p (h c) -> p h c", h=H)
        L2 = wmem[:, H * SC:2 * H * SC].rearrange("p (h c) -> p h c", h=H)
        pT = wmem[:, 2 * H * SC:3 * H * SC].rearrange("p (h c) -> p h c", h=H)
        tabC = wmem[:, 3 * H * SC:4 * H * SC].rearrange("p (h c) -> p h c", h=H)
        hankel = wmem[:, WIN_END:WIN_END + H * T].rearrange("p (h c) -> p h c", h=H)
        assert 5 * UNIT < WIN_END and WIN_END + H * T <= 6 * UNIT
        spb = wmem[:, 2 * H * SC:2 * H * SC + NT * H * P].rearrange("p (n c) -> p n c", c=P)
        assert 4 * H * SC <= KD * COLS["D"]
        oT = xs[:].rearrange("p a b -> p (a b)").rearrange("p (k t) -> p k t", t=T)
        qf = qkT[:].rearrange("p a b t -> p (a b t)")
        xTe = qf[:, 0:KD * P].rearrange("p (k t) -> p k t", t=P)
        sel = qf[:, 1024:1280].rearrange("p (a t) -> p a t", t=P)
        selg = qf[:, 1280:1536].rearrange("p (a t) -> p a t", t=P)
        back = qf[:, 1536:1792]
        ye = vbuf[:].rearrange("p a b c -> p (a b c)")
        hbuf = stage
        silu = [sq[:], obuf[:].rearrange("p a b -> p (a b)")]

        def win(g):
            return wmem[:, WIN[g]:WIN[g] + KD * COLS[g]].rearrange("p (k c) -> p k c", k=KD)

        def unit(u, k=KD, cols=FT):
            return wmem[:, u * UNIT:u * UNIT + k * cols].rearrange("p (k c) -> p k c", k=k)

        wo = wmem[:, 6 * UNIT:8 * UNIT].rearrange("p (k c) -> p k c", k=KD)

        s_x = sem("x_loaded")
        s_con = sem("consts_loaded")
        s_gain = sem("gain_rows_loaded")
        s_small = sem("biases_loaded")
        s_wr = sem("w_router_loaded")
        s_win = {g: sem(f"w_in_{g}_loaded") for g in ORDER}
        s_wo = [sem(f"w_out_{i}_loaded") for i in range(2)]
        s_unit = [sem(f"unit_{u}_loaded") for u in range(9)]
        s_ext = sem("rel_bias_extended")
        s_tabc = sem("rel_table_loaded")
        s_tabm = sem("rel_table_masked")
        s_out = sem("output_stored")
        gains_T = sem("gains_transposed")
        gains = sem("gains_ready")
        ssx_ready = sem("x_squares_summed")
        rx_part = sem("x_mean_ready")
        rx_ready = sem("x_rstd_ready")
        xs_ready = sem("x_scaled")
        tr_full = sem("transposes_done")
        tr_free = [sem(f"transposed_bank_{b}_read") for b in range(2)]
        pr_full = sem("projection_done")
        pr_free = [sem(f"projection_bank_{b}_read") for b in range(2)]
        sc_full = sem("scores_done")
        sc_free = sem("scores_read")
        sq_ready = sem("qk_squared")
        ssq_ready = sem("qk_squares_summed")
        rq_part = sem("qk_mean_ready")
        rq_ready = sem("qk_rstd_ready")
        vf_ready = sem("gate_logits_copied")
        f_dve = sem("forget_dve_step")
        f_act = sem("forget_act_step")
        spb_ready = sem("forget_spread")
        m_ready = sem("row_max_ready")
        mx_part = sem("row_max_part")
        p_ready = sem("exps_ready")
        es_ready = sem("sink_exp_ready")
        rs_part = sem("row_sum_with_sink")
        ri_ready = sem("row_inverse_ready")
        a_relu = sem("stick_relu_ready")
        a_abs = sem("stick_act_step")
        a_sp = sem("stick_softplus_step")
        o_ready = sem("group_output_step")
        sso_ready = sem("group_squares_summed")
        ro_part = sem("group_mean_ready")
        ro_ready = sem("group_rstd_ready")
        g_full = sem("ffn_gate_done")
        u_full = sem("ffn_up_done")
        silu_ready = sem("ffn_silu_ready")
        h_ready = sem("ffn_hidden_ready")
        d_full = sem("ffn_down_done")
        yT_dve = sem("ffn_out_read_dve")
        yT_act = sem("ffn_out_read_act")
        e_full = sem("ffn_out_transposed")
        x_added = sem("ffn_added")
        r_pe = sem("router_pe_step")
        r_dve = sem("router_dve_step")
        r_act = sem("router_act_step")
        sel_ready = sem("selection_ready")
        gx_full = sem("gather_done")
        gx_dve = sem("gather_read_dve")
        gx_act = sem("gather_read_act")
        ye_dve = sem("expert_out_read_dve")
        ye_act = sem("expert_out_read_act")

        def filled(eng, l, name):
            eng.wait_ge(tr_full, l * NFILL + FILL[name] + 1)

        def emptied(eng, l, name):
            n = FILL[name]
            eng.wait_ge(tr_free[n % 2], l * (NFILL // 2) + n // 2 + 1)

        def bank(name):
            return ps[:, 6 + FILL[name] % 2, :]

        def pbank(m):
            return ps[:, m % 2, :]

        DENSE_GROUPS = FD // 256
        EXPERT_GROUPS = FE // 256
        DENSE_LOOPS = (FD - FT // 2 - FT) // (2 * FT)
        EXPERT_LOOPS = (FE - FT) // (2 * FT)
        assert DENSE_GROUPS == 3 + 4 * DENSE_LOOPS and EXPERT_GROUPS == 2 + 4 * EXPERT_LOOPS
        VARIANTS = [128]

        def by_count(eng, n, run):
            def choose(widths):
                if not widths:
                    run(T)
                    return
                with eng.If(n < widths[0] + 1):
                    run(widths[0])
                with eng.Else():
                    choose(widths[1:])
                eng.end_ifs()
            choose(VARIANTS)

        def wait_from(eng, semaphore, value):
            if not isinstance(value, int) or value > 0:
                eng.wait_ge(semaphore, value)

        def scale_qk(eng, l, gi, g, t):
            filled(eng, l, (g, "qk", t))
            nb = 3 if g == "B" else 4
            if g == "A":
                sq_, sk_ = SCALE, 1.0
            else:
                n = l * 3 + QK[g]
                sq_, sk_ = gT[:, G_Q + n:G_Q + n + 1], gT[:, G_K + n:G_K + n + 1]
            for b0, b1, s in ((0, 2, sq_), (2, nb, sk_)):
                dst = qkT[:, gi % 2, b0:b1, t * P:(t + 1) * P]
                src = bank((g, "qk", t))[:, b0 * P:b1 * P].rearrange("p (b c) -> p b c", c=P)
                if t == 0:
                    ins = eng.tensor_scalar(dst, src, s, None, ALU.mult)
                else:
                    ins = eng.activation(dst, src, ACT.Copy, scale=s)
            ins.then_inc(tr_free[FILL[g, "qk", t] % 2], 1)

        block = ctx.enter_context(nc.Block())

        @block.sync
        def _(sp):
            def load_w_in(l, g):
                sp.dma_start(win(g), w_in[l, :, COL0[g]:COL0[g] + COLS[g]].rearrange("(k p) c -> p k c", p=P)) \
                    .then_inc(s_win[g], 16)

            def load_w_out(l, i):
                sp.dma_start(wo[:, 4 * i:4 * i + 4, :],
                             w_out[l, 512 * i:512 * (i + 1), :].rearrange("(k p) c -> p k c", p=P)).then_inc(s_wo[i], 16)

            def load_up(w, u, f0, cols=FT):
                sp.dma_start(unit(u, KD, cols), w[:, ds(f0, cols)].rearrange("(k p) c -> p k c", p=P)) \
                    .then_inc(s_unit[u], 16)

            def load_down(w, u, f0, rows=FT):
                sp.dma_start(unit(u, rows // P, D), w[ds(f0, rows), :].rearrange("(k p) c -> p k c", p=P)) \
                    .then_inc(s_unit[u], 16)

            def extend():
                rows = ext.rearrange("l h c -> (l h) c")
                sp.dma_start(rows[:, 0:RB - 1], rel_bias.rearrange("l h c -> (l h) c")[:, 1:RB]).then_inc(s_ext, 16)
                last = bass.AP(tensor=rel_bias.tensor, offset=rel_bias.offset + RB - 1, 
                               ap=[[RB, L * H], [0, EXT - RB + 1], [1, 1]])
                sp.dma_start(rows[:, RB - 1:EXT].unsqueeze(2), last).then_inc(s_ext, 16)

            def load_table(l):
                sp.wait_ge(s_ext, 16 * 2)
                sp.dma_start(hankel, bass.AP(tensor=ext.tensor, offset=ext.offset + l * H * EXT,
                                             ap=[[1, P], [EXT, H], [1, T]])).then_inc(s_tabc, 16)

            for t in range(NT):
                sp.dma_start(x[:, t, :], x_in[0, t * P:(t + 1) * P, :]).then_inc(s_x, 16)
            sp.dma_start(con[:], consts).then_inc(s_con, 16)
            sp.dma_start(grow[G_MIX:G_FFN, :], g_mix.rearrange("l (k c) -> (l k) c", c=P)).then_inc(s_gain, 16)
            sp.dma_start(grow[G_FFN:G_OUT, :], g_ffn.rearrange("l (k c) -> (l k) c", c=P)).then_inc(s_gain, 16)
            sp.dma_start(grow[G_OUT:G_Q, :], g_out.rearrange("l g (k c) -> (l g k) c", c=P)).then_inc(s_gain, 16)
            for half in range(2):
                sp.dma_start(grow[G_Q:G_K, half * HD:(half + 1) * HD], g_q.rearrange("l i c -> (l i) c")).then_inc(s_gain, 16)
                sp.dma_start(grow[G_K:G_ALL, half * HD:(half + 1) * HD], g_k.rearrange("l i c -> (l i) c")).then_inc(s_gain, 16)
            load_w_in(0, "D")
            sp.dma_start(bfr[:].rearrange("p l h -> p (l h)"),
                         bass.AP(tensor=b_f.tensor, offset=b_f.offset, ap=[[0, P], [1, L * H]])).then_inc(s_small, 16)
            for t in range(NT):
                sp.dma_start(sink[:, :, t, :],
                             bass.AP(tensor=swa_sinks.tensor, offset=swa_sinks.offset, ap=[[0, P], [H, L], [1, H]])) \
                    .then_inc(s_small, 16)
            load_w_in(0, "A")
            extend()
            load_table(0)
            load_w_in(0, "C")
            load_w_in(0, "B")
            load_w_out(0, 0)
            load_w_out(0, 1)
            sp.dma_start(wr[:], w_router[0].rearrange("(k p) e -> p k e", p=P)).then_inc(s_wr, 16)

            def first_step(l, gate, up, down, cols):
                if l:
                    sp.wait_ge(g_full, DENSE_GROUPS)
                load_up(gate, 8, 0, cols)
                sp.wait_ge(pr_full, l * NPF + PUNIT["A", 3] + 1)
                sp.wait_ge(pr_full, l * NPF + PUNIT["C", 3] + 1)
                load_up(up, 2, 0, cols)
                load_down(down, 3, 0, cols)

            def second_step(l, gate, up, down, f0):
                sp.wait_ge(pr_full, l * NPF + PUNIT["B", 1] + 1)
                sp.wait_ge(s_tabm, l + 1)
                load_up(gate, 4, f0)
                load_up(up, 5, f0)
                sp.wait_ge(sc_full, l * NSU + SUSE["out"] + 1)
                load_down(down, 6, f0)

            def third_step(gate, up, down, f0):
                load_up(gate, 0, f0)
                load_up(up, 1, f0)
                load_down(down, 7, f0)

            def step(s, gate, up, down, f0, free):
                g, u, d = SETS[s]
                sp.wait_ge(g_full, free)
                load_up(gate, g, f0)
                sp.wait_ge(u_full, free)
                load_up(up, u, f0)
                sp.wait_ge(d_full, free)
                load_down(down, d, f0)

            dense = (w_ff_gate[0], w_ff_up[0], w_ff_down[0])
            first_step(0, *dense, FT // 2)
            second_step(0, *dense, FT // 2)
            third_step(*dense, FT // 2 + FT)
            with sp.Fori(1, DENSE_LOOPS) as i:
                f0 = i * (2 * FT) + FT // 2
                step(1, *dense, f0, i * 4 - 1)
                step(2, *dense, f0 + FT, i * 4 + 1)
            step(0, *dense, FD - FT, 1)

            sp.wait_ge(g_full, DENSE_GROUPS - 2)
            sp.wait_ge(u_full, DENSE_GROUPS - 2)
            load_w_in(1, "D")
            load_w_in(1, "B")
            sp.wait_ge(d_full, DENSE_GROUPS)
            load_w_in(1, "A")
            load_table(1)
            load_w_in(1, "C")
            load_w_out(1, 0)
            load_w_out(1, 1)

            def expert(e):
                return w_exp_gate[0, e], w_exp_up[0, e], w_exp_down[0, e]

            first_step(1, *expert(0), FT)
            second_step(1, *expert(0), FT)
            third_step(*expert(0), 2 * FT)
            with sp.Fori(1, EXPERT_LOOPS) as i:
                f0 = i * (2 * FT) + FT
                step(1, *expert(0), f0, i * 4 + DENSE_GROUPS)
                step(2, *expert(0), f0 + FT, i * 4 + (DENSE_GROUPS + 2))
            with sp.Fori(1, E) as e:
                def weights(e):
                    return [w[0, ds(e, 1)].rearrange("a b c -> (a b) c") for w in (w_exp_gate, w_exp_up, w_exp_down)]
                before = sp.snap(e * EXPERT_GROUPS + DENSE_GROUPS)
                step(0, *weights(e), 0, before - (EXPERT_GROUPS - 2))
                step(1, *weights(e), FT, before - 2)
                step(2, *weights(e), 2 * FT, before)
                with sp.Fori(1, EXPERT_LOOPS) as i:
                    f0 = i * (2 * FT) + FT
                    step(1, *weights(e), f0, before + i * 4)
                    step(2, *weights(e), f0 + FT, before + (i * 4 + 2))
            sp.wait_ge(x_added, 4 * (1 + E))
            for t in range(NT):
                sp.dma_start(out[0, t * P:(t + 1) * P, :], x[:, t, :]).then_inc(s_out, 16)
            sp.wait_ge(s_out, 16 * NT)

        @block.tensor
        def _(pe):
            ident = con[:, C_ID:C_ID + P]
            up = con[:, C_UP:C_UP + 257]
            neglow = con[:, C_NEGLOW:C_NEGLOW + 256]

            def open_fill(l, name):
                n = FILL[name]
                if n >= 2:
                    pe.wait_ge(tr_free[n % 2], l * (NFILL // 2) + n // 2)

            def norm(l, name):
                for i in range(4):
                    open_fill(l, (name, i))
                    for kk in range(2):
                        k = 2 * i + kk
                        for t in range(NT):
                            if i == 0 and kk == 0:
                                pe.wait_ge(xs_ready, 2 * (2 * l + (name == "y")) + t + 1)
                            mm = pe.transpose(bank((name, i))[:, kk * T + t * P:kk * T + (t + 1) * P],
                                              xs[:, t, k * P:(k + 1) * P], ident)
                    mm.then_inc(tr_full, 1)

            def project(l, g, u):
                c0, cols, t = UNITS[g][u]
                m = PUNIT[g, u]
                if m == 0:
                    emptied(pe, l, ("x", 2))
                    emptied(pe, l, ("x", 3))
                if m >= 2:
                    pe.wait_ge(pr_free[m % 2], l * (NPF // 2) + m // 2)
                if u == 0:
                    pe.wait_ge(s_win[g], 16 * (l + 1))
                for k in range(KD):
                    mm = pe.matmul(pbank(m)[:, 0:cols], hT[:, k, t * P:(t + 1) * P], win(g)[:, k, c0:c0 + cols],
                                   start=(k == 0), stop=(k == KD - 1))
                mm.then_inc(pr_full, 1)

            def qk_transposes(l, gi, g):
                nb = 3 if g == "B" else 4
                for t in range(NT):
                    open_fill(l, (g, "qk", t))
                    pe.wait_ge(pr_free[t], l * (NPF // 2) + PUNIT[g, t] // 2 + 1)
                    for b in range(nb):
                        mm = pe.transpose(bank((g, "qk", t))[:, b * P:(b + 1) * P], stage[:, t, b * P:(b + 1) * P], ident)
                    mm.then_inc(tr_full, 1)

            def q_k(gi, g, h):
                if g == "B":
                    qb, lo = h % 2, HD * (h // 2)
                    kb = 2
                else:
                    qb, kb, lo = h // 2, 2 + h // 2, HD * (h % 2)
                return qkT[lo:lo + HD, gi % 2, qb, :], qkT[lo:lo + HD, gi % 2, kb, :]

            def wait_scores_free(l, use):
                n = SUSE[use]
                if n:
                    pe.wait_ge(sc_free, l * NSU + n)

            def forget_sums(l):
                pe.wait_ge(spb_ready, l + 1)
                wait_scores_free(l, "Dsum")
                for h in range(H):
                    pe.matmul(ps[:, 2 + h, 0:T], spb[:, h, :], up[:, 1:1 + T], start=True, stop=False)
                    mm = pe.matmul(ps[:, 2 + h, P:T], spb[:, H + h, :], up[:, 1:1 + P], start=False, stop=True)
                mm.then_inc(sc_full, 1)

            def scores(l, gi, g):
                emptied(pe, l, (g, "qk", 0))
                emptied(pe, l, (g, "qk", 1))
                wait_scores_free(l, "Az" if g == "A" else g)
                for h in range(H):
                    q, k = q_k(gi, g, h)
                    if g == "A":
                        pe.matmul(ps[:, 2 + h, 0:T], k[:, 0:P], q[:, 0:T], start=True, stop=True, skip_group_check=True)
                        mm = pe.matmul(ps[:, 2 + h, T:SC], k[:, P:T], q[:, P:T], start=False, stop=True,
                                       skip_group_check=True)
                    else:
                        pe.matmul(ps[:, 2 + h, 0:P], q[:, 0:P], k[:, 0:P], start=True, stop=True)
                        mm = pe.matmul(ps[:, 2 + h, P:SC], q[:, P:T], k[:, 0:T], start=True, stop=True)
                mm.then_inc(sc_full, 1)

            def stick_sums(l):
                pe.wait_ge(a_sp, 2 * (l + 1))
                pe.wait_ge(sc_free, l * NSU + SUSE["Aw"])
                for h in range(H):
                    o, sp_ = ps[:, 2 + h, :], L2[:, h, :]
                    pe.matmul(o[:, 0:T], neglow[:, P:2 * P], sp_[:, 0:T], start=False, stop=True, skip_group_check=True)
                    pe.matmul(o[:, P:T], neglow[:, 0:P], sp_[:, T:SC], start=False, stop=True, skip_group_check=True)
                    mm = pe.matmul(o[:, T:SC], neglow[:, P:2 * P], sp_[:, T:SC], start=False, stop=True,
                                   skip_group_check=True)
                mm.then_inc(sc_full, 1)

            def p_transposes(l, g):
                for h in range(H):
                    open_fill(l, (g, "p", h))
                    pe.wait_ge(p_ready, 4 * (4 * l + ORDER.index(g)) + h + 1)
                    for b in range(3):
                        mm = pe.transpose(bank((g, "p", h))[:, b * P:(b + 1) * P], Lbuf[:, h, b * P:(b + 1) * P], ident)
                    mm.then_inc(tr_full, 1)

            def values(l, gi, g):
                if g == "A":
                    pe.wait_ge(p_ready, 4 * (4 * l + gi) + H)
                    w = Lbuf
                else:
                    emptied(pe, l, (g, "p", 2))
                    emptied(pe, l, (g, "p", 3))
                    w = pT
                last = len(UNITS[g]) - 1
                for u in (last - 1, last):
                    m = PUNIT[g, u]
                    pe.wait_ge(pr_free[m % 2], l * (NPF // 2) + m // 2 + 1)
                open_fill(l, (g, "o"))
                for h in range(H):
                    hv = h // 2 if g == "B" else h
                    v = [vbuf[:, gi % 2, t, hv * HD:(hv + 1) * HD] for t in range(NT)]
                    o = [bank((g, "o"))[:, t * GW + h * HD:t * GW + (h + 1) * HD] for t in range(NT)]
                    pe.matmul(o[0], w[:, h, 0:P], v[0], start=True, stop=True)
                    pe.matmul(o[1], w[:, h, P:2 * P], v[0], start=True, stop=False)
                    mm = pe.matmul(o[1], w[:, h, 2 * P:SC], v[1], start=False, stop=True)
                mm.then_inc(tr_full, 1)

            def o_transposes(l, gi, g):
                open_fill(l, (g, "oT"))
                pe.wait_ge(o_ready, 4 * l + gi + 1)
                for kk in range(2):
                    for t in range(NT):
                        mm = pe.transpose(bank((g, "oT"))[:, kk * T + t * P:kk * T + (t + 1) * P],
                                          obuf[:, t, kk * P:(kk + 1) * P], ident)
                mm.then_inc(tr_full, 1)

            def out_project(l, t, groups):
                if groups[0] == ORDER[0]:
                    if t == 0:
                        for b in range(2):
                            pe.wait_ge(pr_free[(NPU + b) % 2], l * (NPF // 2) + (NPU + b) // 2)
                        for i in range(2):
                            pe.wait_ge(s_wo[i], 16 * (l + 1))
                    else:
                        wait_scores_free(l, "out")
                for g in groups:
                    emptied(pe, l, (g, "oT"))
                    for kk in range(2):
                        k = 2 * CAT[g] + kk
                        for half in range(2):
                            mm = pe.matmul(ps[:, 2 * t + half, :], oT[:, k, t * P:(t + 1) * P],
                                           wo[:, k, half * 512:(half + 1) * 512],
                                           start=(g == ORDER[0] and kk == 0), stop=(g == ORDER[-1] and kk == 1))
                            if g == ORDER[-1] and kk == 1 and t == 0:
                                mm.then_inc(pr_full, 1)
                if groups[-1] == ORDER[-1] and t == 1:
                    mm.then_inc(sc_full, 1)

            def attention(l):
                norm(l, "x")
                for gi, g in enumerate(ORDER + [None]):
                    before = ORDER[gi - 1] if gi else None
                    units = list(range(len(UNITS[g]))) if g else []

                    def some(n):
                        for _ in range(n):
                            if units:
                                project(l, g, units.pop(0))
                    if not gi:
                        some(4)
                        continue
                    some(1)
                    if before == "D":
                        forget_sums(l)
                    qk_transposes(l, gi - 1, before)
                    scores(l, gi - 1, before)
                    if g is None:
                        out_project(l, 0, ORDER[:-1])
                        out_project(l, 1, ORDER[:-1])
                    some(1)
                    if before == "A":
                        stick_sums(l)
                    some(1)
                    if before != "A":
                        p_transposes(l, before)
                    some(1)
                    values(l, gi - 1, before)
                    some(4)
                    o_transposes(l, gi - 1, before)
                out_project(l, 0, ORDER[-1:])
                out_project(l, 1, ORDER[-1:])
                norm(l, "y")
                emptied(pe, l, ("y", 2))
                emptied(pe, l, ("y", 3))

            def ffn_step(s, use, q, n, src, groups=NJ, first=False, last=False, after_half=False):
                ug, uu, ud = SETS[s]
                ft = 2 * groups
                wg, wu, wd = unit(ug, KD, ft * P), unit(uu, KD, ft * P), unit(ud, ft, D)
                for j in range(groups):
                    for w, u, bk, full, read in ((wg, ug, j, g_full, silu_ready), (wu, uu, 6 + j, u_full, h_ready)):
                        wait_from(pe, read, q + (j - 1 + int(after_half and j == 0)))
                        if j == 0:
                            pe.wait_ge(s_unit[u], (use + 1) * 16)
                        for f in range(2):
                            for k in range(KD):
                                mm = pe.matmul(ps[:, bk, f * n:(f + 1) * n], w[:, k, (2 * j + f) * P:(2 * j + f + 1) * P],
                                               src[:, k, 0:n], start=(k == 0), stop=(k == KD - 1))
                        mm.then_inc(full, 1)
                pe.wait_ge(s_unit[ud], (use + 1) * 16)
                for j in range(groups):
                    pe.wait_ge(h_ready, q + (j + 1))
                    for f in range(2):
                        for b in range(KD):
                            begin = first and j == 0 and f == 0 and b % 2 == 0
                            mm = pe.matmul(ps[:, 2 + b // 2, (b % 2) * T:(b % 2) * T + n],
                                           wd[:, 2 * j + f, b * P:(b + 1) * P], hbuf[:, j, f * n:(f + 1) * n],
                                           start=begin, stop=(last and j == groups - 1 and f == 1), skip_group_check=True)
                    mm.then_inc(d_full, 1)

            def back_all(c, last_inc=1):
                pe.wait_ge(yT_dve, c * 2 + 2)
                pe.wait_ge(yT_act, c * 2 + 2)
                for t in range(NT):
                    for half in range(2):
                        for b in range(4):
                            mm = pe.transpose(ps[:, 6 * t + half, b * P:(b + 1) * P],
                                              qf[:, (4 * half + b) * T + t * P:(4 * half + b) * T + (t + 1) * P], ident)
                        mm.then_inc(e_full, last_inc if (t, half) == (NT - 1, 1) else 1)

            pe.wait_ge(s_con, 16)
            pe.wait_ge(s_gain, 16 * 7)
            pe.transpose(ps[:, 0, 0:G_ALL], grow[:, :], con[0:G_ALL, C_ID:C_ID + G_ALL]).then_inc(gains_T, 1)

            attention(0)
            ffn_step(0, 0, 0, T, hT, groups=1, first=True)
            ffn_step(1, 0, 1, T, hT, after_half=True)
            ffn_step(2, 0, 3, T, hT)
            with pe.Fori(1, DENSE_LOOPS) as i:
                ffn_step(1, i, i * 4 + 1, T, hT)
                ffn_step(2, i, i * 4 + 3, T, hT)
            ffn_step(0, 1, DENSE_GROUPS - 2, T, hT, last=True)
            back_all(0)

            attention(1)
            pe.wait_ge(s_wr, 16)
            for t in range(NT):
                for k in range(KD):
                    mm = pe.matmul(ps[:, 0, t * E:(t + 1) * E], hT[:, k, t * P:(t + 1) * P], wr[:, k, :],
                                   start=(k == 0), stop=(k == KD - 1))
            mm.then_inc(r_pe, 1)
            pe.wait_ge(r_dve, R_MASK)
            pe.matmul(ps[:, 1, 0:E], up[:, 0:P], mask[:, 0, :], start=True, stop=True)
            pe.matmul(ps[:, 1, E:2 * E], up[:, P + 1:2 * P + 1], mask[:, 0, :], start=True, stop=False)
            pe.matmul(ps[:, 1, E:2 * E], up[:, 0:P], mask[:, 1, :], start=False, stop=True)
            pe.matmul(ps[:, 1, 2 * E:3 * E], up[:, P + 1:2 * P + 1], mask[:, 0, :], start=True, stop=False)
            pe.matmul(ps[:, 1, 2 * E:3 * E], up[:, P + 1:2 * P + 1], mask[:, 1, :], start=False, stop=True).then_inc(r_pe, 1)
            pe.wait_ge(r_dve, R_ALL)
            with pe.Fori(0, E) as e:
                n_e = pe.value_load(cnt[0:1, ds(e, 1)], min_val=0, max_val=T)
                before = pe.snap(e * EXPERT_GROUPS + DENSE_GROUPS)

                def run(n):
                    src = hT if n == T else xTe
                    pe.wait_ge(x_added, e * 4 + 4)
                    pe.wait_ge(sel_ready, e + 1)
                    if n < T:
                        for half in range(2):
                            for b in range(4):
                                for t in range(NT):
                                    mm = pe.matmul(ps[:, 6 + half, b * P:b * P + n],
                                                   xs[:, t, (4 * half + b) * P:(4 * half + b + 1) * P],
                                                   sel[:, t, 0:n], start=(t == 0), stop=(t == NT - 1))
                            mm.then_inc(gx_full, 1)
                        for t in range(NT):
                            mm = pe.transpose(ps[0:n, 0, t * P:(t + 1) * P], selg[:, t, 0:n], ident)
                        mm.then_inc(gx_full, 1)
                        pe.wait_ge(gx_dve, e + 1)
                        pe.wait_ge(gx_act, e + 1)
                    else:
                        pe.sem_inc(gx_full, 3)
                    ffn_step(0, e + 2, before, n, src, first=True)
                    with pe.Fori(0, EXPERT_LOOPS) as i:
                        use = e * EXPERT_LOOPS + i + 2
                        q = pe.snap(before + i * 4)
                        ffn_step(1, use, q + 2, n, src)
                        ffn_step(2, use, q + 4, n, src)
                    if n == T:
                        back_all(e + 1, last_inc=3)
                        return
                    pe.wait_ge(yT_dve, e * 2 + 4)
                    pe.wait_ge(yT_act, e * 2 + 4)
                    for half in range(2):
                        for b in range(4):
                            dst, src = ps[0:n, half, b * P:(b + 1) * P], xTe[:, 4 * half + b, 0:n]
                            if half == 0 and b == 0:
                                pe.matmul(dst, src, ident, start=True, stop=True)
                            else:
                                mm = pe.transpose(dst, src, ident)
                        mm.then_inc(e_full, 1)
                    pe.wait_ge(ye_dve, e + 1)
                    pe.wait_ge(ye_act, e + 1)
                    for t in range(NT):
                        for half in range(2):
                            pe.matmul(ps[:, 6 * (1 - t) + half, :], back[0:n, t * P:(t + 1) * P],
                                      ye[0:n, half * 512:(half + 1) * 512], start=True, stop=True).then_inc(e_full, 1)
                by_count(pe, n_e, run)

        @block.scalar
        def _(act):
            def norm(l, name):
                y = name == "y"
                if y:
                    act.wait_ge(pr_free[0], (l + 1) * (NPF // 2))
                    act.wait_ge(pr_free[1], (l + 1) * (NPF // 2))
                    act.wait_ge(sc_free, (l + 1) * NSU)
                elif l:
                    act.wait_ge(x_added, 4 * l)
                for t in range(NT):
                    if not y and not l:
                        act.wait_ge(s_x, 16 * NT)
                    act.activation(xs[:, t, :], x[:, t, :], ACT.Square, accum_out=ssx[:, t:t + 1]).then_inc(ssx_ready, 1)
                act.wait_ge(gains, 1)
                for i in (1, 3):
                    filled(act, l, (name, i))
                    for kk in range(2):
                        k = 2 * i + kk
                        c = (G_FFN if y else G_MIX) + l * KD + k
                        ins = act.activation(hT[:, k, :], bank((name, i))[:, kk * T:(kk + 1) * T], ACT.Copy,
                                             scale=gT[:, c:c + 1])
                    ins.then_inc(tr_free[1], 1)

            def read_unit(l, gi, g, u):
                m = PUNIT[g, u]
                act.wait_ge(pr_full, l * NPF + m + 1)
                if u >= 2:
                    if gi >= 2:
                        filled(act, l, (ORDER[gi - 2], "o"))
                    if g == "D":
                        act.activation(fraw[:, u - 2, :], pbank(m)[:, GW:GW + H], ACT.Copy)
                    act.activation(vbuf[:, gi % 2, u - 2, :], pbank(m)[:, 0:GW], ACT.Copy).then_inc(pr_free[m % 2], 1)
                elif g != "A":
                    cols = 384 if g == "B" else 512
                    n = NORMED[g, u] + l * len(NORMED)
                    if n:
                        act.wait_ge(ssq_ready, n)
                    act.activation(sq[:, 0:cols], pbank(m)[:, 0:cols], ACT.Square).then_inc(sq_ready, 1)

            def forget(l):
                act.wait_ge(f_dve, 3 * l + 1)
                act.activation(fa[:], fu[:], ACT.Abs).then_inc(f_act, 1)
                act.wait_ge(f_act, 3 * l + 1)
                act.activation(fe[:], fa[:], ACT.Exp, scale=-1.0).then_inc(f_act, 1)
                act.wait_ge(f_act, 3 * l + 2)
                act.activation(fl[:], fe[:], ACT.Ln, bias=1.0).then_inc(f_act, 1)

            def read_qk(l, gi, g):
                scale_qk(act, l, gi, g, 1)

            def softmax(l, gi, g):
                act.wait_ge(m_ready, 3 * l + SOFT.index(g) + 1)
                for h in range(H):
                    for t in range(NT):
                        c0, c1 = (0, P) if t == 0 else (P, SC)
                        n = t * H + h
                        ins = act.activation(Lbuf[:, h, c0:c1], Lbuf[:, h, c0:c1], ACT.Exp, bias=nm[:, n:n + 1],
                                             accum_out=rsum[:, n:n + 1])
                    ins.then_inc(p_ready, 1)
                if g == "B":
                    act.wait_ge(mx_part, 2 * (l + 1))
                    act.activation(esink[:], esink[:], ACT.Exp).then_inc(es_ready, 1)

            def stick_softplus(l):
                act.wait_ge(a_relu, l + 1)
                act.activation(Lbuf[:], ps[:, 2:2 + H, 0:SC], ACT.Abs).then_inc(sc_free, 1)
                act.wait_ge(sc_free, l * NSU + SUSE["Az"] + 1)
                act.activation(Lbuf[:], Lbuf[:], ACT.Exp, scale=-1.0).then_inc(a_abs, 1)
                act.wait_ge(a_abs, 2 * l + 1)
                act.activation(Lbuf[:], Lbuf[:], ACT.Ln, bias=1.0).then_inc(a_abs, 1)

            def stick_exp(l, gi):
                act.wait_ge(sc_free, l * NSU + SUSE["Aw"] + 1)
                act.activation(Lbuf[:], Lbuf[:], ACT.Exp).then_inc(p_ready, H)

            def read_p(l, g):
                for h in (1, 3):
                    filled(act, l, (g, "p", h))
                    act.activation(pT[:, h, :], bank((g, "p", h))[:, 0:SC], ACT.Copy).then_inc(tr_free[FILL[g, "p", h] % 2], 1)

            def read_oT(l, g):
                filled(act, l, (g, "oT"))
                for kk in range(2):
                    k = 2 * CAT[g] + kk
                    c = G_OUT + l * 8 + k
                    ins = act.activation(oT[:, k, :], bank((g, "oT"))[:, kk * T:(kk + 1) * T], ACT.Copy, scale=gT[:, c:c + 1])
                ins.then_inc(tr_free[FILL[g, "oT"] % 2], 1)

            def attention(l):
                norm(l, "x")
                for gi, g in enumerate(ORDER + [None]):
                    before = ORDER[gi - 1] if gi else None
                    units = list(range(len(UNITS[g]))) if g else []

                    def some(n):
                        for _ in range(n):
                            if units:
                                read_unit(l, gi, g, units.pop(0))
                    if not gi:
                        some(4)
                        forget(l)
                        continue
                    some(1)
                    read_qk(l, gi - 1, before)
                    if before == "A":
                        stick_softplus(l)
                    else:
                        softmax(l, gi - 1, before)
                    some(1)
                    if before == "A":
                        stick_exp(l, gi - 1)
                    some(1)
                    if before != "A":
                        read_p(l, before)
                    some(5)
                    read_oT(l, before)
                norm(l, "y")

            def ffn_step(q, n, groups=NJ, after_half=False):
                for j in range(groups):
                    act.wait_ge(g_full, q + (j + 1))
                    wait_from(act, h_ready, q + (j - 1 + int(after_half and j == 0)))
                    act.activation(silu[j][:, 0:2 * n], ps[:, j, 0:2 * n], ACT.Silu).then_inc(silu_ready, 1)

            def read_y(c, done, n):
                act.wait_ge(d_full, done)
                for i, b in enumerate((1, 3)):
                    if n == T:
                        dst = qf[:, b * 512:(b + 1) * 512]
                        src = ps[:, 2 + b, :]
                    else:
                        dst = xTe[:, 2 * b:2 * b + 2, 0:n]
                        src = ps[:, 2 + b, :].rearrange("p (a t) -> p a t", a=2)[:, :, 0:n]
                    act.activation(dst, src, ACT.Copy).then_inc(yT_act, 1)

            attention(0)
            ffn_step(0, T, groups=1)
            ffn_step(1, T, after_half=True)
            ffn_step(3, T)
            with act.Fori(1, DENSE_LOOPS) as i:
                ffn_step(i * 4 + 1, T)
                ffn_step(i * 4 + 3, T)
            ffn_step(DENSE_GROUPS - 2, T)
            read_y(0, DENSE_GROUPS, T)

            attention(1)
            act.wait_ge(r_dve, R_DIFF)
            act.activation(em[:], dm[:], ACT.Exp).then_inc(r_act, 1)
            act.wait_ge(r_dve, R_ALL)
            with act.Fori(0, E) as e:
                n_e = act.value_load(cnt[0:1, ds(e, 1)], min_val=0, max_val=T)
                before = act.snap(e * EXPERT_GROUPS + DENSE_GROUPS)

                def run(n):
                    if n < T:
                        act.wait_ge(gx_full, e * 3 + 2)
                        for b in range(4):
                            c = G_FFN + KD + 4 + b
                            ins = act.activation(xTe[:, 4 + b, 0:n], ps[:, 7, b * P:b * P + n], ACT.Copy, scale=gT[:, c:c + 1])
                        ins.then_inc(gx_act, 1)
                    else:
                        act.sem_inc(gx_act, 1)
                    ffn_step(before, n)
                    with act.Fori(0, EXPERT_LOOPS) as i:
                        q = act.snap(before + i * 4)
                        ffn_step(q + 2, n)
                        ffn_step(q + 4, n)
                    read_y(e + 1, before + EXPERT_GROUPS, n)
                    if n < T:
                        act.wait_ge(e_full, e * 6 + 6)
                        act.activation(ye[0:n, 512:1024], ps[0:n, 1, :], ACT.Copy).then_inc(ye_act, 1)
                    else:
                        act.sem_inc(ye_act, 1)
                by_count(act, n_e, run)

        @block.gpsimd
        def _(pool):
            pool.memset(mhalf[:], -0.5).then_inc(rx_part, 1)
            done = [1]

            def rstd(mean, total, scale, out_, part, ready, value):
                pool.tensor_scalar(mean, total, scale, EPS, ALU.mult, ALU.add).then_inc(part, 1)
                pool.wait_ge(part, value)
                n = mean.shape[-1]
                pool.tensor_tensor(out_, mean, mhalf[:, 0:n], ALU.pow).then_inc(ready, 1)

            def norm(l, name):
                n = 2 * l + (name == "y")
                pool.wait_ge(ssx_ready, NT * (n + 1))
                if not n:
                    pool.wait_ge(rx_part, 1)
                rstd(rx0[:], ssx[:], 1.0 / D, rx[:], rx_part, rx_ready, n + 2)

            def unit_rstd(l, g, u):
                n = NORMED[g, u] + l * len(NORMED)
                k = 6 if g == "B" else 8
                pool.wait_ge(ssq_ready, n + 1)
                rstd(rq0[:, u, 0:k], ssq[:, u, 0:k], 1.0 / HD, rq[:, u, 0:k], rq_part, rq_ready, n + 1)

            def group_rstd(l, gi):
                n = 4 * l + gi
                pool.wait_ge(sso_ready, NT * (n + 1))
                rstd(ro0[:], sso[:], 1.0 / GW, ro[:], ro_part, ro_ready, n + 1)

            for l in range(L):
                norm(l, "x")
                for gi, g in enumerate(ORDER + [None]):
                    if g is not None and g != "A":
                        unit_rstd(l, g, 0)
                    if g is not None and g != "A":
                        unit_rstd(l, g, 1)
                    if gi:
                        group_rstd(l, gi - 1)
                    if gi == 1:
                        pool.wait_ge(s_tabc, 16 * (l + 1))
                        pool.wait_ge(pr_full, l * NPF + PUNIT["D", 3] + 1)
                        for h in range(H):
                            for c0, c1 in ((0, P), (P, SC)):
                                keys = c1 - c0
                                backward = bass.AP(tensor=hankel.tensor, offset=hankel.offset + h * T + keys - 1,
                                                   ap=[list(hankel.ap[0]), [-1, keys]])
                                ins = pool.tensor_tensor(tabC[:, h, c0:c1], backward,
                                                         con[:, C_BLOCK + c0:C_BLOCK + c1], ALU.add)
                        ins.then_inc(s_tabm, 1)
                norm(l, "y")

        @block.vector
        def _(dve):
            def norm(l, name):
                n = 2 * l + (name == "y")
                dve.wait_ge(rx_ready, n + 1)
                for t in range(NT):
                    dve.tensor_scalar(xs[:, t, :], x[:, t, :], rx[:, t:t + 1], None, ALU.mult).then_inc(xs_ready, 1)
                for i in (0, 2):
                    filled(dve, l, (name, i))
                    for kk in range(2):
                        k = 2 * i + kk
                        c = (G_FFN if name == "y" else G_MIX) + l * KD + k
                        ins = dve.tensor_scalar(hT[:, k, :], bank((name, i))[:, kk * T:(kk + 1) * T], gT[:, c:c + 1],
                                                None, ALU.mult)
                    ins.then_inc(tr_free[0], 1)

            def spread(ap, n, width):
                return ap.unsqueeze(2).broadcast_to([P, n, width])

            def read_unit(l, gi, g, u):
                if u >= 2:
                    return
                m = PUNIT[g, u]
                dve.wait_ge(pr_full, l * NPF + m + 1)
                if g == "A":
                    filled(dve, l, (ORDER[gi - 1], "qk", u))
                    dve.tensor_copy(stage[:, u, :], pbank(m)[:, :]).then_inc(pr_free[m % 2], 1)
                    return
                n = NORMED[g, u] + l * len(NORMED)
                k = 6 if g == "B" else 8
                dve.wait_ge(sq_ready, n + 1)
                dve.tensor_reduce(ssq[:, u, 0:k], sq[:, 0:k * HD].rearrange("p (h c) -> p h c", c=HD), AX.X, ALU.add) \
                    .then_inc(ssq_ready, 1)
                if gi:
                    filled(dve, l, (ORDER[gi - 1], "qk", u))
                dve.wait_ge(rq_ready, n + 1)
                if g == "B":
                    for half in range(2):
                        src = pbank(m)[:, half * P:(half + 1) * P].rearrange("p (b c) -> p b c", c=HD)
                        dst = stage[:, u, 0:2 * P].rearrange("p (b a c) -> p b a c", b=2, a=2)[:, :, half, :]
                        dve.tensor_tensor(dst, src, spread(rq[:, u, 2 * half:2 * half + 2], 2, HD), ALU.mult)
                    dve.tensor_tensor(stage[:, u, 2 * P:3 * P].rearrange("p (h c) -> p h c", c=HD),
                                      pbank(m)[:, 2 * P:3 * P].rearrange("p (h c) -> p h c", c=HD),
                                      spread(rq[:, u, 4:6], 2, HD), ALU.mult)
                    filled(dve, l, (ORDER[gi - 2], "o"))
                    dve.tensor_copy(vbuf[:, gi % 2, u, 0:P], pbank(m)[:, 3 * P:4 * P]).then_inc(pr_free[m % 2], 1)
                else:
                    dve.tensor_tensor(stage[:, u, :].rearrange("p (h c) -> p h c", c=HD),
                                      pbank(m)[:, :].rearrange("p (h c) -> p h c", c=HD),
                                      spread(rq[:, u, :], 8, HD), ALU.mult).then_inc(pr_free[m % 2], 1)

            def forget(l):
                for m in (2, 3):
                    dve.wait_ge(pr_free[m % 2], l * (NPF // 2) + 2)
                dve.tensor_tensor(fu[:], fraw[:], bfr[:, l:l + 1, :].broadcast_to([P, NT, H]), ALU.add).then_inc(f_dve, 1)
                dve.wait_ge(f_dve, 3 * l + 1)
                dve.tensor_scalar(fr[:], fu[:], -1.0, 0.0, ALU.mult, ALU.max).then_inc(f_dve, 1)
                dve.wait_ge(f_dve, 3 * l + 2)
                dve.wait_ge(f_act, 3 * l + 3)
                dve.tensor_tensor(fsp[:], fr[:], fl[:], ALU.add).then_inc(f_dve, 1)
                dve.wait_ge(f_dve, 3 * l + 3)
                dve.tensor_copy(spb, spread(fsp[:].rearrange("p a b -> p (a b)"), NT * H, P)).then_inc(spb_ready, 1)

            def table_d(l):
                dve.wait_ge(sc_full, l * NSU + SUSE["Dsum"] + 1)
                for c0, c1 in ((0, P), (P, SC)):
                    ins = dve.tensor_tensor(L2[:, :, c0:c1], ps[:, 2:2 + H, 0:c1 - c0],
                                            con[:, C_CAUSAL + c0:C_CAUSAL + c1].unsqueeze(1).broadcast_to([P, H, c1 - c0]),
                                            ALU.add)
                ins.then_inc(sc_free, 1)
                dve.wait_ge(sc_free, l * NSU + SUSE["Dsum"] + 1)

            def softmax(l, gi, g):
                dve.wait_ge(sc_full, l * NSU + SUSE[g] + 1)
                if g == "C":
                    dve.wait_ge(s_tabm, l + 1)
                if g == "B":
                    table = con[:, C_ALIBI:C_ALIBI + H * SC].rearrange("p (h c) -> p h c", h=H)
                else:
                    table = {"D": L2, "C": tabC}[g]
                if gi:
                    filled(dve, l, (ORDER[gi - 1], "o"))
                dve.tensor_tensor(Lbuf, ps[:, 2:2 + H, 0:SC], table, ALU.add).then_inc(sc_free, 1)
                dve.wait_ge(sc_free, l * NSU + SUSE[g] + 1)
                dve.tensor_reduce(nm[:, 0:H], Lbuf[:, :, 0:P], AX.X, ALU.max, negate=True)
                ins = dve.tensor_reduce(nm[:, H:2 * H], Lbuf[:, :, P:SC], AX.X, ALU.max, negate=True)
                if g == "B":
                    ins.then_inc(mx_part, 1)
                    dve.wait_ge(mx_part, 2 * l + 1)
                    ns = nsink[:, l, :, :].rearrange("p a b -> p (a b)")
                    dve.tensor_tensor(nm[:], nm[:], ns, ALU.min).then_inc(m_ready, 1)
                    dve.wait_ge(m_ready, 3 * l + 3)
                    dve.tensor_tensor(esink[:], nm[:], sink[:, l, :, :].rearrange("p a b -> p (a b)"), ALU.add) \
                        .then_inc(mx_part, 1)
                else:
                    ins.then_inc(m_ready, 1)

            def stick_relu(l):
                dve.wait_ge(sc_full, l * NSU + SUSE["Az"] + 1)
                dve.tensor_scalar(L2, ps[:, 2:2 + H, 0:SC], 0.0, None, ALU.max).then_inc(a_relu, 1)

            def read_p(l, g):
                for h in (0, 2):
                    filled(dve, l, (g, "p", h))
                    dve.tensor_copy(pT[:, h, :], bank((g, "p", h))[:, 0:SC]).then_inc(tr_free[FILL[g, "p", h] % 2], 1)

            def inverse(l, g):
                n = 3 * l + SOFT.index(g)
                dve.wait_ge(p_ready, 4 * (4 * l + ORDER.index(g)) + H)
                if g == "B":
                    dve.wait_ge(es_ready, l + 1)
                    dve.tensor_tensor(rsum[:], rsum[:], esink[:], ALU.add).then_inc(rs_part, 1)
                    dve.wait_ge(rs_part, l + 1)
                dve.reciprocal(rinv[:], rsum[:]).then_inc(ri_ready, 1)
                dve.wait_ge(ri_ready, n + 1)

            def group_out(l, gi, g):
                filled(dve, l, (g, "o"))
                if gi:
                    filled(dve, l, (ORDER[gi - 1], "oT"))
                o = obuf[:].rearrange("p a (h c) -> p (a h) c", c=HD)
                b = FILL[g, "o"] % 2
                src = bank((g, "o"))[:, :].rearrange("p (n c) -> p n c", c=HD)
                if g == "A":
                    dve.tensor_copy(o, src).then_inc(tr_free[b], 1)
                else:
                    dve.tensor_tensor(o, src, spread(rinv[:], 8, HD), ALU.mult).then_inc(tr_free[b], 1)
                emptied(dve, l, (g, "o"))
                for t in range(NT):
                    dve.tensor_tensor_reduce(out=osq[:, t, :], in0=obuf[:, t, :], in1=obuf[:, t, :], scale=1.0, scalar=0.0,
                                             op0=ALU.mult, op1=ALU.add, accum_out=sso[:, t:t + 1]).then_inc(sso_ready, 1)
                dve.wait_ge(ro_ready, 4 * l + gi + 1)
                for t in range(NT):
                    ins = dve.tensor_scalar(obuf[:, t, :], obuf[:, t, :], ro[:, t:t + 1], None, ALU.mult)
                ins.then_inc(o_ready, 1)

            def add_out(l):
                for half in range(2):
                    dve.wait_ge(pr_full, l * NPF + NPU + half + 1)
                    dve.tensor_tensor(x[:, 0, half * 512:(half + 1) * 512], ps[:, half, :],
                                      x[:, 0, half * 512:(half + 1) * 512], ALU.add).then_inc(pr_free[half], 1)
                dve.wait_ge(sc_full, (l + 1) * NSU)
                dve.tensor_tensor(x[:, 1, 0:512], ps[:, 2, :], x[:, 1, 0:512], ALU.add)
                dve.tensor_tensor(x[:, 1, 512:D], ps[:, 3, :], x[:, 1, 512:D], ALU.add).then_inc(sc_free, 1)

            def attention(l):
                norm(l, "x")
                for gi, g in enumerate(ORDER + [None]):
                    before = ORDER[gi - 1] if gi else None
                    units = list(range(len(UNITS[g]))) if g else []

                    def some(n):
                        for _ in range(n):
                            if units:
                                read_unit(l, gi, g, units.pop(0))
                    if not gi:
                        some(4)
                        forget(l)
                        continue
                    if before == "D":
                        table_d(l)
                    scale_qk(dve, l, gi - 1, before, 0)
                    if before == "A":
                        stick_relu(l)
                        stick_softplus(l)
                    else:
                        softmax(l, gi - 1, before)
                    some(2)
                    if before == "A":
                        stick_logits(l, gi - 1)
                    else:
                        read_p(l, before)
                        inverse(l, before)
                    group_out(l, gi - 1, before)
                add_out(l)
                norm(l, "y")

            def stick_softplus(l):
                m = con[:, C_AMASK:C_AMASK + SC].unsqueeze(1).broadcast_to([P, H, SC])
                dve.wait_ge(a_abs, 2 * (l + 1))
                dve.tensor_tensor(L2, L2, Lbuf, ALU.add).then_inc(a_sp, 1)
                dve.wait_ge(a_sp, 2 * l + 1)
                dve.tensor_tensor(L2, L2, m, ALU.mult).then_inc(a_sp, 1)

            def stick_logits(l, gi):
                m = con[:, C_ANEG:C_ANEG + SC].unsqueeze(1).broadcast_to([P, H, SC])
                dve.wait_ge(sc_full, l * NSU + SUSE["Aw"] + 1)
                dve.tensor_tensor(Lbuf, ps[:, 2:2 + H, 0:SC], m, ALU.add).then_inc(sc_free, 1)
                dve.wait_ge(sc_free, l * NSU + SUSE["Aw"] + 1)

            def ffn_step(q, n, groups=NJ, after_half=False):
                for j in range(groups):
                    dve.wait_ge(silu_ready, q + (j + 1))
                    dve.wait_ge(u_full, q + (j + 1))
                    wait_from(dve, d_full, q + (j - 1 + int(after_half and j == 0)))
                    dve.tensor_tensor(hbuf[:, j, 0:2 * n], ps[:, 6 + j, 0:2 * n], silu[j][:, 0:2 * n], ALU.mult) \
                        .then_inc(h_ready, 1)

            def read_y(done, n):
                dve.wait_ge(d_full, done)
                for b in (0, 2):
                    if n == T:
                        dst, src = qf[:, b * 512:(b + 1) * 512], ps[:, 2 + b, :]
                    else:
                        dst = xTe[:, 2 * b:2 * b + 2, 0:n]
                        src = ps[:, 2 + b, :].rearrange("p (a t) -> p a t", a=2)[:, :, 0:n]
                    dve.tensor_copy(dst, src).then_inc(yT_dve, 1)

            def router():
                rev = con[:, C_REV:C_REV + E].unsqueeze(1).broadcast_to([P, NT, E])
                count = [0]

                def done(ins):
                    count[0] += 1
                    ins.then_inc(r_dve, 1)
                    dve.wait_ge(r_dve, count[0])

                def first_largest(values, top, onehot):
                    done(dve.tensor_reduce(top[:], values[:], AX.X, ALU.max))
                    done(dve.tensor_tensor(tmp[:], values[:], spread(top[:], NT, E), ALU.is_equal))
                    done(dve.tensor_tensor(tmp[:], tmp[:], rev, ALU.mult))
                    done(dve.tensor_reduce(r1[:], tmp[:], AX.X, ALU.max))
                    done(dve.tensor_tensor(onehot[:], rev, spread(r1[:], NT, E), ALU.is_equal))

                dve.wait_ge(r_pe, 1)
                done(dve.tensor_copy(lg[:], ps[:, 0, 0:NT * E].rearrange("p (a e) -> p a e", e=E)))
                first_largest(lg, m1, one1)
                done(dve.tensor_scalar(tmp[:], one1[:], NEG, None, ALU.mult))
                done(dve.tensor_tensor(lg2[:], lg[:], tmp[:], ALU.add))
                first_largest(lg2, m2, one2)
                done(dve.tensor_tensor(dm[:], m2[:], m1[:], ALU.subtract))
                assert count[0] == R_DIFF
                done(dve.tensor_tensor(mask[:], one1[:], one2[:], ALU.add))
                assert count[0] == R_MASK
                dve.wait_ge(r_act, 1)
                done(dve.tensor_scalar(em1[:], em[:], 1.0, None, ALU.add))
                done(dve.reciprocal(p1[:], em1[:]))
                done(dve.tensor_tensor(p2[:], em[:], p1[:], ALU.mult))
                done(dve.tensor_tensor(gates[:], one1[:], spread(p1[:], NT, E), ALU.mult))
                done(dve.tensor_tensor(tmp[:], one2[:], spread(p2[:], NT, E), ALU.mult))
                done(dve.tensor_tensor(gates[:], gates[:], tmp[:], ALU.add))
                dve.wait_ge(r_pe, 2)
                done(dve.scalar_tensor_tensor(out=slot[:], in0=ps[:, 1, 0:NT * E].rearrange("p (a e) -> p a e", e=E),
                                              scalar=1.0, in1=mask[:], op0=ALU.add, op1=ALU.mult))
                done(dve.tensor_scalar(slot[:], slot[:], -1.0, None, ALU.add))
                done(dve.tensor_copy(cnt[:], ps[:, 1, NT * E:(NT + 1) * E]))
                assert count[0] == R_ALL

            dve.wait_ge(gains_T, 1)
            dve.tensor_copy(gT[:], ps[:, 0, 0:G_ALL]).then_inc(gains, 1)
            dve.wait_ge(gains, 1)
            dve.tensor_scalar(gT[:, G_Q:G_K], gT[:, G_Q:G_K], SCALE, None, ALU.mult).then_inc(gains, 1)
            dve.wait_ge(s_small, 16 * 3)
            dve.tensor_scalar(nsink[:], sink[:], -1.0, None, ALU.mult).then_inc(gains, 1)
            dve.wait_ge(gains, 3)

            attention(0)
            ffn_step(0, T, groups=1)
            ffn_step(1, T, after_half=True)
            ffn_step(3, T)
            with dve.Fori(1, DENSE_LOOPS) as i:
                ffn_step(i * 4 + 1, T)
                ffn_step(i * 4 + 3, T)
            ffn_step(DENSE_GROUPS - 2, T)
            read_y(DENSE_GROUPS, T)
            for t in range(NT):
                for half in range(2):
                    xh = x[:, t, half * 512:(half + 1) * 512]
                    dve.wait_ge(e_full, 2 * t + half + 1)
                    dve.tensor_tensor(xh, ps[:, 6 * t + half, :], xh, ALU.add).then_inc(x_added, 1)

            attention(1)
            router()
            with dve.Fori(0, E) as e:
                n_e = dve.value_load(cnt[0:1, ds(e, 1)], min_val=0, max_val=T)
                before = dve.snap(e * EXPERT_GROUPS + DENSE_GROUPS)

                def run(n):
                    iota = con[:, C_IOTA:C_IOTA + P]
                    if n < T:
                        for t in range(NT):
                            at, gate = slot[:, t, ds(e, 1)], gates[:, t, ds(e, 1)]
                            dve.tensor_scalar(sel[:, t, 0:n], iota[:, 0:n], at, None, ALU.is_equal)
                            ins = dve.tensor_scalar(selg[:, t, 0:n], iota[:, 0:n], at, gate, ALU.is_equal, ALU.mult)
                        ins.then_inc(sel_ready, 1)
                        dve.wait_ge(gx_full, e * 3 + 1)
                        for b in range(4):
                            c = G_FFN + KD + b
                            dve.tensor_scalar(xTe[:, b, 0:n], ps[:, 6, b * P:b * P + n], gT[:, c:c + 1], None, ALU.mult)
                        dve.wait_ge(gx_full, e * 3 + 3)
                        dve.tensor_copy(back[0:n, :], ps[0:n, 0, 0:T]).then_inc(gx_dve, 1)
                    else:
                        dve.sem_inc(sel_ready, 1)
                        dve.sem_inc(gx_dve, 1)
                    ffn_step(before, n)
                    with dve.Fori(0, EXPERT_LOOPS) as i:
                        q = dve.snap(before + i * 4)
                        ffn_step(q + 2, n)
                        ffn_step(q + 4, n)
                    read_y(before + EXPERT_GROUPS, n)
                    if n < T:
                        dve.wait_ge(e_full, e * 6 + 5)
                        dve.tensor_copy(ye[0:n, 0:512], ps[0:n, 0, :]).then_inc(ye_dve, 1)
                    else:
                        dve.sem_inc(ye_dve, 1)
                    for t in range(NT):
                        for half in range(2):
                            xh = x[:, t, half * 512:(half + 1) * 512]
                            k = 2 * t + half
                            if n < T:
                                dve.wait_ge(e_full, e * 6 + (7 + k))
                                dve.tensor_tensor(xh, ps[:, 6 * (1 - t) + half, :], xh, ALU.add).then_inc(x_added, 1)
                            else:
                                dve.wait_ge(e_full, e * 6 + (5 + k if k < 3 else 10))
                                dve.scalar_tensor_tensor(out=xh, in0=ps[:, 6 * t + half, :], scalar=gates[:, t, ds(e, 1)],
                                                         in1=xh, op0=ALU.mult, op1=ALU.add).then_inc(x_added, 1)
                by_count(dve, n_e, run)


_INS = ["x", "g_mix", "w_in", "b_f", "g_q", "g_k", "swa_sinks", "rel_bias", "g_out", "w_out", "g_ffn",
        "w_ff_gate", "w_ff_up", "w_ff_down", "w_router", "w_exp_gate", "w_exp_up", "w_exp_down"]
_OUTS = [((1, 256, 1024), "float32")]


def kernel(**inputs):
    import numpy as _np
    import concourse.bacc as _bacc
    from concourse import mybir as _mybir
    from concourse.bass_utils import run_bass_kernel_spmd as _run

    nc = _bacc.Bacc("TRN2", target_bir_lowering=False, num_devices=1)
    arrays, args = {}, []
    given = {name: inputs[name] for name in _INS}
    given["consts"] = shape_constants()
    for name, value in given.items():
        a = _np.ascontiguousarray(value)
        arrays[f"in_{name}_dram"] = a
        args.append(nc.dram_tensor(f"in_{name}_dram", a.shape, _mybir.dt.from_np(a.dtype), kind="ExternalInput").ap())
    for i, (shape, dtype) in enumerate(_OUTS):
        dt = _mybir.dt.from_np(_np.dtype(dtype))
        args.append(nc.dram_tensor(f"out_{i}_dram", shape, dt, kind="ExternalOutput").ap())
    trunk(nc, *args)
    r = _run(nc, [arrays], core_ids=[0])
    got = tuple(r.results[0][f"out_{i}_dram"] for i in range(len(_OUTS)))
    return got[0]
```

```python
from contextlib import ExitStack

import numpy as np

import concourse.bass as bass
from concourse import mybir

ALU = mybir.AluOpType
ACT = mybir.ActivationFunctionType
AX = mybir.AxisListType
F32 = mybir.dt.float32
F32R = mybir.dt.float32r
I32 = mybir.dt.int32
ds = bass.ds

P = 128
T = 256
NT = T // P
D = 1024
KD = D // P
L = 2
H = 4
HD = 64
GW = H * HD
EPS = 1e-6
SCALE = HD ** -0.5
NEG = -1e30
FD = 2816
FE = 3584
E = 8
CLIP = 128
RB = 2 * CLIP + 1
EXT = 384
SC = 3 * P

ORDER = ["D", "A", "C", "B"]
COL0 = {"A": 0, "B": 768, "C": 1280, "D": 2048}
COLS = {"A": 768, "B": 512, "C": 768, "D": 772}
CAT = {"A": 0, "B": 1, "C": 2, "D": 3}
QK = {"B": 0, "C": 1, "D": 2}
IN_COLS = 2820
UNIT = 4096
WIN = [{}, {}]
_at = 0
for _g in ORDER:
    WIN[0][_g] = _at
    _at += KD * COLS[_g]
WIN[1]["D"] = 2 * UNIT
WIN[1]["A"] = WIN[1]["D"] + KD * COLS["D"]
WIN[1]["C"] = 0
WIN[1]["B"] = 8 * UNIT
HANKEL = [_at, WIN[1]["A"] + KD * COLS["A"]]
SETS = [[(8, 2, 3), (0, 1, 6)], [(4, 5, 0), (2, 3, 6)]]
HIGH = [(4, 5, 7), (1, 8, 7)]
UNITS = {g: [(0, 512, 0), (0, 512, 1)] + ([] if g == "B" else [(512, COLS[g] - 512, 0), (512, COLS[g] - 512, 1)])
         for g in ORDER}

FT = 512
QUARTERS = 4

FILLS = [("x", i) for i in range(4)]
for _g in ORDER:
    FILLS += [(_g, "qk", 0), (_g, "qk", 1)]
    if _g != "A":
        FILLS += [(_g, "p", h) for h in range(H)]
    FILLS += [(_g, "o"), (_g, "oT")]
FILLS += [("y", i) for i in range(4)]
FILL = {name: n for n, name in enumerate(FILLS)}
NFILL = len(FILLS)
assert NFILL % 2 == 0
PUNIT = {}
for _g in ORDER:
    for _u in range(len(UNITS[_g])):
        PUNIT[_g, _u] = len(PUNIT)
NPU = len(PUNIT)
NPF = NPU + 2
SUSE = {n: i for i, n in enumerate(["Dsum", "D", "Az", "Aw", "C", "B", "out"])}
NSU = len(SUSE)

C_ID, C_UP, C_NEGLOW = 0, 128, 128 + 257
C_AMASK = C_NEGLOW + 256
C_ANEG, C_CAUSAL, C_BLOCK = C_AMASK + SC, C_AMASK + 2 * SC, C_AMASK + 3 * SC
C_ALIBI = C_AMASK + 4 * SC
C_IOTA = C_ALIBI + H * SC
C_REV = C_IOTA + P
C_ALL = C_REV + E
G_MIX, G_FFN, G_OUT, G_Q, G_K = 0, L * KD, 2 * L * KD, 3 * L * KD, 3 * L * KD + 3 * L
G_ALL = G_K + 3 * L


NORMED = {(g, u): n for n, (g, u) in enumerate((g, u) for g in ORDER if g != "A" for u in range(2))}
SOFT = [g for g in ORDER if g != "A"]
R_DIFF, R_MASK, R_ALL = 14, 15, 26


def shape_constants():
    c = np.zeros((P, C_ALL), np.float32)
    p = np.arange(P)[:, None]
    c[:, C_ID:C_ID + P] = p == np.arange(P)[None]
    c[:, C_UP:C_UP + 257] = p <= np.arange(257)[None] - 1
    c[:, C_NEGLOW:C_NEGLOW + 256] = -(p >= np.arange(256)[None] - P).astype(np.float32)
    col = np.arange(SC)[None]
    s, t = np.where(col < 256, p, p + P), np.where(col < 256, col, col - P)
    c[:, C_AMASK:C_AMASK + SC] = s < t
    c[:, C_ANEG:C_ANEG + SC] = np.where(s < t, 0.0, NEG)
    t, s = np.where(col < P, p, p + P), np.where(col < P, col, col - P)
    c[:, C_CAUSAL:C_CAUSAL + SC] = np.where(s <= t, 0.0, NEG)
    c[:, C_BLOCK:C_BLOCK + SC] = np.where(s // 64 <= t // 64, 0.0, NEG)
    back = t // 64 - s // 64
    for h in range(H):
        slope = 2.0 ** (-8.0 * (h + 1) / H)
        c[:, C_ALIBI + h * SC:C_ALIBI + (h + 1) * SC] = np.where((back >= 0) & (back <= 1), -slope * np.abs(t - s), NEG)
    c[:, C_IOTA:C_IOTA + P] = np.arange(P)[None]
    c[:, C_REV:C_REV + E] = E - np.arange(E)[None]
    return c


def trunk(nc, x_in, g_mix, w_in, b_f, g_q, g_k, swa_sinks, rel_bias, g_out, w_out, g_ffn,
          w_ff_gate, w_ff_up, w_ff_down, w_router, w_exp_gate, w_exp_up, w_exp_down, consts, out):
    with ExitStack() as ctx:
        def sb(name, shape, dt=F32):
            return ctx.enter_context(nc.sbuf_tensor(name, shape, dt))

        def sem(name):
            return ctx.enter_context(nc.semaphore(name))

        def sb_both(name, shape):
            with nc.sbuf_tensor(name, shape, F32) as plain:
                pass
            return plain, ctx.enter_context(nc.sbuf_tensor(name + "_rounded", shape, F32R))

        ext = nc.dram_tensor("ext_rel_bias", [L, H, EXT], F32).ap()

        with nc.sbuf_tensor("wmem", [P, 9 * UNIT], F32) as wmem:
            pass
        units_r = [sb(f"unit_{u}_rounded", [P, UNIT], F32R) for u in range(9)]
        x = sb("x", [P, NT, D])
        xs = sb("xs", [P, NT, D])
        hT, hT_r = sb_both("hT", [P, KD, T])
        con = sb("con", [P, C_ALL])
        gT = sb("gT", [P, G_ALL])
        grow = sb("grow", [G_ALL, P])
        qkT, qkT_r = sb_both("qkT", [P, 2, 4, T])
        vbuf, vbuf_r = sb_both("vbuf", [P, 2, NT, GW])
        stage, stage_r = sb_both("stage", [P, NT, 512])
        sq = sb("sq", [P, 512])
        obuf = sb("obuf", [P, NT, GW])
        osq = sb("osq", [P, NT, GW])
        bfr = sb("bfr", [P, L, H])
        sink = sb("sink", [P, L, NT, H])
        nsink = sb("nsink", [P, L, NT, H])
        wr = sb("wr", [P, KD, E])
        mhalf = sb("mhalf", [P, 8])
        ssx = sb("ssx", [P, NT])
        rx0 = sb("rx0", [P, NT])
        rx = sb("rx", [P, NT])
        ssq = sb("ssq", [P, 2, 8])
        rq0 = sb("rq0", [P, 2, 8])
        rq = sb("rq", [P, 2, 8])
        sso = sb("sso", [P, NT])
        ro0 = sb("ro0", [P, NT])
        ro = sb("ro", [P, NT])
        fraw = sb("fraw", [P, NT, H])
        fu = sb("fu", [P, NT, H])
        fa = sb("fa", [P, NT, H])
        fe = sb("fe", [P, NT, H])
        fl = sb("fl", [P, NT, H])
        fr = sb("fr", [P, NT, H])
        fsp = sb("fsp", [P, NT, H])
        nm = sb("nm", [P, NT * H])
        rsum = sb("rsum", [P, NT * H])
        rinv = sb("rinv", [P, NT * H])
        esink = sb("esink", [P, NT * H])
        lg = sb("lg", [P, NT, E])
        lg2 = sb("lg2", [P, NT, E])
        tmp = sb("tmp", [P, NT, E])
        one1 = sb("one1", [P, NT, E])
        one2 = sb("one2", [P, NT, E])
        mask = sb("mask", [P, NT, E])
        gates = sb("gates", [P, NT, E + 1])
        slot = sb("slot", [P, NT, E + 1])
        m1 = sb("m1", [P, NT])
        m2 = sb("m2", [P, NT])
        r1 = sb("r1", [P, NT])
        dm = sb("dm", [P, NT])
        em = sb("em", [P, NT])
        em1 = sb("em1", [P, NT])
        p1 = sb("p1", [P, NT])
        p2 = sb("p2", [P, NT])
        cnt = sb("cnt", [P, E], I32)
        ps = ctx.enter_context(nc.psum_tensor("ps", [P, 8, 512], F32))

        def scratch(l, n, size=H * SC):
            at = WIN[l]["D"] + n * H * SC
            return wmem[:, at:at + size]

        assert 4 * H * SC <= KD * COLS["D"]
        Lbufs, L2s, pTs, tabCs = [[scratch(l, n).rearrange("p (h c) -> p h c", h=H) for l in range(L)] for n in range(4)]
        spbs = [scratch(l, 2, NT * H * P).rearrange("p (n c) -> p n c", c=P) for l in range(L)]
        hankels = [wmem[:, HANKEL[l]:HANKEL[l] + H * T].rearrange("p (h c) -> p h c", h=H) for l in range(L)]
        assert all(5 * UNIT <= at and at + H * T <= 6 * UNIT for at in HANKEL)
        oT = xs[:].rearrange("p a b -> p (a b)").rearrange("p (k t) -> p k t", t=T)
        def all_t(a):
            return a.rearrange("p (k t) -> p k t", t=T)

        def slots(a, part):
            return a[:, part * KD * P:(part + 1) * KD * P].rearrange("p (k t) -> p k t", t=P)

        qf_r = qkT_r[:].rearrange("p a b t -> p (a b t)")
        xh_r = all_t(qf_r)
        xeh_r = slots(qf_r, 0)
        xel_r = slots(qf_r, 1)
        osf = osq[:].rearrange("p a b -> p (a b)")
        sel = osf[:, 0:T].rearrange("p (a t) -> p a t", t=P)
        selg = osf[:, T:2 * T].rearrange("p (a t) -> p a t", t=P)
        back = con[:, C_ALIBI:C_ALIBI + T]
        ye = vbuf[:].rearrange("p a b c -> p (a b c)")
        hh_r = vbuf_r[:].rearrange("p a b c -> p a (b c)")
        hl_r = stage_r
        hid = [sq[:], obuf[:].rearrange("p a b -> p (a b)")]

        def win(l, g):
            return wmem[:, WIN[l][g]:WIN[l][g] + KD * COLS[g]].rearrange("p (k c) -> p k c", k=KD)

        def unit(u, k=KD, cols=FT):
            return wmem[:, u * UNIT:u * UNIT + k * cols].rearrange("p (k c) -> p k c", k=k)

        wo = wmem[:, 6 * UNIT:8 * UNIT].rearrange("p (k c) -> p k c", k=KD)

        s_x = sem("x_loaded")
        s_con = sem("consts_loaded")
        s_gain = sem("gain_rows_loaded")
        s_small = sem("biases_loaded")
        s_wr = sem("w_router_loaded")
        s_win = {g: sem(f"w_in_{g}_loaded") for g in ORDER}
        s_wo = [sem(f"w_out_{i}_loaded") for i in range(2)]
        s_raw = [[sem(f"set_{i}_{kind}_loaded") for kind in ("gate", "up", "down")] for i in range(2)]
        hi_ready = [sem(f"high_{kind}_ready") for kind in ("gate", "up", "down")]
        lo_ready = [sem(f"low_{kind}_ready") for kind in ("gate", "up", "down")]
        s_ext = sem("rel_bias_extended")
        s_tabc = sem("rel_table_loaded")
        s_tabm = sem("rel_table_masked")
        s_out = sem("output_stored")
        gains_T = sem("gains_transposed")
        gains = sem("gains_ready")
        ssx_ready = sem("x_squares_summed")
        rx_part = sem("x_mean_ready")
        rx_ready = sem("x_rstd_ready")
        xs_ready = sem("x_scaled")
        tr_full = sem("transposes_done")
        tr_free = [sem(f"transposed_bank_{b}_read") for b in range(2)]
        pr_full = sem("projection_done")
        pr_free = [sem(f"projection_bank_{b}_read") for b in range(2)]
        sc_full = sem("scores_done")
        sc_free = sem("scores_read")
        sq_ready = sem("qk_squared")
        ssq_ready = sem("qk_squares_summed")
        rq_part = sem("qk_mean_ready")
        rq_ready = sem("qk_rstd_ready")
        vf_ready = sem("gate_logits_copied")
        f_dve = sem("forget_dve_step")
        f_act = sem("forget_act_step")
        spb_ready = sem("forget_spread")
        m_ready = sem("row_max_ready")
        mx_part = sem("row_max_part")
        p_ready = sem("exps_ready")
        es_ready = sem("sink_exp_ready")
        rs_part = sem("row_sum_with_sink")
        ri_ready = sem("row_inverse_ready")
        a_relu = sem("stick_relu_ready")
        a_abs = sem("stick_act_step")
        a_sp = sem("stick_softplus_step")
        o_ready = sem("group_output_step")
        sso_ready = sem("group_squares_summed")
        ro_part = sem("group_mean_ready")
        ro_ready = sem("group_rstd_ready")
        g_full = sem("ffn_gate_done")
        u_full = sem("ffn_up_done")
        silu_ready = sem("ffn_silu_ready")
        h_ready = sem("ffn_hidden_ready")
        t_full = sem("ffn_hidden_transposed")
        hh_ready = sem("ffn_hidden_high_ready")
        hl_ready = sem("ffn_hidden_low_ready")
        d_full = sem("ffn_down_done")
        xh_ready = sem("ffn_in_high_ready")
        e_full = sem("expert_out_spread")
        x_added = sem("ffn_added")
        whole = sem("ffn_in_whole")
        r_pe = sem("router_pe_step")
        r_dve = sem("router_dve_step")
        r_act = sem("router_act_step")
        sel_ready = sem("selection_ready")
        gx_full = sem("gather_done")
        gx_dve = sem("gather_low_ready")
        gx_act = sem("gather_high_ready")
        gx_back = sem("slot_to_token_ready")
        ye_dve = sem("expert_out_read_dve")
        ye_act = sem("expert_out_read_act")

        def filled(eng, l, name):
            eng.wait_ge(tr_full, l * NFILL + FILL[name] + 1)

        def emptied(eng, l, name):
            n = FILL[name]
            eng.wait_ge(tr_free[n % 2], l * (NFILL // 2) + n // 2 + 1)

        def bank(name):
            return ps[:, 6 + FILL[name] % 2, :]

        def pbank(m):
            return ps[:, m % 2, :]

        DENSE_STEPS = FD // FT + 1
        EXPERT_STEPS = FE // FT
        assert FD == (DENSE_STEPS - 1) * FT + FT // 2 and DENSE_STEPS % 2 == 0 and EXPERT_STEPS % 2 == 1
        VARIANTS = [P]

        def steps(eng, one, n, first, use, parity):
            peeled = n - 4
            for s in range(peeled):
                one(s, (parity + s) % 2, first + s, use + (parity + s) // 2, None)
            with eng.Fori(0, 2) as i:
                for s in (peeled, peeled + 1):
                    one(s, (parity + s) % 2, eng.snap(i * 2 + (first + s)), eng.snap(i + (use + (parity + s) // 2)), i)

        def pairs(eng, body):
            with eng.Fori(0, E // 2) as pair:
                for p in range(2):
                    body(pair, p, eng.snap(pair * 2 + p), eng.snap(pair * (2 * EXPERT_STEPS) + (DENSE_STEPS + p * EXPERT_STEPS)),
                         eng.snap(pair * EXPERT_STEPS + (DENSE_STEPS // 2 + p * (EXPERT_STEPS // 2))))

        def by_count(eng, n, run):
            def choose(widths):
                if not widths:
                    run(T)
                    return
                with eng.If(n < widths[0] + 1):
                    run(widths[0])
                with eng.Else():
                    choose(widths[1:])
                eng.end_ifs()
            choose(VARIANTS)

        def unless_last(eng, s, n, loop, run):
            if s < n - 3:
                run()
                return
            with eng.If(loop < 1):
                run()
            eng.end_ifs()

        def next_expert(eng, pair, p, run):
            if p == 0:
                run()
                return
            with eng.If(pair < E // 2 - 1):
                run()
            eng.end_ifs()

        def hidden_cols(s, dense):
            return FT // 2 if dense and s == 0 else FT

        def weight(l, u, kind, cols):
            k, c = (KD, cols) if kind < 2 else (cols // P, D)
            return units_r[u][:, 0:k * c].rearrange("p (k c) -> p k c", k=k)

        def quarter_r(u, q, cols):
            n = KD * cols // QUARTERS
            return units_r[u][:, q * n:(q + 1) * n]

        def quarter(u, q, cols):
            n = KD * cols // QUARTERS
            return wmem[:, u * UNIT + q * n:u * UNIT + (q + 1) * n]

        def scale_qk(eng, l, gi, g, t):
            filled(eng, l, (g, "qk", t))
            nb = 3 if g == "B" else 4
            if g == "A":
                sq_, sk_ = SCALE, 1.0
            else:
                n = l * 3 + QK[g]
                sq_, sk_ = gT[:, G_Q + n:G_Q + n + 1], gT[:, G_K + n:G_K + n + 1]
            for b0, b1, s in ((0, 2, sq_), (2, nb, sk_)):
                dst = qkT[:, gi % 2, b0:b1, t * P:(t + 1) * P]
                src = bank((g, "qk", t))[:, b0 * P:b1 * P].rearrange("p (b c) -> p b c", c=P)
                if t == 0:
                    ins = eng.tensor_scalar(dst, src, s, None, ALU.mult)
                else:
                    ins = eng.activation(dst, src, ACT.Copy, scale=s)
            ins.then_inc(tr_free[FILL[g, "qk", t] % 2], 1)

        block = ctx.enter_context(nc.Block())

        @block.sync
        def _(sp):
            def load_w_in(l, g):
                sp.dma_start(win(l, g), w_in[l, :, COL0[g]:COL0[g] + COLS[g]].rearrange("(k p) c -> p k c", p=P)) \
                    .then_inc(s_win[g], 16)

            def load_w_out(l, i):
                sp.dma_start(wo[:, 4 * i:4 * i + 4, :],
                             w_out[l, 512 * i:512 * (i + 1), :].rearrange("(k p) c -> p k c", p=P)).then_inc(s_wo[i], 16)

            def load_up(w, l, i, kind, f0, cols=FT):
                sp.dma_start(unit(SETS[l][i][kind], KD, cols), w[:, ds(f0, cols)].rearrange("(k p) c -> p k c", p=P)) \
                    .then_inc(s_raw[i][kind], 16)

            def load_down(w, l, i, f0, rows=FT):
                sp.dma_start(unit(SETS[l][i][2], rows // P, D), w[ds(f0, rows), :].rearrange("(k p) c -> p k c", p=P)) \
                    .then_inc(s_raw[i][2], 16)

            def extend():
                rows = ext.rearrange("l h c -> (l h) c")
                sp.dma_start(rows[:, 0:RB - 1], rel_bias.rearrange("l h c -> (l h) c")[:, 1:RB]).then_inc(s_ext, 16)
                last = bass.AP(tensor=rel_bias.tensor, offset=rel_bias.offset + RB - 1, 
                               ap=[[RB, L * H], [0, EXT - RB + 1], [1, 1]])
                sp.dma_start(rows[:, RB - 1:EXT].unsqueeze(2), last).then_inc(s_ext, 16)

            def load_table(l):
                sp.wait_ge(s_ext, 16 * 2)
                sp.dma_start(hankels[l], bass.AP(tensor=ext.tensor, offset=ext.offset + l * H * EXT,
                                             ap=[[1, P], [EXT, H], [1, T]])).then_inc(s_tabc, 16)

            for t in range(NT):
                sp.dma_start(x[:, t, :], x_in[0, t * P:(t + 1) * P, :]).then_inc(s_x, 16)
            sp.dma_start(con[:], consts).then_inc(s_con, 16)
            sp.dma_start(grow[G_MIX:G_FFN, :], g_mix.rearrange("l (k c) -> (l k) c", c=P)).then_inc(s_gain, 16)
            sp.dma_start(grow[G_FFN:G_OUT, :], g_ffn.rearrange("l (k c) -> (l k) c", c=P)).then_inc(s_gain, 16)
            sp.dma_start(grow[G_OUT:G_Q, :], g_out.rearrange("l g (k c) -> (l g k) c", c=P)).then_inc(s_gain, 16)
            for half in range(2):
                sp.dma_start(grow[G_Q:G_K, half * HD:(half + 1) * HD], g_q.rearrange("l i c -> (l i) c")).then_inc(s_gain, 16)
                sp.dma_start(grow[G_K:G_ALL, half * HD:(half + 1) * HD], g_k.rearrange("l i c -> (l i) c")).then_inc(s_gain, 16)
            load_w_in(0, "D")
            sp.dma_start(bfr[:].rearrange("p l h -> p (l h)"),
                         bass.AP(tensor=b_f.tensor, offset=b_f.offset, ap=[[0, P], [1, L * H]])).then_inc(s_small, 16)
            for t in range(NT):
                sp.dma_start(sink[:, :, t, :],
                             bass.AP(tensor=swa_sinks.tensor, offset=swa_sinks.offset, ap=[[0, P], [H, L], [1, H]])) \
                    .then_inc(s_small, 16)
            load_w_in(0, "A")
            extend()
            load_table(0)
            load_w_in(0, "C")
            load_w_in(0, "B")
            load_w_out(0, 0)
            load_w_out(0, 1)
            sp.dma_start(wr[:], w_router[0].rearrange("(k p) e -> p k e", p=P)).then_inc(s_wr, 16)

            def first_steps(l, gate, up, down, cols):
                if l == 0:
                    load_up(gate, 0, 0, 0, 0, cols)
                sp.wait_ge(pr_full, l * NPF + PUNIT["A", 3] + 1)
                if l:
                    load_up(gate, 1, 0, 0, 0, cols)
                    sp.wait_ge(s_tabm, l + 1)
                    load_up(up, 1, 0, 1, 0, cols)
                sp.wait_ge(pr_full, l * NPF + PUNIT["C", 3] + 1)
                if l == 0:
                    load_up(up, 0, 0, 1, 0, cols)
                load_down(down, l, 0, 0, cols)
                sp.wait_ge(sc_full, l * NSU + SUSE["out"] + 1)
                load_up(gate, l, 1, 0, cols)
                load_up(up, l, 1, 1, cols)
                if l == 0:
                    load_down(down, l, 1, cols)

            def step(l, i, kinds, weights, f0, step_):
                for kind in kinds:
                    sp.wait_ge((g_full, u_full, d_full)[kind], step_ * 2 - 2)
                    if kind < 2:
                        load_up(weights[kind], l, i, kind, f0)
                    else:
                        load_down(weights[2], l, i, f0)

            dense = (w_ff_gate[0], w_ff_up[0], w_ff_down[0])
            first_steps(0, *dense, FT // 2)
            with sp.Fori(1, DENSE_STEPS // 2) as i:
                f0 = i * (2 * FT) - FT // 2
                step(0, 0, (0, 1, 2), dense, f0, sp.snap(i * 2))
                step(0, 1, (0, 1, 2), dense, f0 + FT, sp.snap(i * 2 + 1))

            for done in (g_full, u_full, d_full):
                sp.wait_ge(done, 2 * (DENSE_STEPS - 1))
            load_w_in(1, "D")
            load_w_in(1, "B")
            sp.wait_ge(g_full, 2 * DENSE_STEPS)
            sp.wait_ge(u_full, 2 * DENSE_STEPS)
            load_w_in(1, "A")
            load_table(1)
            load_w_in(1, "C")
            sp.wait_ge(d_full, 2 * DENSE_STEPS)
            load_w_out(1, 0)
            load_w_out(1, 1)

            def expert(e):
                if isinstance(e, int):
                    return w_exp_gate[0, e], w_exp_up[0, e], w_exp_down[0, e]
                return [w[0, ds(e, 1)].rearrange("a b c -> (a b) c") for w in (w_exp_gate, w_exp_up, w_exp_down)]

            def expert_steps(e, parity, first, s0):
                def load(s, f0, step_):
                    i = (parity + s) % 2
                    if s >= 2 or s0 == 0:
                        step(1, i, (0, 1), expert(e), f0, step_)
                    if s:
                        step(1, 1 - i, (2,), expert(e), f0 - FT, step_ - 1)
                for s in range(s0, EXPERT_STEPS - 4):
                    load(s, s * FT, first + s)
                with sp.Fori(0, 2) as i:
                    for s in (EXPERT_STEPS - 4, EXPERT_STEPS - 3):
                        load(s, i * (2 * FT) + s * FT, sp.snap(i * 2 + (first + s)))
                last = EXPERT_STEPS - 1
                step(1, (parity + last) % 2, (2,), expert(e), last * FT, first + last)

            first_steps(1, *expert(0), FT)
            expert_steps(0, 0, DENSE_STEPS, 2)
            expert_steps(1, 1, DENSE_STEPS + EXPERT_STEPS, 0)
            with sp.Fori(1, E // 2) as pair:
                for p in range(2):
                    expert_steps(sp.snap(pair * 2 + p), p,
                                 sp.snap(pair * (2 * EXPERT_STEPS) + (DENSE_STEPS + p * EXPERT_STEPS)), 0)
            sp.wait_ge(x_added, 4 * (1 + E))
            for t in range(NT):
                sp.dma_start(out[0, t * P:(t + 1) * P, :], x[:, t, :]).then_inc(s_out, 16)
            sp.wait_ge(s_out, 16 * NT)

        @block.tensor
        def _(pe):
            ident = con[:, C_ID:C_ID + P]
            up = con[:, C_UP:C_UP + 257]
            neglow = con[:, C_NEGLOW:C_NEGLOW + 256]

            def open_fill(l, name):
                n = FILL[name]
                if n >= 2:
                    pe.wait_ge(tr_free[n % 2], l * (NFILL // 2) + n // 2)

            def norm(l, name):
                for i in range(4):
                    open_fill(l, (name, i))
                    for kk in range(2):
                        k = 2 * i + kk
                        for t in range(NT):
                            if i == 0 and kk == 0:
                                pe.wait_ge(xs_ready, 2 * (2 * l + (name == "y")) + t + 1)
                            mm = pe.transpose(bank((name, i))[:, kk * T + t * P:kk * T + (t + 1) * P],
                                              xs[:, t, k * P:(k + 1) * P], ident)
                    mm.then_inc(tr_full, 1)

            def project(l, g, u):
                c0, cols, t = UNITS[g][u]
                m = PUNIT[g, u]
                if m == 0:
                    emptied(pe, l, ("x", 2))
                    emptied(pe, l, ("x", 3))
                if m >= 2:
                    pe.wait_ge(pr_free[m % 2], l * (NPF // 2) + m // 2)
                if u == 0:
                    pe.wait_ge(s_win[g], 16 * (l + 1))
                for k in range(KD):
                    mm = pe.matmul(pbank(m)[:, 0:cols], hT[:, k, t * P:(t + 1) * P], win(l, g)[:, k, c0:c0 + cols],
                                   start=(k == 0), stop=(k == KD - 1))
                mm.then_inc(pr_full, 1)

            def qk_transposes(l, gi, g):
                nb = 3 if g == "B" else 4
                for t in range(NT):
                    open_fill(l, (g, "qk", t))
                    pe.wait_ge(pr_free[t], l * (NPF // 2) + PUNIT[g, t] // 2 + 1)
                    for b in range(nb):
                        mm = pe.transpose(bank((g, "qk", t))[:, b * P:(b + 1) * P], stage[:, t, b * P:(b + 1) * P], ident)
                    mm.then_inc(tr_full, 1)

            def q_k(gi, g, h):
                if g == "B":
                    qb, lo = h % 2, HD * (h // 2)
                    kb = 2
                else:
                    qb, kb, lo = h // 2, 2 + h // 2, HD * (h % 2)
                return qkT[lo:lo + HD, gi % 2, qb, :], qkT[lo:lo + HD, gi % 2, kb, :]

            def wait_scores_free(l, use):
                n = SUSE[use]
                if n:
                    pe.wait_ge(sc_free, l * NSU + n)

            def forget_sums(l):
                pe.wait_ge(spb_ready, l + 1)
                wait_scores_free(l, "Dsum")
                for h in range(H):
                    pe.matmul(ps[:, 2 + h, 0:T], spbs[l][:, h, :], up[:, 1:1 + T], start=True, stop=False)
                    mm = pe.matmul(ps[:, 2 + h, P:T], spbs[l][:, H + h, :], up[:, 1:1 + P], start=False, stop=True)
                mm.then_inc(sc_full, 1)

            def scores(l, gi, g):
                emptied(pe, l, (g, "qk", 0))
                emptied(pe, l, (g, "qk", 1))
                wait_scores_free(l, "Az" if g == "A" else g)
                for h in range(H):
                    q, k = q_k(gi, g, h)
                    if g == "A":
                        pe.matmul(ps[:, 2 + h, 0:T], k[:, 0:P], q[:, 0:T], start=True, stop=True, skip_group_check=True)
                        mm = pe.matmul(ps[:, 2 + h, T:SC], k[:, P:T], q[:, P:T], start=False, stop=True,
                                       skip_group_check=True)
                    else:
                        pe.matmul(ps[:, 2 + h, 0:P], q[:, 0:P], k[:, 0:P], start=True, stop=True)
                        mm = pe.matmul(ps[:, 2 + h, P:SC], q[:, P:T], k[:, 0:T], start=True, stop=True)
                mm.then_inc(sc_full, 1)

            def stick_sums(l):
                pe.wait_ge(a_sp, 2 * (l + 1))
                pe.wait_ge(sc_free, l * NSU + SUSE["Aw"])
                for h in range(H):
                    o, sp_ = ps[:, 2 + h, :], L2s[l][:, h, :]
                    pe.matmul(o[:, 0:T], neglow[:, P:2 * P], sp_[:, 0:T], start=False, stop=True, skip_group_check=True)
                    pe.matmul(o[:, P:T], neglow[:, 0:P], sp_[:, T:SC], start=False, stop=True, skip_group_check=True)
                    mm = pe.matmul(o[:, T:SC], neglow[:, P:2 * P], sp_[:, T:SC], start=False, stop=True,
                                   skip_group_check=True)
                mm.then_inc(sc_full, 1)

            def p_transposes(l, g):
                for h in range(H):
                    open_fill(l, (g, "p", h))
                    pe.wait_ge(p_ready, 4 * (4 * l + ORDER.index(g)) + h + 1)
                    for b in range(3):
                        mm = pe.transpose(bank((g, "p", h))[:, b * P:(b + 1) * P], Lbufs[l][:, h, b * P:(b + 1) * P], ident)
                    mm.then_inc(tr_full, 1)

            def values(l, gi, g):
                if g == "A":
                    pe.wait_ge(p_ready, 4 * (4 * l + gi) + H)
                    w = Lbufs[l]
                else:
                    emptied(pe, l, (g, "p", 2))
                    emptied(pe, l, (g, "p", 3))
                    w = pTs[l]
                last = len(UNITS[g]) - 1
                for u in (last - 1, last):
                    m = PUNIT[g, u]
                    pe.wait_ge(pr_free[m % 2], l * (NPF // 2) + m // 2 + 1)
                open_fill(l, (g, "o"))
                for h in range(H):
                    hv = h // 2 if g == "B" else h
                    v = [vbuf[:, gi % 2, t, hv * HD:(hv + 1) * HD] for t in range(NT)]
                    o = [bank((g, "o"))[:, t * GW + h * HD:t * GW + (h + 1) * HD] for t in range(NT)]
                    pe.matmul(o[0], w[:, h, 0:P], v[0], start=True, stop=True)
                    pe.matmul(o[1], w[:, h, P:2 * P], v[0], start=True, stop=False)
                    mm = pe.matmul(o[1], w[:, h, 2 * P:SC], v[1], start=False, stop=True)
                mm.then_inc(tr_full, 1)

            def o_transposes(l, gi, g):
                open_fill(l, (g, "oT"))
                pe.wait_ge(o_ready, 4 * l + gi + 1)
                for kk in range(2):
                    for t in range(NT):
                        mm = pe.transpose(bank((g, "oT"))[:, kk * T + t * P:kk * T + (t + 1) * P],
                                          obuf[:, t, kk * P:(kk + 1) * P], ident)
                mm.then_inc(tr_full, 1)

            def out_project(l, t, groups):
                if groups[0] == ORDER[0]:
                    if t == 0:
                        for b in range(2):
                            pe.wait_ge(pr_free[(NPU + b) % 2], l * (NPF // 2) + (NPU + b) // 2)
                        for i in range(2):
                            pe.wait_ge(s_wo[i], 16 * (l + 1))
                    else:
                        wait_scores_free(l, "out")
                for g in groups:
                    emptied(pe, l, (g, "oT"))
                    for kk in range(2):
                        k = 2 * CAT[g] + kk
                        for half in range(2):
                            mm = pe.matmul(ps[:, 2 * t + half, :], oT[:, k, t * P:(t + 1) * P],
                                           wo[:, k, half * 512:(half + 1) * 512],
                                           start=(g == ORDER[0] and kk == 0), stop=(g == ORDER[-1] and kk == 1))
                            if g == ORDER[-1] and kk == 1 and t == 0:
                                mm.then_inc(pr_full, 1)
                if groups[-1] == ORDER[-1] and t == 1:
                    mm.then_inc(sc_full, 1)

            def attention(l):
                norm(l, "x")
                for gi, g in enumerate(ORDER + [None]):
                    before = ORDER[gi - 1] if gi else None
                    units = list(range(len(UNITS[g]))) if g else []

                    def some(n):
                        for _ in range(n):
                            if units:
                                project(l, g, units.pop(0))
                    if not gi:
                        some(4)
                        continue
                    some(1)
                    if before == "D":
                        forget_sums(l)
                    qk_transposes(l, gi - 1, before)
                    scores(l, gi - 1, before)
                    if g is None:
                        out_project(l, 0, ORDER[:-1])
                        out_project(l, 1, ORDER[:-1])
                    some(1)
                    if before == "A":
                        stick_sums(l)
                    some(1)
                    if before != "A":
                        p_transposes(l, before)
                    some(1)
                    values(l, gi - 1, before)
                    some(4)
                    o_transposes(l, gi - 1, before)
                out_project(l, 0, ORDER[-1:])
                out_project(l, 1, ORDER[-1:])
                norm(l, "y")
                emptied(pe, l, ("y", 2))
                emptied(pe, l, ("y", 3))

            def gate_up(l, i, step, bufs, src, t, cols, count, loaded=None, before_up=None):
                for kind, full in ((0, g_full), (1, u_full)):
                    hi, lo = weight(l, HIGH[l][kind], kind, cols), weight(l, SETS[l][i][kind], kind, cols)
                    if kind and before_up:
                        before_up()
                    o = ps[:, 2 * bufs + kind, 0:cols]
                    for k in range(KD):
                        if kind == 0 and loaded:
                            loaded(k)
                        if t == 0 and k % 2 == 0:
                            pe.wait_ge(lo_ready[kind], step * QUARTERS + (k // 2 + 1))
                        xhk, xlk = src[0][:, k, t * P:(t + 1) * P], src[1][:, k, t * P:(t + 1) * P]
                        pe.matmul(o, xhk, hi[:, k, :], start=(k == 0), stop=False)
                        pe.matmul(o, xhk, lo[:, k, :], start=False, stop=False)
                        mm = pe.matmul(o, xlk, hi[:, k, :], start=False, stop=(k == KD - 1))
                    mm.then_inc(full, count)

            def transposes(bufs, cols, done, count):
                pe.wait_ge(h_ready, done)
                for b in range(cols // P):
                    mm = pe.transpose(ps[:, 2 * bufs, b * P:(b + 1) * P], hid[bufs][:, b * P:(b + 1) * P], ident)
                mm.then_inc(t_full, count)

            def down(l, i, step, bufs, t, cols, done, count, first=False):
                hi, lo = weight(l, HIGH[l][2], 2, cols), weight(l, SETS[l][i][2], 2, cols)
                pe.wait_ge(hl_ready, done)
                blocks = cols // P
                for b in range(blocks):
                    hhb, hlb = [a[:, bufs, b * P:(b + 1) * P] for a in (hh_r, hl_r)]
                    for half in range(2):
                        part = b * QUARTERS // blocks + (half if blocks < QUARTERS else 0)
                        if t == 0 and (half == 0 or blocks < QUARTERS):
                            pe.wait_ge(lo_ready[2], step * QUARTERS + (part + 1))
                        o, c = ps[:, 4 + 2 * t + half, :], slice(half * 512, (half + 1) * 512)
                        pe.matmul(o, hhb, hi[:, b, c], start=(first and b == 0), stop=False, skip_group_check=True)
                        pe.matmul(o, hhb, lo[:, b, c], start=False, stop=False, skip_group_check=True)
                        mm = pe.matmul(o, hlb, hi[:, b, c], start=False, stop=(b == blocks - 1), skip_group_check=True)
                mm.then_inc(d_full, count)

            def all_tokens(l, n, first_step, use, parity):
                src = (xh_r, hT_r)

                def one(s, i, step, use_, _):
                    cols = hidden_cols(s, l == 0)
                    gate_up(l, i, step, 0, src, 0, cols, 1)
                    if s:
                        down(l, 1 - i, step - 1, 1, 1, hidden_cols(s - 1, l == 0), step * 2, 1, first=(s == 1))
                    transposes(0, cols, step * 2 + 1, 1)
                    gate_up(l, i, step, 1, src, 1, cols, 1)
                    down(l, i, step, 0, 0, cols, step * 2 + 1, 1, first=(s == 0))
                    transposes(1, cols, step * 2 + 2, 1)
                steps(pe, one, n, first_step, use, parity)
                down(l, (parity + n - 1) % 2, first_step + (n - 1), 1, 1, FT, first_step * 2 + 2 * n, 1)

            pe.wait_ge(s_con, 16)
            pe.wait_ge(s_gain, 16 * 7)
            pe.transpose(ps[:, 0, 0:G_ALL], grow[:, :], con[0:G_ALL, C_ID:C_ID + G_ALL]).then_inc(gains_T, 1)

            attention(0)
            all_tokens(0, DENSE_STEPS, 0, 0, 0)

            attention(1)
            pe.wait_ge(s_wr, 16)
            for t in range(NT):
                for k in range(KD):
                    mm = pe.matmul(ps[:, 0, t * E:(t + 1) * E], hT[:, k, t * P:(t + 1) * P], wr[:, k, :],
                                   start=(k == 0), stop=(k == KD - 1))
            mm.then_inc(r_pe, 1)
            pe.wait_ge(r_dve, R_MASK)
            pe.matmul(ps[:, 1, 0:E], up[:, 0:P], mask[:, 0, :], start=True, stop=True)
            pe.matmul(ps[:, 1, E:2 * E], up[:, P + 1:2 * P + 1], mask[:, 0, :], start=True, stop=False)
            pe.matmul(ps[:, 1, E:2 * E], up[:, 0:P], mask[:, 1, :], start=False, stop=True)
            pe.matmul(ps[:, 1, 2 * E:3 * E], up[:, P + 1:2 * P + 1], mask[:, 0, :], start=True, stop=False)
            pe.matmul(ps[:, 1, 2 * E:3 * E], up[:, P + 1:2 * P + 1], mask[:, 1, :], start=False, stop=True).then_inc(r_pe, 1)
            pe.wait_ge(r_dve, R_ALL)
            def gathered(e, p, first_step, use):
                pe.wait_ge(sel_ready, e + 1)
                for half in range(2):
                    for b in range(4):
                        for t in range(NT):
                            mm = pe.matmul(ps[:, 4 + half, b * P:(b + 1) * P], xs[:, t, (4 * half + b) * P:(4 * half + b + 1) * P],
                                           sel[:, t, :], start=(t == 0), stop=(t == NT - 1))
                    mm.then_inc(gx_full, 1)
                for t in range(NT):
                    mm = pe.transpose(ps[:, 2 * p + 1, t * P:(t + 1) * P], selg[:, t, :], ident)
                mm.then_inc(gx_full, 1)

                def loaded(k):
                    pe.wait_ge(gx_dve, e * KD + (k + 1))

                def back_read():
                    pe.wait_ge(gx_back, e + 1)

                src = (xeh_r, xel_r)

                def one(s, i, step, use_, _):
                    if s == 1:
                        pe.wait_ge(x_added, e * 4 + 4)
                    gate_up(1, i, step, i, src, 0, FT, 2, *((loaded, back_read) if s == 0 else ()))
                    if s:
                        down(1, 1 - i, step - 1, 1 - i, 0, FT, step * 2, 2, first=(s == 1))
                    transposes(i, FT, step * 2 + 2, 2)
                steps(pe, one, EXPERT_STEPS, first_step, use, p)
                down(1, p, first_step + (EXPERT_STEPS - 1), p, 0, FT, first_step * 2 + 2 * EXPERT_STEPS, 2)
                pe.wait_ge(ye_dve, e + 1)
                pe.wait_ge(ye_act, e + 1)
                for t in range(NT):
                    for half in range(2):
                        pe.matmul(ps[:, (6, 2 * p)[t] + half, :], back[:, t * P:(t + 1) * P],
                                  ye[:, half * 512:(half + 1) * 512], start=True, stop=True).then_inc(e_full, 1)

            def expert(pair, p, e, first_step, use):
                n_e = pe.value_load(cnt[0:1, ds(e, 1)], min_val=0, max_val=T)

                def run(n):
                    if n < T:
                        gathered(e, p, first_step, use)
                        return
                    pe.sem_inc(gx_full, 3)
                    pe.wait_ge(x_added, e * 4 + 4)
                    pe.wait_ge(gx_dve, e * KD + KD)
                    all_tokens(1, EXPERT_STEPS, first_step, use, p)
                    pe.sem_inc(e_full, 4)
                    pe.wait_ge(x_added, e * 4 + 8)
                by_count(pe, n_e, run)
            pairs(pe, expert)

        @block.scalar
        def _(act):
            def norm(l, name):
                y = name == "y"
                if y:
                    act.wait_ge(pr_free[0], (l + 1) * (NPF // 2))
                    act.wait_ge(pr_free[1], (l + 1) * (NPF // 2))
                    act.wait_ge(sc_free, (l + 1) * NSU)
                elif l:
                    act.wait_ge(x_added, 4 * l)
                for t in range(NT):
                    if not y and not l:
                        act.wait_ge(s_x, 16 * NT)
                    act.activation(xs[:, t, :], x[:, t, :], ACT.Square, accum_out=ssx[:, t:t + 1]).then_inc(ssx_ready, 1)
                act.wait_ge(gains, 1)
                if y and l == 0:
                    for i in range(4):
                        filled(act, l, (name, i))
                        for kk in range(2):
                            k = 2 * i + kk
                            c = G_FFN + l * KD + k
                            ins = act.activation(xh_r[:, k, :], bank((name, i))[:, kk * T:(kk + 1) * T], ACT.Copy,
                                                 scale=gT[:, c:c + 1])
                        ins.then_inc(xh_ready, 1)
                    return
                for i in (1, 3):
                    filled(act, l, (name, i))
                    for kk in range(2):
                        k = 2 * i + kk
                        c = (G_FFN if y else G_MIX) + l * KD + k
                        ins = act.activation(hT[:, k, :], bank((name, i))[:, kk * T:(kk + 1) * T], ACT.Copy,
                                             scale=gT[:, c:c + 1])
                    ins.then_inc(tr_free[1], 1)

            def read_unit(l, gi, g, u):
                m = PUNIT[g, u]
                act.wait_ge(pr_full, l * NPF + m + 1)
                if u >= 2:
                    if gi >= 2:
                        filled(act, l, (ORDER[gi - 2], "o"))
                    if g == "D":
                        act.activation(fraw[:, u - 2, :], pbank(m)[:, GW:GW + H], ACT.Copy)
                    act.activation(vbuf[:, gi % 2, u - 2, :], pbank(m)[:, 0:GW], ACT.Copy).then_inc(pr_free[m % 2], 1)
                elif g != "A":
                    cols = 384 if g == "B" else 512
                    n = NORMED[g, u] + l * len(NORMED)
                    if n:
                        act.wait_ge(ssq_ready, n)
                    act.activation(sq[:, 0:cols], pbank(m)[:, 0:cols], ACT.Square).then_inc(sq_ready, 1)

            def forget(l):
                act.wait_ge(f_dve, 3 * l + 1)
                act.activation(fa[:], fu[:], ACT.Abs).then_inc(f_act, 1)
                act.wait_ge(f_act, 3 * l + 1)
                act.activation(fe[:], fa[:], ACT.Exp, scale=-1.0).then_inc(f_act, 1)
                act.wait_ge(f_act, 3 * l + 2)
                act.activation(fl[:], fe[:], ACT.Ln, bias=1.0).then_inc(f_act, 1)

            def read_qk(l, gi, g):
                scale_qk(act, l, gi, g, 1)

            def softmax(l, gi, g):
                act.wait_ge(m_ready, 3 * l + SOFT.index(g) + 1)
                for h in range(H):
                    for t in range(NT):
                        c0, c1 = (0, P) if t == 0 else (P, SC)
                        n = t * H + h
                        ins = act.activation(Lbufs[l][:, h, c0:c1], Lbufs[l][:, h, c0:c1], ACT.Exp, bias=nm[:, n:n + 1],
                                             accum_out=rsum[:, n:n + 1])
                    ins.then_inc(p_ready, 1)
                if g == "B":
                    act.wait_ge(mx_part, 2 * (l + 1))
                    act.activation(esink[:], esink[:], ACT.Exp).then_inc(es_ready, 1)

            def stick_softplus(l):
                act.wait_ge(a_relu, l + 1)
                act.activation(Lbufs[l][:], ps[:, 2:2 + H, 0:SC], ACT.Abs).then_inc(sc_free, 1)
                act.wait_ge(sc_free, l * NSU + SUSE["Az"] + 1)
                act.activation(Lbufs[l][:], Lbufs[l][:], ACT.Exp, scale=-1.0).then_inc(a_abs, 1)
                act.wait_ge(a_abs, 2 * l + 1)
                act.activation(Lbufs[l][:], Lbufs[l][:], ACT.Ln, bias=1.0).then_inc(a_abs, 1)

            def stick_exp(l, gi):
                act.wait_ge(sc_free, l * NSU + SUSE["Aw"] + 1)
                act.activation(Lbufs[l][:], Lbufs[l][:], ACT.Exp).then_inc(p_ready, H)

            def read_p(l, g):
                for h in (1, 3):
                    filled(act, l, (g, "p", h))
                    act.activation(pTs[l][:, h, :], bank((g, "p", h))[:, 0:SC], ACT.Copy).then_inc(tr_free[FILL[g, "p", h] % 2], 1)

            def read_oT(l, g):
                filled(act, l, (g, "oT"))
                for kk in range(2):
                    k = 2 * CAT[g] + kk
                    c = G_OUT + l * 8 + k
                    ins = act.activation(oT[:, k, :], bank((g, "oT"))[:, kk * T:(kk + 1) * T], ACT.Copy, scale=gT[:, c:c + 1])
                ins.then_inc(tr_free[FILL[g, "oT"] % 2], 1)

            def attention(l):
                norm(l, "x")
                for gi, g in enumerate(ORDER + [None]):
                    before = ORDER[gi - 1] if gi else None
                    units = list(range(len(UNITS[g]))) if g else []

                    def some(n):
                        for _ in range(n):
                            if units:
                                read_unit(l, gi, g, units.pop(0))
                    if not gi:
                        some(4)
                        forget(l)
                        continue
                    some(1)
                    read_qk(l, gi - 1, before)
                    if before == "A":
                        stick_softplus(l)
                    else:
                        softmax(l, gi - 1, before)
                    if g is None:
                        first_high(l)
                    some(1)
                    if before == "A":
                        stick_exp(l, gi - 1)
                    some(1)
                    if before != "A":
                        read_p(l, before)
                    some(5)
                    read_oT(l, before)
                norm(l, "y")

            def high(l, i, kind, step, use, cols=FT, first=False):
                act.wait_ge(s_raw[i][kind], (use + 1) * 16)
                if not first:
                    act.wait_ge((g_full, u_full, d_full)[kind], step * 2)
                for q in range(QUARTERS):
                    act.activation(quarter_r(HIGH[l][kind], q, cols), quarter(SETS[l][i][kind], q, cols),
                                   ACT.Copy).then_inc(hi_ready[kind], 1)

            def first_high(l):
                act.wait_ge(pr_full, l * NPF + PUNIT["B", 1] + 1)
                act.wait_ge(s_tabm, l + 1)
                for kind in range(2 - l):
                    high(l, 0, kind, l * DENSE_STEPS, l * (DENSE_STEPS // 2), hidden_cols(0, l == 0), first=True)

            def silu(bufs, done, count, cols):
                act.wait_ge(g_full, done)
                act.activation(hid[bufs][:, 0:cols], ps[:, 2 * bufs, 0:cols], ACT.Silu).then_inc(silu_ready, count)

            def hidden_high(bufs, done, count, cols):
                act.wait_ge(t_full, done)
                act.activation(hh_r[:, bufs, 0:cols], ps[:, 2 * bufs, 0:cols], ACT.Copy).then_inc(hh_ready, count)

            def all_tokens(l, n, first_step, use, parity):
                def one(s, i, step, use_, loop):
                    cols = hidden_cols(s, l == 0)
                    silu(0, step * 2 + 1, 1, cols)
                    high(l, i, 2, step, use_, cols, first=(s == 0 and l == 0))
                    hidden_high(0, step * 2 + 1, 1, cols)
                    unless_last(act, s, n, loop, lambda: high(l, 1 - i, 0, step + 1, use_ + i))
                    silu(1, step * 2 + 2, 1, cols)
                    unless_last(act, s, n, loop, lambda: high(l, 1 - i, 1, step + 1, use_ + i))
                    hidden_high(1, step * 2 + 2, 1, cols)
                steps(act, one, n, first_step, use, parity)

            attention(0)
            all_tokens(0, DENSE_STEPS, 0, 0, 0)

            attention(1)
            act.wait_ge(r_dve, R_DIFF)
            act.activation(em[:], dm[:], ACT.Exp).then_inc(r_act, 1)
            act.wait_ge(r_dve, R_ALL)

            def expert(pair, p, e, first_step, use):
                n_e = act.value_load(cnt[0:1, ds(e, 1)], min_val=0, max_val=T)

                def up_high():
                    high(1, p, 1, first_step, use)

                def next_gate_high():
                    next_expert(act, pair, p, lambda: high(1, 1 - p, 0, first_step + EXPERT_STEPS, use + (EXPERT_STEPS + p) // 2))

                def run(n):
                    act.wait_ge(whole, e + 1)
                    if n == T:
                        act.wait_ge(u_full, first_step * 2)
                        act.activation(xh_r, hT[:], ACT.Copy).then_inc(gx_act, KD)
                        up_high()
                        all_tokens(1, EXPERT_STEPS, first_step, use, p)
                        next_gate_high()
                        act.sem_inc(ye_act, 1)
                        return
                    for k in range(KD):
                        if k % 4 == 0:
                            act.wait_ge(gx_full, e * 3 + (k // 4 + 1))
                        c = G_FFN + KD + k
                        act.activation(xeh_r[:, k, :], ps[:, 4 + k // 4, (k % 4) * P:(k % 4 + 1) * P], ACT.Copy,
                                       scale=gT[:, c:c + 1]).then_inc(gx_act, 1)
                    up_high()

                    def one(s, i, step, use_, loop):
                        silu(i, step * 2 + 2, 2, FT)

                        def next_high():
                            for kind in range(2):
                                high(1, 1 - i, kind, step + 1, use_ + i)
                        unless_last(act, s, EXPERT_STEPS, loop, next_high)
                        hidden_high(i, step * 2 + 2, 2, FT)
                        high(1, i, 2, step, use_)
                    steps(act, one, EXPERT_STEPS, first_step, use, p)
                    act.wait_ge(d_full, first_step * 2 + 2 * EXPERT_STEPS)
                    act.activation(ye[:, 512:1024], ps[:, 5, :], ACT.Copy).then_inc(ye_act, 1)
                    next_gate_high()
                by_count(act, n_e, run)
            pairs(act, expert)

        @block.gpsimd
        def _(pool):
            pool.memset(mhalf[:], -0.5).then_inc(rx_part, 1)
            done = [1]

            def rstd(mean, total, scale, out_, part, ready, value):
                pool.tensor_scalar(mean, total, scale, EPS, ALU.mult, ALU.add).then_inc(part, 1)
                pool.wait_ge(part, value)
                n = mean.shape[-1]
                pool.tensor_tensor(out_, mean, mhalf[:, 0:n], ALU.pow).then_inc(ready, 1)

            def norm(l, name):
                n = 2 * l + (name == "y")
                pool.wait_ge(ssx_ready, NT * (n + 1))
                if not n:
                    pool.wait_ge(rx_part, 1)
                rstd(rx0[:], ssx[:], 1.0 / D, rx[:], rx_part, rx_ready, n + 2)

            def unit_rstd(l, g, u):
                n = NORMED[g, u] + l * len(NORMED)
                k = 6 if g == "B" else 8
                pool.wait_ge(ssq_ready, n + 1)
                rstd(rq0[:, u, 0:k], ssq[:, u, 0:k], 1.0 / HD, rq[:, u, 0:k], rq_part, rq_ready, n + 1)

            def group_rstd(l, gi):
                n = 4 * l + gi
                pool.wait_ge(sso_ready, NT * (n + 1))
                rstd(ro0[:], sso[:], 1.0 / GW, ro[:], ro_part, ro_ready, n + 1)

            for l in range(L):
                norm(l, "x")
                for gi, g in enumerate(ORDER + [None]):
                    if g is not None and g != "A":
                        unit_rstd(l, g, 0)
                    if g is not None and g != "A":
                        unit_rstd(l, g, 1)
                    if gi:
                        group_rstd(l, gi - 1)
                    if gi == 1:
                        pool.wait_ge(s_tabc, 16 * (l + 1))
                        pool.wait_ge(pr_full, l * NPF + PUNIT["D", 3] + 1)
                        for h in range(H):
                            for c0, c1 in ((0, P), (P, SC)):
                                keys = c1 - c0
                                backward = bass.AP(tensor=hankels[l].tensor, offset=hankels[l].offset + h * T + keys - 1,
                                                   ap=[list(hankels[l].ap[0]), [-1, keys]])
                                ins = pool.tensor_tensor(tabCs[l][:, h, c0:c1], backward,
                                                         con[:, C_BLOCK + c0:C_BLOCK + c1], ALU.add)
                        ins.then_inc(s_tabm, 1)
                norm(l, "y")

        @block.vector
        def _(dve):
            def norm(l, name):
                n = 2 * l + (name == "y")
                dve.wait_ge(rx_ready, n + 1)
                for t in range(NT):
                    dve.tensor_scalar(xs[:, t, :], x[:, t, :], rx[:, t:t + 1], None, ALU.mult).then_inc(xs_ready, 1)
                if name == "y" and l == 0:
                    for i in range(4):
                        dve.wait_ge(xh_ready, i + 1)
                        for kk in range(2):
                            k = 2 * i + kk
                            c = G_FFN + l * KD + k
                            ins = dve.scalar_tensor_tensor(
                                out=hT_r[:, k, :], in0=bank((name, i))[:, kk * T:(kk + 1) * T],
                                scalar=gT[:, c:c + 1], in1=xh_r[:, k, :], op0=ALU.mult, op1=ALU.subtract)
                        ins.then_inc(tr_free[i % 2], 1)
                    return
                for i in (0, 2):
                    filled(dve, l, (name, i))
                    for kk in range(2):
                        k = 2 * i + kk
                        c = (G_FFN if name == "y" else G_MIX) + l * KD + k
                        ins = dve.tensor_scalar(hT[:, k, :], bank((name, i))[:, kk * T:(kk + 1) * T], gT[:, c:c + 1],
                                                None, ALU.mult)
                    ins.then_inc(tr_free[0], 1)

            def spread(ap, n, width):
                return ap.unsqueeze(2).broadcast_to([P, n, width])

            def read_unit(l, gi, g, u):
                if u >= 2:
                    return
                m = PUNIT[g, u]
                dve.wait_ge(pr_full, l * NPF + m + 1)
                if g == "A":
                    filled(dve, l, (ORDER[gi - 1], "qk", u))
                    dve.tensor_copy(stage[:, u, :], pbank(m)[:, :]).then_inc(pr_free[m % 2], 1)
                    return
                n = NORMED[g, u] + l * len(NORMED)
                k = 6 if g == "B" else 8
                dve.wait_ge(sq_ready, n + 1)
                dve.tensor_reduce(ssq[:, u, 0:k], sq[:, 0:k * HD].rearrange("p (h c) -> p h c", c=HD), AX.X, ALU.add) \
                    .then_inc(ssq_ready, 1)
                if gi:
                    filled(dve, l, (ORDER[gi - 1], "qk", u))
                dve.wait_ge(rq_ready, n + 1)
                if g == "B":
                    for half in range(2):
                        src = pbank(m)[:, half * P:(half + 1) * P].rearrange("p (b c) -> p b c", c=HD)
                        dst = stage[:, u, 0:2 * P].rearrange("p (b a c) -> p b a c", b=2, a=2)[:, :, half, :]
                        dve.tensor_tensor(dst, src, spread(rq[:, u, 2 * half:2 * half + 2], 2, HD), ALU.mult)
                    dve.tensor_tensor(stage[:, u, 2 * P:3 * P].rearrange("p (h c) -> p h c", c=HD),
                                      pbank(m)[:, 2 * P:3 * P].rearrange("p (h c) -> p h c", c=HD),
                                      spread(rq[:, u, 4:6], 2, HD), ALU.mult)
                    filled(dve, l, (ORDER[gi - 2], "o"))
                    dve.tensor_copy(vbuf[:, gi % 2, u, 0:P], pbank(m)[:, 3 * P:4 * P]).then_inc(pr_free[m % 2], 1)
                else:
                    dve.tensor_tensor(stage[:, u, :].rearrange("p (h c) -> p h c", c=HD),
                                      pbank(m)[:, :].rearrange("p (h c) -> p h c", c=HD),
                                      spread(rq[:, u, :], 8, HD), ALU.mult).then_inc(pr_free[m % 2], 1)

            def forget(l):
                for m in (2, 3):
                    dve.wait_ge(pr_free[m % 2], l * (NPF // 2) + 2)
                dve.tensor_tensor(fu[:], fraw[:], bfr[:, l:l + 1, :].broadcast_to([P, NT, H]), ALU.add).then_inc(f_dve, 1)
                dve.wait_ge(f_dve, 3 * l + 1)
                dve.tensor_scalar(fr[:], fu[:], -1.0, 0.0, ALU.mult, ALU.max).then_inc(f_dve, 1)
                dve.wait_ge(f_dve, 3 * l + 2)
                dve.wait_ge(f_act, 3 * l + 3)
                dve.tensor_tensor(fsp[:], fr[:], fl[:], ALU.add).then_inc(f_dve, 1)
                dve.wait_ge(f_dve, 3 * l + 3)
                dve.tensor_copy(spbs[l], spread(fsp[:].rearrange("p a b -> p (a b)"), NT * H, P)).then_inc(spb_ready, 1)

            def table_d(l):
                dve.wait_ge(sc_full, l * NSU + SUSE["Dsum"] + 1)
                for c0, c1 in ((0, P), (P, SC)):
                    ins = dve.tensor_tensor(L2s[l][:, :, c0:c1], ps[:, 2:2 + H, 0:c1 - c0],
                                            con[:, C_CAUSAL + c0:C_CAUSAL + c1].unsqueeze(1).broadcast_to([P, H, c1 - c0]),
                                            ALU.add)
                ins.then_inc(sc_free, 1)
                dve.wait_ge(sc_free, l * NSU + SUSE["Dsum"] + 1)

            def softmax(l, gi, g):
                dve.wait_ge(sc_full, l * NSU + SUSE[g] + 1)
                if g == "C":
                    dve.wait_ge(s_tabm, l + 1)
                if g == "B":
                    table = con[:, C_ALIBI:C_ALIBI + H * SC].rearrange("p (h c) -> p h c", h=H)
                else:
                    table = {"D": L2s[l], "C": tabCs[l]}[g]
                if gi:
                    filled(dve, l, (ORDER[gi - 1], "o"))
                dve.tensor_tensor(Lbufs[l], ps[:, 2:2 + H, 0:SC], table, ALU.add).then_inc(sc_free, 1)
                dve.wait_ge(sc_free, l * NSU + SUSE[g] + 1)
                dve.tensor_reduce(nm[:, 0:H], Lbufs[l][:, :, 0:P], AX.X, ALU.max, negate=True)
                ins = dve.tensor_reduce(nm[:, H:2 * H], Lbufs[l][:, :, P:SC], AX.X, ALU.max, negate=True)
                if g == "B":
                    ins.then_inc(mx_part, 1)
                    dve.wait_ge(mx_part, 2 * l + 1)
                    ns = nsink[:, l, :, :].rearrange("p a b -> p (a b)")
                    dve.tensor_tensor(nm[:], nm[:], ns, ALU.min).then_inc(m_ready, 1)
                    dve.wait_ge(m_ready, 3 * l + 3)
                    dve.tensor_tensor(esink[:], nm[:], sink[:, l, :, :].rearrange("p a b -> p (a b)"), ALU.add) \
                        .then_inc(mx_part, 1)
                else:
                    ins.then_inc(m_ready, 1)

            def stick_relu(l):
                dve.wait_ge(sc_full, l * NSU + SUSE["Az"] + 1)
                dve.tensor_scalar(L2s[l], ps[:, 2:2 + H, 0:SC], 0.0, None, ALU.max).then_inc(a_relu, 1)

            def read_p(l, g):
                for h in (0, 2):
                    filled(dve, l, (g, "p", h))
                    dve.tensor_copy(pTs[l][:, h, :], bank((g, "p", h))[:, 0:SC]).then_inc(tr_free[FILL[g, "p", h] % 2], 1)

            def inverse(l, g):
                n = 3 * l + SOFT.index(g)
                dve.wait_ge(p_ready, 4 * (4 * l + ORDER.index(g)) + H)
                if g == "B":
                    dve.wait_ge(es_ready, l + 1)
                    dve.tensor_tensor(rsum[:], rsum[:], esink[:], ALU.add).then_inc(rs_part, 1)
                    dve.wait_ge(rs_part, l + 1)
                dve.reciprocal(rinv[:], rsum[:]).then_inc(ri_ready, 1)
                dve.wait_ge(ri_ready, n + 1)

            def group_out(l, gi, g):
                filled(dve, l, (g, "o"))
                if gi:
                    filled(dve, l, (ORDER[gi - 1], "oT"))
                o = obuf[:].rearrange("p a (h c) -> p (a h) c", c=HD)
                b = FILL[g, "o"] % 2
                src = bank((g, "o"))[:, :].rearrange("p (n c) -> p n c", c=HD)
                if g == "A":
                    dve.tensor_copy(o, src).then_inc(tr_free[b], 1)
                else:
                    dve.tensor_tensor(o, src, spread(rinv[:], 8, HD), ALU.mult).then_inc(tr_free[b], 1)
                emptied(dve, l, (g, "o"))
                for t in range(NT):
                    dve.tensor_tensor_reduce(out=osq[:, t, :], in0=obuf[:, t, :], in1=obuf[:, t, :], scale=1.0, scalar=0.0,
                                             op0=ALU.mult, op1=ALU.add, accum_out=sso[:, t:t + 1]).then_inc(sso_ready, 1)
                dve.wait_ge(ro_ready, 4 * l + gi + 1)
                for t in range(NT):
                    ins = dve.tensor_scalar(obuf[:, t, :], obuf[:, t, :], ro[:, t:t + 1], None, ALU.mult)
                ins.then_inc(o_ready, 1)

            def add_out(l):
                for half in range(2):
                    dve.wait_ge(pr_full, l * NPF + NPU + half + 1)
                    dve.tensor_tensor(x[:, 0, half * 512:(half + 1) * 512], ps[:, half, :],
                                      x[:, 0, half * 512:(half + 1) * 512], ALU.add).then_inc(pr_free[half], 1)
                dve.wait_ge(sc_full, (l + 1) * NSU)
                dve.tensor_tensor(x[:, 1, 0:512], ps[:, 2, :], x[:, 1, 0:512], ALU.add)
                dve.tensor_tensor(x[:, 1, 512:D], ps[:, 3, :], x[:, 1, 512:D], ALU.add).then_inc(sc_free, 1)

            def attention(l):
                norm(l, "x")
                for gi, g in enumerate(ORDER + [None]):
                    before = ORDER[gi - 1] if gi else None
                    units = list(range(len(UNITS[g]))) if g else []

                    def some(n):
                        for _ in range(n):
                            if units:
                                read_unit(l, gi, g, units.pop(0))
                    if not gi:
                        some(4)
                        forget(l)
                        continue
                    if before == "D":
                        table_d(l)
                    scale_qk(dve, l, gi - 1, before, 0)
                    if before == "A":
                        stick_relu(l)
                        stick_softplus(l)
                    else:
                        softmax(l, gi - 1, before)
                    if g is None:
                        for kind in range(2 - l):
                            low(l, 0, kind, l * DENSE_STEPS, hidden_cols(0, l == 0))
                    some(2)
                    if before == "A":
                        stick_logits(l, gi - 1)
                    else:
                        read_p(l, before)
                        inverse(l, before)
                    group_out(l, gi - 1, before)
                add_out(l)
                norm(l, "y")

            def stick_softplus(l):
                m = con[:, C_AMASK:C_AMASK + SC].unsqueeze(1).broadcast_to([P, H, SC])
                dve.wait_ge(a_abs, 2 * (l + 1))
                dve.tensor_tensor(L2s[l], L2s[l], Lbufs[l], ALU.add).then_inc(a_sp, 1)
                dve.wait_ge(a_sp, 2 * l + 1)
                dve.tensor_tensor(L2s[l], L2s[l], m, ALU.mult).then_inc(a_sp, 1)

            def stick_logits(l, gi):
                m = con[:, C_ANEG:C_ANEG + SC].unsqueeze(1).broadcast_to([P, H, SC])
                dve.wait_ge(sc_full, l * NSU + SUSE["Aw"] + 1)
                dve.tensor_tensor(Lbufs[l], ps[:, 2:2 + H, 0:SC], m, ALU.add).then_inc(sc_free, 1)
                dve.wait_ge(sc_free, l * NSU + SUSE["Aw"] + 1)

            def low(l, i, kind, step, cols=FT):
                for q in range(QUARTERS):
                    dve.wait_ge(hi_ready[kind], step * QUARTERS + (q + 1))
                    u = SETS[l][i][kind]
                    dve.tensor_tensor(quarter_r(u, q, cols), quarter(u, q, cols),
                                      quarter_r(HIGH[l][kind], q, cols), ALU.subtract).then_inc(lo_ready[kind], 1)

            def hidden(bufs, done, count, cols):
                dve.wait_ge(silu_ready, done)
                dve.wait_ge(u_full, done)
                dve.tensor_tensor(hid[bufs][:, 0:cols], ps[:, 2 * bufs + 1, 0:cols], hid[bufs][:, 0:cols], ALU.mult) \
                    .then_inc(h_ready, count)

            def hidden_low(bufs, done, count, cols):
                dve.wait_ge(hh_ready, done)
                dve.tensor_tensor(hl_r[:, bufs, 0:cols], ps[:, 2 * bufs, 0:cols], hh_r[:, bufs, 0:cols],
                                  ALU.subtract).then_inc(hl_ready, count)

            def all_tokens(l, n, first_step, use, parity):
                def one(s, i, step, use_, loop):
                    cols = hidden_cols(s, l == 0)
                    hidden(0, step * 2 + 1, 1, cols)
                    low(l, i, 2, step, cols)
                    hidden_low(0, step * 2 + 1, 1, cols)
                    unless_last(dve, s, n, loop, lambda: low(l, 1 - i, 0, step + 1))
                    hidden(1, step * 2 + 2, 1, cols)
                    unless_last(dve, s, n, loop, lambda: low(l, 1 - i, 1, step + 1))
                    hidden_low(1, step * 2 + 2, 1, cols)
                steps(dve, one, n, first_step, use, parity)

            def router():
                rev = con[:, C_REV:C_REV + E].unsqueeze(1).broadcast_to([P, NT, E])
                count = [0]

                def done(ins):
                    count[0] += 1
                    ins.then_inc(r_dve, 1)
                    dve.wait_ge(r_dve, count[0])

                def first_largest(values, top, onehot):
                    done(dve.tensor_reduce(top[:], values[:], AX.X, ALU.max))
                    done(dve.tensor_tensor(tmp[:], values[:], spread(top[:], NT, E), ALU.is_equal))
                    done(dve.tensor_tensor(tmp[:], tmp[:], rev, ALU.mult))
                    done(dve.tensor_reduce(r1[:], tmp[:], AX.X, ALU.max))
                    done(dve.tensor_tensor(onehot[:], rev, spread(r1[:], NT, E), ALU.is_equal))

                dve.wait_ge(r_pe, 1)
                done(dve.tensor_copy(lg[:], ps[:, 0, 0:NT * E].rearrange("p (a e) -> p a e", e=E)))
                first_largest(lg, m1, one1)
                done(dve.tensor_scalar(tmp[:], one1[:], NEG, None, ALU.mult))
                done(dve.tensor_tensor(lg2[:], lg[:], tmp[:], ALU.add))
                first_largest(lg2, m2, one2)
                done(dve.tensor_tensor(dm[:], m2[:], m1[:], ALU.subtract))
                assert count[0] == R_DIFF
                done(dve.tensor_tensor(mask[:], one1[:], one2[:], ALU.add))
                assert count[0] == R_MASK
                dve.wait_ge(r_act, 1)
                done(dve.tensor_scalar(em1[:], em[:], 1.0, None, ALU.add))
                done(dve.reciprocal(p1[:], em1[:]))
                done(dve.tensor_tensor(p2[:], em[:], p1[:], ALU.mult))
                done(dve.tensor_tensor(gates[:, :, 0:E], one1[:], spread(p1[:], NT, E), ALU.mult))
                done(dve.tensor_tensor(tmp[:], one2[:], spread(p2[:], NT, E), ALU.mult))
                done(dve.tensor_tensor(gates[:, :, 0:E], gates[:, :, 0:E], tmp[:], ALU.add))
                dve.wait_ge(r_pe, 2)
                done(dve.scalar_tensor_tensor(out=slot[:, :, 0:E], in0=ps[:, 1, 0:NT * E].rearrange("p (a e) -> p a e", e=E),
                                              scalar=1.0, in1=mask[:], op0=ALU.add, op1=ALU.mult))
                done(dve.tensor_scalar(slot[:, :, 0:E], slot[:, :, 0:E], -1.0, None, ALU.add))
                done(dve.memset(slot[:, :, E:E + 1], -1.0))
                done(dve.memset(gates[:, :, E:E + 1], 0.0))
                done(dve.tensor_copy(cnt[:], ps[:, 1, NT * E:(NT + 1) * E]))
                assert count[0] == R_ALL

            dve.wait_ge(gains_T, 1)
            dve.tensor_copy(gT[:], ps[:, 0, 0:G_ALL]).then_inc(gains, 1)
            dve.wait_ge(gains, 1)
            dve.tensor_scalar(gT[:, G_Q:G_K], gT[:, G_Q:G_K], SCALE, None, ALU.mult).then_inc(gains, 1)
            dve.wait_ge(s_small, 16 * 3)
            dve.tensor_scalar(nsink[:], sink[:], -1.0, None, ALU.mult).then_inc(gains, 1)
            dve.wait_ge(gains, 3)

            attention(0)
            all_tokens(0, DENSE_STEPS, 0, 0, 0)
            for t in range(NT):
                dve.wait_ge(d_full, 2 * DENSE_STEPS - 1 + t)
                for half in range(2):
                    xt = x[:, t, half * 512:(half + 1) * 512]
                    dve.tensor_tensor(xt, ps[:, 4 + 2 * t + half, :], xt, ALU.add).then_inc(x_added, 1)

            attention(1)
            router()

            def select(e):
                iota = con[:, C_IOTA:C_IOTA + P]
                for t in range(NT):
                    at, gate = slot[:, t, ds(e, 1)], gates[:, t, ds(e, 1)]
                    dve.tensor_scalar(sel[:, t, :], iota, at, None, ALU.is_equal)
                    ins = dve.tensor_scalar(selg[:, t, :], iota, at, gate, ALU.is_equal, ALU.mult)
                ins.then_inc(sel_ready, 1)

            select(0)
            dve.sem_inc(whole, 1)

            def expert(pair, p, e, first_step, use):
                n_e = dve.value_load(cnt[0:1, ds(e, 1)], min_val=0, max_val=T)

                def up_low():
                    low(1, p, 1, first_step)

                def next_gate_low():
                    next_expert(dve, pair, p, lambda: low(1, 1 - p, 0, first_step + EXPERT_STEPS))

                def run(n):
                    if n == T:
                        dve.wait_ge(gx_act, e * KD + KD)
                        dve.tensor_tensor(hT_r[:], hT[:], xh_r, ALU.subtract).then_inc(gx_dve, KD)
                        dve.sem_inc(gx_back, 1)
                        up_low()
                        all_tokens(1, EXPERT_STEPS, first_step, use, p)
                        next_gate_low()
                        dve.wait_ge(u_full, first_step * 2 + 2 * EXPERT_STEPS)
                        dve.tensor_tensor(hT[:], hT_r[:], xh_r, ALU.add).then_inc(whole, 1)
                        dve.wait_ge(gx_full, e * 3 + 3)
                        select(e + 1)
                        dve.sem_inc(ye_dve, 1)
                        for t in range(NT):
                            dve.wait_ge(d_full, first_step * 2 + (2 * EXPERT_STEPS - 1 + t))
                            for half in range(2):
                                xt = x[:, t, half * 512:(half + 1) * 512]
                                dve.scalar_tensor_tensor(out=xt, in0=ps[:, 4 + 2 * t + half, :], scalar=gates[:, t, ds(e, 1)],
                                                         in1=xt, op0=ALU.mult, op1=ALU.add).then_inc(x_added, 1)
                        return
                    for k in range(KD):
                        c = G_FFN + KD + k
                        if k % 4 == 0:
                            dve.wait_ge(gx_act, e * KD + (k + 4))
                        dve.scalar_tensor_tensor(out=xel_r[:, k, :], in0=ps[:, 4 + k // 4, (k % 4) * P:(k % 4 + 1) * P],
                                                 scalar=gT[:, c:c + 1], in1=xeh_r[:, k, :], op0=ALU.mult, op1=ALU.subtract) \
                            .then_inc(gx_dve, 1)
                    dve.wait_ge(gx_full, e * 3 + 3)
                    dve.tensor_copy(back[:], ps[:, 2 * p + 1, 0:T]).then_inc(gx_back, 1)
                    up_low()

                    def one(s, i, step, use_, loop):
                        hidden(i, step * 2 + 2, 2, FT)

                        def next_low():
                            for kind in range(2):
                                low(1, 1 - i, kind, step + 1)
                        unless_last(dve, s, EXPERT_STEPS, loop, next_low)
                        hidden_low(i, step * 2 + 2, 2, FT)
                        low(1, i, 2, step)
                    steps(dve, one, EXPERT_STEPS, first_step, use, p)
                    select(e + 1)
                    dve.wait_ge(d_full, first_step * 2 + 2 * EXPERT_STEPS)
                    dve.tensor_copy(ye[:, 0:512], ps[:, 4, :]).then_inc(ye_dve, 1)
                    next_gate_low()
                    for t in range(NT):
                        for half in range(2):
                            k = 2 * t + half
                            xt = x[:, t, half * 512:(half + 1) * 512]
                            dve.wait_ge(e_full, e * 4 + (k + 1))
                            dve.tensor_tensor(xt, ps[:, (6, 2 * p)[t] + half, :], xt, ALU.add).then_inc(x_added, 1)
                    dve.sem_inc(whole, 1)
                by_count(dve, n_e, run)
            pairs(dve, expert)


_INS = ["x", "g_mix", "w_in", "b_f", "g_q", "g_k", "swa_sinks", "rel_bias", "g_out", "w_out", "g_ffn",
        "w_ff_gate", "w_ff_up", "w_ff_down", "w_router", "w_exp_gate", "w_exp_up", "w_exp_down"]
_OUTS = [((1, 256, 1024), "float32")]


def kernel(**inputs):
    import numpy as _np
    import concourse.bacc as _bacc
    from concourse import mybir as _mybir
    from concourse.bass_utils import run_bass_kernel_spmd as _run

    nc = _bacc.Bacc("TRN2", target_bir_lowering=False, num_devices=1)
    arrays, args = {}, []
    given = {name: inputs[name] for name in _INS}
    given["consts"] = shape_constants()
    for name, value in given.items():
        a = _np.ascontiguousarray(value)
        arrays[f"in_{name}_dram"] = a
        args.append(nc.dram_tensor(f"in_{name}_dram", a.shape, _mybir.dt.from_np(a.dtype), kind="ExternalInput").ap())
    for i, (shape, dtype) in enumerate(_OUTS):
        dt = _mybir.dt.from_np(_np.dtype(dtype))
        args.append(nc.dram_tensor(f"out_{i}_dram", shape, dt, kind="ExternalOutput").ap())
    trunk(nc, *args)
    r = _run(nc, [arrays], core_ids=[0])
    got = tuple(r.results[0][f"out_{i}_dram"] for i in range(len(_OUTS)))
    return got[0]
```

```python
from contextlib import ExitStack

import numpy as np

import concourse.bass as bass
from concourse import mybir

ALU = mybir.AluOpType
ACT = mybir.ActivationFunctionType
AX = mybir.AxisListType
F32 = mybir.dt.float32
F32R = mybir.dt.float32r
I32 = mybir.dt.int32
ds = bass.ds

P = 128
T = 256
NT = T // P
D = 1024
KD = D // P
L = 2
H = 4
HD = 64
GW = H * HD
EPS = 1e-6
SCALE = HD ** -0.5
NEG = -1e30
FD = 2816
FE = 3584
E = 8
CLIP = 128
RB = 2 * CLIP + 1
EXT = 384
SC = 3 * P

ORDER = ["D", "A", "C", "B"]
COL0 = {"A": 0, "B": 768, "C": 1280, "D": 2048}
COLS = {"A": 768, "B": 512, "C": 768, "D": 772}
CAT = {"A": 0, "B": 1, "C": 2, "D": 3}
QK = {"B": 0, "C": 1, "D": 2}
YB = (6, 4)
UNIT = 4096
WIN = [{}, {}]
_at = 0
for _g in ORDER:
    WIN[0][_g] = _at
    _at += KD * COLS[_g]
WIN[1]["D"] = 2 * UNIT
WIN[1]["A"] = WIN[1]["D"] + KD * COLS["D"]
WIN[1]["C"] = 0
WIN[1]["B"] = 8 * UNIT
HANKEL = [_at, WIN[1]["A"] + KD * COLS["A"]]
SETS = [[(8, 2, 3), (0, 1, 6)], [(4, 5, 0), (2, 3, 6)]]
HIGH = [(4, 5, 7), (1, 8, 7)]
UNITS = {g: [(0, 512, 0), (0, 512, 1)] + ([] if g == "B" else [(512, COLS[g] - 512, 0), (512, COLS[g] - 512, 1)])
         for g in ORDER}

FT = 512
QUARTERS = 4

FILLS = [("x", i) for i in range(4)]
for _i, _g in enumerate(ORDER):
    FILLS += [(_g, "qk", 0), (_g, "qk", 1)]
    if _i:
        FILLS += [(ORDER[_i - 1], "oT")]
    if _g != "A":
        FILLS += [(_g, "p", h) for h in range(H)]
    FILLS += [(_g, "o")]
FILLS += [(ORDER[-1], "oT")]
FILLS += [("y", i) for i in range(4)]
FILL = {name: n for n, name in enumerate(FILLS)}
NFILL = len(FILLS)
assert NFILL % 2 == 0
PUNIT = {}
for _g in ORDER:
    for _u in range(len(UNITS[_g])):
        PUNIT[_g, _u] = len(PUNIT)
NPU = len(PUNIT)
NPF = NPU + 2
SUSE = {n: i for i, n in enumerate(["Dsum", "D", "Az", "Aw", "C", "B", "out"])}
NSU = len(SUSE)

C_ID, C_UP, C_NEGLOW = 0, 128, 128 + 257
C_AMASK = C_NEGLOW + 256
C_ANEG, C_CAUSAL, C_BLOCK = C_AMASK + SC, C_AMASK + 2 * SC, C_AMASK + 3 * SC
C_ALIBI = C_AMASK + 4 * SC
C_IOTA = C_ALIBI + H * SC
C_REV = C_IOTA + P
C_ALL = C_REV + E
G_MIX, G_FFN, G_OUT, G_Q, G_K = 0, L * KD, 2 * L * KD, 3 * L * KD, 3 * L * KD + 3 * L
G_ALL = G_K + 3 * L


NORMED = {(g, u): n for n, (g, u) in enumerate((g, u) for g in ORDER if g != "A" for u in range(2))}
SOFT = [g for g in ORDER if g != "A"]
R_DIFF, R_MASK, R_ALL = 14, 15, 26


def shape_constants():
    c = np.zeros((P, C_ALL), np.float32)
    p = np.arange(P)[:, None]
    c[:, C_ID:C_ID + P] = p == np.arange(P)[None]
    c[:, C_UP:C_UP + 257] = p <= np.arange(257)[None] - 1
    c[:, C_NEGLOW:C_NEGLOW + 256] = -(p >= np.arange(256)[None] - P).astype(np.float32)
    col = np.arange(SC)[None]
    s, t = np.where(col < 256, p, p + P), np.where(col < 256, col, col - P)
    c[:, C_AMASK:C_AMASK + SC] = s < t
    c[:, C_ANEG:C_ANEG + SC] = np.where(s < t, 0.0, NEG)
    t, s = np.where(col < P, p, p + P), np.where(col < P, col, col - P)
    c[:, C_CAUSAL:C_CAUSAL + SC] = np.where(s <= t, 0.0, NEG)
    c[:, C_BLOCK:C_BLOCK + SC] = np.where(s // 64 <= t // 64, 0.0, NEG)
    back = t // 64 - s // 64
    for h in range(H):
        slope = 2.0 ** (-8.0 * (h + 1) / H)
        c[:, C_ALIBI + h * SC:C_ALIBI + (h + 1) * SC] = np.where((back >= 0) & (back <= 1), -slope * np.abs(t - s), NEG)
    c[:, C_IOTA:C_IOTA + P] = np.arange(P)[None]
    c[:, C_REV:C_REV + E] = E - np.arange(E)[None]
    return c


def trunk(nc, x_in, g_mix, w_in, b_f, g_q, g_k, swa_sinks, rel_bias, g_out, w_out, g_ffn,
          w_ff_gate, w_ff_up, w_ff_down, w_router, w_exp_gate, w_exp_up, w_exp_down, consts, out):
    with ExitStack() as ctx:
        def sb(name, shape, dt=F32):
            return ctx.enter_context(nc.sbuf_tensor(name, shape, dt))

        def sem(name):
            return ctx.enter_context(nc.semaphore(name))

        def sb_both(name, shape):
            with nc.sbuf_tensor(name, shape, F32) as plain:
                pass
            return plain, ctx.enter_context(nc.sbuf_tensor(name + "_rounded", shape, F32R))

        ext = nc.dram_tensor("ext_rel_bias", [L, H, EXT], F32).ap()

        with nc.sbuf_tensor("wmem", [P, 9 * UNIT], F32) as wmem:
            pass
        units_r = [sb(f"unit_{u}_rounded", [P, UNIT], F32R) for u in range(9)]
        x = sb("x", [P, NT, D])
        xs = sb("xs", [P, NT, D])
        hT, hT_r = sb_both("hT", [P, KD, T])
        con = sb("con", [P, C_ALL])
        gT = sb("gT", [P, G_ALL])
        grow = sb("grow", [G_ALL, P])
        qkT, qkT_r = sb_both("qkT", [P, 2, 4, T])
        vbuf, vbuf_r = sb_both("vbuf", [P, 2, NT, GW])
        stage, stage_r = sb_both("stage", [P, NT, 512])
        sq = sb("sq", [P, 512])
        obuf = sb("obuf", [P, NT, GW])
        osq = sb("osq", [P, NT, GW])
        bfr = sb("bfr", [P, L, H])
        sink = sb("sink", [P, L, NT, H])
        nsink = sb("nsink", [P, L, NT, H])
        wr = sb("wr", [P, KD, E])
        mhalf = sb("mhalf", [P, 8])
        ssx = sb("ssx", [P, NT])
        rx0 = sb("rx0", [P, NT])
        rx = sb("rx", [P, NT])
        ssq = sb("ssq", [P, 2, 8])
        rq0 = sb("rq0", [P, 2, 8])
        rq = sb("rq", [P, 2, 8])
        sso = sb("sso", [P, NT])
        ro0 = sb("ro0", [P, NT])
        ro = sb("ro", [P, NT])
        fraw = sb("fraw", [P, NT, H])
        fu = sb("fu", [P, NT, H])
        fa = sb("fa", [P, NT, H])
        fe = sb("fe", [P, NT, H])
        fl = sb("fl", [P, NT, H])
        fr = sb("fr", [P, NT, H])
        fsp = sb("fsp", [P, NT, H])
        nm = sb("nm", [P, NT * H])
        rsum = sb("rsum", [P, NT * H])
        rinv = sb("rinv", [P, NT * H])
        esink = sb("esink", [P, NT * H])
        lg = sb("lg", [P, NT, E])
        lg2 = sb("lg2", [P, NT, E])
        tmp = sb("tmp", [P, NT, E])
        one1 = sb("one1", [P, NT, E])
        one2 = sb("one2", [P, NT, E])
        mask = sb("mask", [P, NT, E])
        gates = sb("gates", [P, NT, E + 1])
        slot = sb("slot", [P, NT, E + 1])
        m1 = sb("m1", [P, NT])
        m2 = sb("m2", [P, NT])
        r1 = sb("r1", [P, NT])
        dm = sb("dm", [P, NT])
        em = sb("em", [P, NT])
        em1 = sb("em1", [P, NT])
        p1 = sb("p1", [P, NT])
        p2 = sb("p2", [P, NT])
        cnt = sb("cnt", [P, E], I32)
        ps = ctx.enter_context(nc.psum_tensor("ps", [P, 8, 512], F32))

        def scratch(l, n, size=H * SC):
            at = WIN[l]["D"] + n * H * SC
            return wmem[:, at:at + size]

        assert 4 * H * SC <= KD * COLS["D"]
        Lbufs, L2s, pTs, tabCs = [[scratch(l, n).rearrange("p (h c) -> p h c", h=H) for l in range(L)] for n in range(4)]
        spbs = [scratch(l, 2, NT * H * P).rearrange("p (n c) -> p n c", c=P) for l in range(L)]
        hankels = [wmem[:, HANKEL[l]:HANKEL[l] + H * T].rearrange("p (h c) -> p h c", h=H) for l in range(L)]
        assert all(5 * UNIT <= at and at + H * T <= 6 * UNIT for at in HANKEL)
        oT = xs
        squares = [[qkT[:, t, :, :].rearrange("p b t -> p (b t)") for t in range(NT)],
                   [stage[:].rearrange("p a b -> p (a b)"), vbuf[:].rearrange("p a b c -> p (a b c)")]]
        def all_t(a):
            return a.rearrange("p (k t) -> p k t", t=T)

        def slots(a, part):
            return a[:, part * KD * P:(part + 1) * KD * P].rearrange("p (k t) -> p k t", t=P)

        qf_r = qkT_r[:].rearrange("p a b t -> p (a b t)")
        xh_r = all_t(qf_r)
        xeh_r = slots(qf_r, 0)
        xel_r = slots(qf_r, 1)
        osf = osq[:].rearrange("p a b -> p (a b)")
        sel = osf[:, 0:T].rearrange("p (a t) -> p a t", t=P)
        selg = osf[:, T:2 * T].rearrange("p (a t) -> p a t", t=P)
        back = [con[:, C_ALIBI + i * T:C_ALIBI + (i + 1) * T] for i in range(2)]
        ye = vbuf[:].rearrange("p a b c -> p (a b c)")
        hh_r = vbuf_r[:].rearrange("p a b c -> p a (b c)")
        hl_r = stage_r
        hid = [sq[:], obuf[:].rearrange("p a b -> p (a b)")]

        def win(l, g):
            return wmem[:, WIN[l][g]:WIN[l][g] + KD * COLS[g]].rearrange("p (k c) -> p k c", k=KD)

        def unit(u, k=KD, cols=FT):
            return wmem[:, u * UNIT:u * UNIT + k * cols].rearrange("p (k c) -> p k c", k=k)

        wo = wmem[:, 6 * UNIT:8 * UNIT].rearrange("p (k c) -> p k c", k=KD)

        s_x = [sem(f"x_{t}_loaded") for t in range(NT)]
        s_id = sem("identity_loaded")
        s_con = sem("consts_loaded")
        s_gain = sem("gain_rows_loaded")
        s_small = sem("biases_loaded")
        s_wr = sem("w_router_loaded")
        s_win = {g: sem(f"w_in_{g}_loaded") for g in ORDER}
        s_wd = [sem("w_in_D_second_half_loaded"), sem("w_in_D_values_loaded")]
        s_wo = [sem(f"w_out_{i}_loaded") for i in range(2)]
        s_raw = [[sem(f"set_{i}_{kind}_loaded") for kind in ("gate", "up", "down")] for i in range(2)]
        hi_ready = [sem(f"high_{kind}_ready") for kind in ("gate", "up", "down")]
        lo_ready = [sem(f"low_{kind}_ready") for kind in ("gate", "up", "down")]
        s_ext = sem("rel_bias_extended")
        s_tabc = sem("rel_table_loaded")
        s_tabm = sem("rel_table_masked")
        s_out = sem("output_stored")
        gains_T = sem("gains_transposed")
        gains = sem("gains_ready")
        ssx_ready = sem("x_squares_summed")
        rx_part = sem("x_mean_ready")
        rx_ready = sem("x_rstd_ready")
        xs_ready = sem("x_scaled")
        tr_full = sem("transposes_done")
        tr_free = [sem(f"transposed_bank_{b}_read") for b in range(2)]
        pr_full = sem("projection_done")
        pr_free = [sem(f"projection_bank_{b}_read") for b in range(2)]
        sc_full = sem("scores_done")
        sc_free = sem("scores_read")
        sq_ready = sem("qk_squared")
        ssq_ready = sem("qk_squares_summed")
        rq_part = sem("qk_mean_ready")
        rq_ready = sem("qk_rstd_ready")
        f_dve = sem("forget_dve_step")
        f_act = sem("forget_act_step")
        spb_ready = sem("forget_spread")
        m_ready = sem("row_max_ready")
        mx_part = sem("row_max_part")
        p_ready = sem("exps_ready")
        es_ready = sem("sink_exp_ready")
        rs_part = sem("row_sum_with_sink")
        ri_ready = sem("row_inverse_ready")
        a_relu = sem("stick_relu_ready")
        a_abs = sem("stick_act_step")
        a_sp = sem("stick_softplus_step")
        o_ready = sem("group_output_step")
        sso_ready = sem("group_squares_summed")
        ro_part = sem("group_mean_ready")
        ro_ready = sem("group_rstd_ready")
        g_full = sem("ffn_gate_done")
        u_full = sem("ffn_up_done")
        silu_ready = sem("ffn_silu_ready")
        h_ready = sem("ffn_hidden_ready")
        t_full = sem("ffn_hidden_transposed")
        hh_ready = sem("ffn_hidden_high_ready")
        hl_ready = sem("ffn_hidden_low_ready")
        d_full = sem("ffn_down_done")
        xh_ready = sem("ffn_in_high_ready")
        e_full = sem("expert_out_spread")
        x_added = sem("ffn_added")
        whole = sem("ffn_in_whole")
        all_high = sem("ffn_in_high_again")
        all_low = sem("ffn_in_low_again")
        r_pe = sem("router_pe_step")
        r_dve = sem("router_dve_step")
        r_act = sem("router_act_step")
        sel_ready = sem("selection_ready")
        gx_full = sem("gather_done")
        gx_dve = sem("gather_low_ready")
        gx_act = sem("gather_high_ready")
        gx_back = sem("slot_to_token_ready")
        ye_dve = sem("expert_out_read_dve")
        ye_act = sem("expert_out_read_act")

        def filled(eng, l, name):
            eng.wait_ge(tr_full, l * NFILL + FILL[name] + 1)

        def emptied(eng, l, name):
            n = FILL[name]
            eng.wait_ge(tr_free[n % 2], l * (NFILL // 2) + n // 2 + 1)

        def bank(name):
            return ps[:, 6 + FILL[name] % 2, :]

        def pbank(m):
            return ps[:, m % 2, :]

        DENSE_STEPS = FD // FT + 1
        EXPERT_STEPS = FE // FT
        assert FD == (DENSE_STEPS - 1) * FT + FT // 2 and DENSE_STEPS % 2 == 0 and EXPERT_STEPS % 2 == 1
        VARIANTS = [P]

        def steps(eng, one, n, first, use, parity):
            peeled = n - 4
            for s in range(peeled):
                one(s, (parity + s) % 2, first + s, use + (parity + s) // 2, None)
            with eng.Fori(0, 2) as i:
                for s in (peeled, peeled + 1):
                    one(s, (parity + s) % 2, eng.snap(i * 2 + (first + s)), eng.snap(i + (use + (parity + s) // 2)), i)

        def pairs(eng, body):
            with eng.Fori(0, E // 2) as pair:
                for p in range(2):
                    body(pair, p, eng.snap(pair * 2 + p), eng.snap(pair * (2 * EXPERT_STEPS) + (DENSE_STEPS + p * EXPERT_STEPS)),
                         eng.snap(pair * EXPERT_STEPS + (DENSE_STEPS // 2 + p * (EXPERT_STEPS // 2))))

        def by_count(eng, n, run):
            def choose(widths):
                if not widths:
                    run(T)
                    return
                with eng.If(n < widths[0] + 1):
                    run(widths[0])
                with eng.Else():
                    choose(widths[1:])
                eng.end_ifs()
            choose(VARIANTS)

        def unless_last(eng, s, n, loop, run):
            if s < n - 3:
                run()
                return
            with eng.If(loop < 1):
                run()
            eng.end_ifs()

        def next_expert(eng, pair, p, run):
            if p == 0:
                run()
                return
            with eng.If(pair < E // 2 - 1):
                run()
            eng.end_ifs()

        def hidden_cols(s, dense):
            return FT // 2 if dense and s == 0 else FT

        def weight(u, kind, cols):
            k, c = (KD, cols) if kind < 2 else (cols // P, D)
            return units_r[u][:, 0:k * c].rearrange("p (k c) -> p k c", k=k)

        def quarter_r(u, q, cols):
            n = KD * cols // QUARTERS
            return units_r[u][:, q * n:(q + 1) * n]

        def quarter(u, q, cols):
            n = KD * cols // QUARTERS
            return wmem[:, u * UNIT + q * n:u * UNIT + (q + 1) * n]

        def scale_qk(eng, l, gi, g, t):
            filled(eng, l, (g, "qk", t))
            nb = 3 if g == "B" else 4
            if g == "A":
                sq_, sk_ = SCALE, 1.0
            else:
                n = l * 3 + QK[g]
                sq_, sk_ = gT[:, G_Q + n:G_Q + n + 1], gT[:, G_K + n:G_K + n + 1]
            for b0, b1, s in ((0, 2, sq_), (2, nb, sk_)):
                dst = qkT[:, gi % 2, b0:b1, t * P:(t + 1) * P]
                src = bank((g, "qk", t))[:, b0 * P:b1 * P].rearrange("p (b c) -> p b c", c=P)
                if t == 0:
                    ins = eng.tensor_scalar(dst, src, s, None, ALU.mult)
                else:
                    ins = eng.activation(dst, src, ACT.Copy, scale=s)
            ins.then_inc(tr_free[FILL[g, "qk", t] % 2], 1)

        block = ctx.enter_context(nc.Block())

        @block.sync
        def _(sp):
            def load_w_in(l, g):
                sp.dma_start(win(l, g), w_in[l, :, COL0[g]:COL0[g] + COLS[g]].rearrange("(k p) c -> p k c", p=P)) \
                    .then_inc(s_win[g], 16)

            def load_w_in_d(l):
                for k0, k1, c0, c1, done in ((0, 4, 0, 2 * GW, s_win["D"]), (4, KD, 0, 2 * GW, s_wd[0]),
                                             (0, KD, 2 * GW, COLS["D"], s_wd[1])):
                    sp.dma_start(win(l, "D")[:, k0:k1, c0:c1],
                                 w_in[l, k0 * P:k1 * P, COL0["D"] + c0:COL0["D"] + c1].rearrange("(k p) c -> p k c", p=P)) \
                        .then_inc(done, 16)

            def load_w_out(l, i):
                sp.dma_start(wo[:, 4 * i:4 * i + 4, :],
                             w_out[l, 512 * i:512 * (i + 1), :].rearrange("(k p) c -> p k c", p=P)).then_inc(s_wo[i], 16)

            def load_up(w, l, i, kind, f0, cols=FT):
                sp.dma_start(unit(SETS[l][i][kind], KD, cols), w[:, ds(f0, cols)].rearrange("(k p) c -> p k c", p=P)) \
                    .then_inc(s_raw[i][kind], 16)

            def load_down(w, l, i, f0, rows=FT):
                sp.dma_start(unit(SETS[l][i][2], rows // P, D), w[ds(f0, rows), :].rearrange("(k p) c -> p k c", p=P)) \
                    .then_inc(s_raw[i][2], 16)

            def extend():
                rows = ext.rearrange("l h c -> (l h) c")
                sp.dma_start(rows[:, 0:RB - 1], rel_bias.rearrange("l h c -> (l h) c")[:, 1:RB]).then_inc(s_ext, 16)
                last = bass.AP(tensor=rel_bias.tensor, offset=rel_bias.offset + RB - 1, 
                               ap=[[RB, L * H], [0, EXT - RB + 1], [1, 1]])
                sp.dma_start(rows[:, RB - 1:EXT].unsqueeze(2), last).then_inc(s_ext, 16)

            def load_table(l):
                sp.wait_ge(s_ext, 16 * 2)
                sp.dma_start(hankels[l], bass.AP(tensor=ext.tensor, offset=ext.offset + l * H * EXT,
                                             ap=[[1, P], [EXT, H], [1, T]])).then_inc(s_tabc, 16)

            for t in range(NT):
                sp.dma_start(x[:, t, :], x_in[0, t * P:(t + 1) * P, :]).then_inc(s_x[t], 16)
            sp.dma_start(con[:, 0:P], consts[:, 0:P]).then_inc(s_id, 16)
            sp.dma_start(grow[G_MIX:G_FFN, :], g_mix.rearrange("l (k c) -> (l k) c", c=P)).then_inc(s_gain, 16)
            sp.dma_start(grow[G_FFN:G_OUT, :], g_ffn.rearrange("l (k c) -> (l k) c", c=P)).then_inc(s_gain, 16)
            sp.dma_start(grow[G_OUT:G_Q, :], g_out.rearrange("l g (k c) -> (l g k) c", c=P)).then_inc(s_gain, 16)
            for half in range(2):
                sp.dma_start(grow[G_Q:G_K, half * HD:(half + 1) * HD], g_q.rearrange("l i c -> (l i) c")).then_inc(s_gain, 16)
                sp.dma_start(grow[G_K:G_ALL, half * HD:(half + 1) * HD], g_k.rearrange("l i c -> (l i) c")).then_inc(s_gain, 16)
            load_w_in_d(0)
            sp.dma_start(con[:, P:C_ALL], consts[:, P:C_ALL]).then_inc(s_con, 16)
            sp.dma_start(bfr[:].rearrange("p l h -> p (l h)"),
                         bass.AP(tensor=b_f.tensor, offset=b_f.offset, ap=[[0, P], [1, L * H]])).then_inc(s_small, 16)
            for t in range(NT):
                sp.dma_start(sink[:, :, t, :],
                             bass.AP(tensor=swa_sinks.tensor, offset=swa_sinks.offset, ap=[[0, P], [H, L], [1, H]])) \
                    .then_inc(s_small, 16)
            load_w_in(0, "A")
            extend()
            load_table(0)
            load_w_in(0, "C")
            load_w_in(0, "B")
            load_w_out(0, 0)
            load_w_out(0, 1)
            sp.dma_start(wr[:], w_router[0].rearrange("(k p) e -> p k e", p=P)).then_inc(s_wr, 16)

            def first_steps(l, gate, up, down, cols):
                if l == 0:
                    load_up(gate, 0, 0, 0, 0, cols)
                sp.wait_ge(pr_full, l * NPF + PUNIT["A", 3] + 1)
                if l:
                    load_up(gate, 1, 0, 0, 0, cols)
                    sp.wait_ge(s_tabm, l + 1)
                    load_up(up, 1, 0, 1, 0, cols)
                sp.wait_ge(pr_full, l * NPF + PUNIT["C", 3] + 1)
                if l == 0:
                    load_up(up, 0, 0, 1, 0, cols)
                load_down(down, l, 0, 0, cols)
                sp.wait_ge(sc_full, l * NSU + SUSE["out"] + 1)
                load_up(gate, l, 1, 0, cols)
                load_up(up, l, 1, 1, cols)
                if l == 0:
                    load_down(down, l, 1, cols)

            def step(l, i, kinds, weights, f0, step_):
                for kind in kinds:
                    sp.wait_ge((g_full, u_full, d_full)[kind], step_ * 2 - 2)
                    if kind < 2:
                        load_up(weights[kind], l, i, kind, f0)
                    else:
                        load_down(weights[2], l, i, f0)

            dense = (w_ff_gate[0], w_ff_up[0], w_ff_down[0])
            first_steps(0, *dense, FT // 2)
            with sp.Fori(1, DENSE_STEPS // 2) as i:
                f0 = i * (2 * FT) - FT // 2
                step(0, 0, (0, 1, 2), dense, f0, sp.snap(i * 2))
                step(0, 1, (0, 1, 2), dense, f0 + FT, sp.snap(i * 2 + 1))

            for done in (g_full, u_full, d_full):
                sp.wait_ge(done, 2 * (DENSE_STEPS - 1))
            load_w_in_d(1)
            load_w_in(1, "B")
            sp.wait_ge(g_full, 2 * DENSE_STEPS)
            sp.wait_ge(u_full, 2 * DENSE_STEPS)
            load_w_in(1, "A")
            load_table(1)
            load_w_in(1, "C")
            sp.wait_ge(d_full, 2 * DENSE_STEPS)
            load_w_out(1, 0)
            load_w_out(1, 1)

            def expert(e):
                if isinstance(e, int):
                    return w_exp_gate[0, e], w_exp_up[0, e], w_exp_down[0, e]
                return [w[0, ds(e, 1)].rearrange("a b c -> (a b) c") for w in (w_exp_gate, w_exp_up, w_exp_down)]

            def expert_steps(e, parity, first, s0):
                def load(s, f0, step_):
                    i = (parity + s) % 2
                    if s >= 2 or s0 == 0:
                        step(1, i, (0, 1), expert(e), f0, step_)
                    if s:
                        step(1, 1 - i, (2,), expert(e), f0 - FT, step_ - 1)
                for s in range(s0, EXPERT_STEPS - 4):
                    load(s, s * FT, first + s)
                with sp.Fori(0, 2) as i:
                    for s in (EXPERT_STEPS - 4, EXPERT_STEPS - 3):
                        load(s, i * (2 * FT) + s * FT, sp.snap(i * 2 + (first + s)))
                last = EXPERT_STEPS - 1
                step(1, (parity + last) % 2, (2,), expert(e), last * FT, first + last)

            first_steps(1, *expert(0), FT)
            expert_steps(0, 0, DENSE_STEPS, 2)
            expert_steps(1, 1, DENSE_STEPS + EXPERT_STEPS, 0)
            with sp.Fori(1, E // 2) as pair:
                for p in range(2):
                    expert_steps(sp.snap(pair * 2 + p), p,
                                 sp.snap(pair * (2 * EXPERT_STEPS) + (DENSE_STEPS + p * EXPERT_STEPS)), 0)
            for t in range(NT):
                sp.wait_ge(x_added, 4 * E + 2 * (t + 1))
                sp.dma_start(out[0, t * P:(t + 1) * P, :], x[:, t, :]).then_inc(s_out, 16)
            sp.wait_ge(s_out, 16 * NT)

        @block.tensor
        def _(pe):
            ident = con[:, C_ID:C_ID + P]
            up = con[:, C_UP:C_UP + 257]
            neglow = con[:, C_NEGLOW:C_NEGLOW + 256]

            def open_fill(l, name):
                n = FILL[name]
                if n >= 2:
                    pe.wait_ge(tr_free[n % 2], l * (NFILL // 2) + n // 2)

            def norm(l, name):
                for i in range(4):
                    t = i // 2
                    if i % 2 == 0:
                        pe.wait_ge(xs_ready, 2 * (2 * l + (name == "y")) + t + 1)
                    open_fill(l, (name, i))
                    for b in range(4):
                        k = 4 * (i % 2) + b
                        mm = pe.transpose(bank((name, i))[:, b * P:(b + 1) * P], xs[:, t, k * P:(k + 1) * P], ident)
                    mm.then_inc(tr_full, 1)

            def project(l, g, u):
                c0, cols, t = UNITS[g][u]
                m = PUNIT[g, u]
                if m < NT:
                    emptied(pe, l, ("x", 2 * m))
                    emptied(pe, l, ("x", 2 * m + 1))
                if m >= 2:
                    pe.wait_ge(pr_free[m % 2], l * (NPF // 2) + m // 2)
                if u == 0:
                    pe.wait_ge(s_win[g], 16 * (l + 1))
                if u == 2 and g == "D":
                    pe.wait_ge(s_wd[1], 16 * (l + 1))
                for k in range(KD):
                    if u == 0 and g == "D" and k == 4:
                        pe.wait_ge(s_wd[0], 16 * (l + 1))
                    mm = pe.matmul(pbank(m)[:, 0:cols], hT[:, k, t * P:(t + 1) * P], win(l, g)[:, k, c0:c0 + cols],
                                   start=(k == 0), stop=(k == KD - 1))
                mm.then_inc(pr_full, 1)

            def qk_transposes(l, gi, g):
                nb = 3 if g == "B" else 4
                for t in range(NT):
                    open_fill(l, (g, "qk", t))
                    pe.wait_ge(pr_free[t], l * (NPF // 2) + PUNIT[g, t] // 2 + 1)
                    for b in range(nb):
                        mm = pe.transpose(bank((g, "qk", t))[:, b * P:(b + 1) * P], stage[:, t, b * P:(b + 1) * P], ident)
                    mm.then_inc(tr_full, 1)

            def q_k(gi, g, h):
                if g == "B":
                    qb, lo = h % 2, HD * (h // 2)
                    kb = 2
                else:
                    qb, kb, lo = h // 2, 2 + h // 2, HD * (h % 2)
                return qkT[lo:lo + HD, gi % 2, qb, :], qkT[lo:lo + HD, gi % 2, kb, :]

            def wait_scores_free(l, use):
                n = SUSE[use]
                if n:
                    pe.wait_ge(sc_free, l * NSU + n)

            def forget_sums(l):
                pe.wait_ge(spb_ready, l + 1)
                if not l:
                    pe.wait_ge(s_con, 16)
                wait_scores_free(l, "Dsum")
                for h in range(H):
                    pe.matmul(ps[:, 2 + h, 0:T], spbs[l][:, h, :], up[:, 1:1 + T], start=True, stop=False)
                    mm = pe.matmul(ps[:, 2 + h, P:T], spbs[l][:, H + h, :], up[:, 1:1 + P], start=False, stop=True)
                mm.then_inc(sc_full, 1)

            def scores(l, gi, g):
                emptied(pe, l, (g, "qk", 0))
                emptied(pe, l, (g, "qk", 1))
                wait_scores_free(l, "Az" if g == "A" else g)
                for h in range(H):
                    q, k = q_k(gi, g, h)
                    if g == "A":
                        pe.matmul(ps[:, 2 + h, 0:T], k[:, 0:P], q[:, 0:T], start=True, stop=True, skip_group_check=True)
                        mm = pe.matmul(ps[:, 2 + h, T:SC], k[:, P:T], q[:, P:T], start=False, stop=True,
                                       skip_group_check=True)
                    else:
                        pe.matmul(ps[:, 2 + h, 0:P], q[:, 0:P], k[:, 0:P], start=True, stop=True)
                        mm = pe.matmul(ps[:, 2 + h, P:SC], q[:, P:T], k[:, 0:T], start=True, stop=True)
                mm.then_inc(sc_full, 1)

            def stick_sums(l):
                pe.wait_ge(a_sp, 2 * (l + 1))
                pe.wait_ge(sc_free, l * NSU + SUSE["Aw"])
                for h in range(H):
                    o, sp_ = ps[:, 2 + h, :], L2s[l][:, h, :]
                    pe.matmul(o[:, 0:T], neglow[:, P:2 * P], sp_[:, 0:T], start=False, stop=True, skip_group_check=True)
                    pe.matmul(o[:, P:T], neglow[:, 0:P], sp_[:, T:SC], start=False, stop=True, skip_group_check=True)
                    mm = pe.matmul(o[:, T:SC], neglow[:, P:2 * P], sp_[:, T:SC], start=False, stop=True,
                                   skip_group_check=True)
                mm.then_inc(sc_full, 1)

            def p_transposes(l, g):
                for h in range(H):
                    open_fill(l, (g, "p", h))
                    pe.wait_ge(p_ready, 4 * (4 * l + ORDER.index(g)) + h + 1)
                    for b in range(3):
                        mm = pe.transpose(bank((g, "p", h))[:, b * P:(b + 1) * P], Lbufs[l][:, h, b * P:(b + 1) * P], ident)
                    mm.then_inc(tr_full, 1)

            def values(l, gi, g):
                if g == "A":
                    pe.wait_ge(p_ready, 4 * (4 * l + gi) + H)
                    w = Lbufs[l]
                else:
                    emptied(pe, l, (g, "p", 2))
                    emptied(pe, l, (g, "p", 3))
                    w = pTs[l]
                last = len(UNITS[g]) - 1
                for u in (last - 1, last):
                    m = PUNIT[g, u]
                    pe.wait_ge(pr_free[m % 2], l * (NPF // 2) + m // 2 + 1)
                open_fill(l, (g, "o"))
                for h in range(H):
                    hv = h // 2 if g == "B" else h
                    v = [vbuf[:, gi % 2, t, hv * HD:(hv + 1) * HD] for t in range(NT)]
                    o = [bank((g, "o"))[:, t * GW + h * HD:t * GW + (h + 1) * HD] for t in range(NT)]
                    pe.matmul(o[0], w[:, h, 0:P], v[0], start=True, stop=True)
                    pe.matmul(o[1], w[:, h, P:2 * P], v[0], start=True, stop=False)
                    mm = pe.matmul(o[1], w[:, h, 2 * P:SC], v[1], start=False, stop=True)
                mm.then_inc(tr_full, 1)

            def o_transposes(l, gi, g):
                open_fill(l, (g, "oT"))
                pe.wait_ge(o_ready, 4 * l + gi + 1)
                for kk in range(2):
                    for t in range(NT):
                        mm = pe.transpose(bank((g, "oT"))[:, kk * T + t * P:kk * T + (t + 1) * P],
                                          obuf[:, t, kk * P:(kk + 1) * P], ident)
                mm.then_inc(tr_full, 1)

            def out_project(l, t, groups):
                if groups[0] == ORDER[0]:
                    if t == 0:
                        for b in range(2):
                            pe.wait_ge(pr_free[(NPU + b) % 2], l * (NPF // 2) + (NPU + b) // 2)
                        for i in range(2):
                            pe.wait_ge(s_wo[i], 16 * (l + 1))
                    else:
                        wait_scores_free(l, "out")
                for g in groups:
                    emptied(pe, l, (g, "oT"))
                    for kk in range(2):
                        k = 2 * CAT[g] + kk
                        for half in range(2):
                            mm = pe.matmul(ps[:, 2 * t + half, :], oT[:, t, k * P:(k + 1) * P],
                                           wo[:, k, half * 512:(half + 1) * 512],
                                           start=(g == ORDER[0] and kk == 0), stop=(g == ORDER[-1] and kk == 1))
                            if g == ORDER[-1] and kk == 1 and t == 0:
                                mm.then_inc(pr_full, 1)
                if groups[-1] == ORDER[-1] and t == 1:
                    mm.then_inc(sc_full, 1)

            def attention(l):
                norm(l, "x")
                for u in range(4):
                    project(l, "D", u)
                project(l, "A", 0)
                forget_sums(l)
                qk_transposes(l, 0, "D")
                scores(l, 0, "D")
                project(l, "A", 1)
                project(l, "A", 2)
                p_transposes(l, "D")
                project(l, "A", 3)
                values(l, 0, "D")
                project(l, "C", 0)
                qk_transposes(l, 1, "A")
                o_transposes(l, 0, "D")
                scores(l, 1, "A")
                project(l, "C", 1)
                project(l, "C", 2)
                stick_sums(l)
                project(l, "C", 3)
                values(l, 1, "A")
                qk_transposes(l, 2, "C")
                scores(l, 2, "C")
                project(l, "B", 0)
                o_transposes(l, 1, "A")
                project(l, "B", 1)
                p_transposes(l, "C")
                values(l, 2, "C")
                out_project(l, 0, ["D", "A"])
                qk_transposes(l, 3, "B")
                o_transposes(l, 2, "C")
                scores(l, 3, "B")
                out_project(l, 0, ["C"])
                out_project(l, 1, ["D", "A"])
                p_transposes(l, "B")
                values(l, 3, "B")
                out_project(l, 1, ["C"])
                o_transposes(l, 3, "B")
                out_project(l, 0, ["B"])
                out_project(l, 1, ["B"])
                norm(l, "y")
                emptied(pe, l, ("y", 2))
                emptied(pe, l, ("y", 3))

            def gate_up(l, i, step, bufs, src, t, cols, count, before_up=None):
                for kind, full in ((0, g_full), (1, u_full)):
                    hi, lo = weight(HIGH[l][kind], kind, cols), weight(SETS[l][i][kind], kind, cols)
                    if kind and before_up:
                        before_up()
                    o = ps[:, 2 * bufs + kind, 0:cols]
                    for k in range(KD):
                        if t == 0 and k % 2 == 0:
                            pe.wait_ge(lo_ready[kind], step * QUARTERS + (k // 2 + 1))
                        xhk, xlk = src[0][:, k, t * P:(t + 1) * P], src[1][:, k, t * P:(t + 1) * P]
                        pe.matmul(o, xhk, hi[:, k, :], start=(k == 0), stop=False)
                        pe.matmul(o, xhk, lo[:, k, :], start=False, stop=False)
                        mm = pe.matmul(o, xlk, hi[:, k, :], start=False, stop=(k == KD - 1))
                    mm.then_inc(full, count)

            def transposes(bufs, cols, done, count):
                pe.wait_ge(h_ready, done)
                for b in range(cols // P):
                    mm = pe.transpose(ps[:, 2 * bufs, b * P:(b + 1) * P], hid[bufs][:, b * P:(b + 1) * P], ident)
                mm.then_inc(t_full, count)

            def down(l, i, step, bufs, t, cols, done, count, first=False):
                hi, lo = weight(HIGH[l][2], 2, cols), weight(SETS[l][i][2], 2, cols)
                pe.wait_ge(hl_ready, done)
                blocks = cols // P
                for b in range(blocks):
                    hhb, hlb = [a[:, bufs, b * P:(b + 1) * P] for a in (hh_r, hl_r)]
                    for half in range(2):
                        part = b * QUARTERS // blocks + (half if blocks < QUARTERS else 0)
                        if t == 0 and (half == 0 or blocks < QUARTERS):
                            pe.wait_ge(lo_ready[2], step * QUARTERS + (part + 1))
                        o, c = ps[:, YB[t] + half, :], slice(half * 512, (half + 1) * 512)
                        pe.matmul(o, hhb, hi[:, b, c], start=(first and b == 0), stop=False, skip_group_check=True)
                        pe.matmul(o, hhb, lo[:, b, c], start=False, stop=False, skip_group_check=True)
                        mm = pe.matmul(o, hlb, hi[:, b, c], start=False, stop=(b == blocks - 1), skip_group_check=True)
                mm.then_inc(d_full, count)

            def all_tokens(l, n, first_step, use, parity):
                src = (xh_r, hT_r)

                def one(s, i, step, use_, _):
                    cols = hidden_cols(s, l == 0)
                    gate_up(l, i, step, 0, src, 0, cols, 1)
                    if s:
                        down(l, 1 - i, step - 1, 1, 1, hidden_cols(s - 1, l == 0), step * 2, 1, first=(s == 1))
                    transposes(0, cols, step * 2 + 1, 1)
                    gate_up(l, i, step, 1, src, 1, cols, 1)
                    down(l, i, step, 0, 0, cols, step * 2 + 1, 1, first=(s == 0))
                    transposes(1, cols, step * 2 + 2, 1)
                steps(pe, one, n, first_step, use, parity)
                down(l, (parity + n - 1) % 2, first_step + (n - 1), 1, 1, FT, first_step * 2 + 2 * n, 1)

            pe.wait_ge(s_id, 16)
            pe.wait_ge(s_gain, 16 * 7)
            pe.transpose(ps[:, 0, 0:G_ALL], grow[:, :], con[0:G_ALL, C_ID:C_ID + G_ALL]).then_inc(gains_T, 1)

            attention(0)
            all_tokens(0, DENSE_STEPS, 0, 0, 0)

            attention(1)
            pe.wait_ge(s_wr, 16)
            for t in range(NT):
                for k in range(KD):
                    mm = pe.matmul(ps[:, 0, t * E:(t + 1) * E], hT[:, k, t * P:(t + 1) * P], wr[:, k, :],
                                   start=(k == 0), stop=(k == KD - 1))
            mm.then_inc(r_pe, 1)
            pe.wait_ge(r_dve, R_MASK)
            pe.matmul(ps[:, 1, 0:E], up[:, 0:P], mask[:, 0, :], start=True, stop=True)
            pe.matmul(ps[:, 1, E:2 * E], up[:, P + 1:2 * P + 1], mask[:, 0, :], start=True, stop=False)
            pe.matmul(ps[:, 1, E:2 * E], up[:, 0:P], mask[:, 1, :], start=False, stop=True)
            pe.matmul(ps[:, 1, 2 * E:3 * E], up[:, P + 1:2 * P + 1], mask[:, 0, :], start=True, stop=False)
            pe.matmul(ps[:, 1, 2 * E:3 * E], up[:, P + 1:2 * P + 1], mask[:, 1, :], start=False, stop=True).then_inc(r_pe, 1)
            pe.wait_ge(r_dve, R_ALL)
            def gather(e, p):
                pe.wait_ge(sel_ready, e + 1)
                for half in range(2):
                    for b in range(4):
                        for t in range(NT):
                            mm = pe.matmul(ps[:, 4 + half, b * P:(b + 1) * P], xs[:, t, (4 * half + b) * P:(4 * half + b + 1) * P],
                                           sel[:, t, :], start=(t == 0), stop=(t == NT - 1))
                    mm.then_inc(gx_full, 1)
                for t in range(NT):
                    mm = pe.transpose(ps[:, 2 * p + 1, t * P:(t + 1) * P], selg[:, t, :], ident)
                mm.then_inc(gx_full, 1)

            def gathered(e, p, first_step, use):
                def back_read():
                    pe.wait_ge(gx_back, e + 1)

                src = (xeh_r, xel_r)
                pe.wait_ge(gx_dve, e * KD + KD)

                def one(s, i, step, use_, _):
                    if s == 1:
                        pe.wait_ge(x_added, e * 4 + 4)
                    between_ = {0: back_read, 1: lambda: transposes(1 - i, FT, step * 2, 2)}.get(s)
                    gate_up(1, i, step, i, src, 0, FT, 2, between_)
                    if s:
                        down(1, 1 - i, step - 1, 1 - i, 0, FT, step * 2, 2, first=(s == 1))
                        transposes(i, FT, step * 2 + 2, 2)
                steps(pe, one, EXPERT_STEPS, first_step, use, p)
                gather(e + 1, 1 - p)
                down(1, p, first_step + (EXPERT_STEPS - 1), p, 0, FT, first_step * 2 + 2 * EXPERT_STEPS, 2)
                pe.wait_ge(ye_dve, e + 1)
                pe.wait_ge(ye_act, e + 1)
                pe.wait_ge(gx_dve, e * KD + 2 * KD)
                for t in range(NT):
                    for half in range(2):
                        pe.matmul(ps[:, (4, 2 * p)[t] + half, :], back[p][:, t * P:(t + 1) * P],
                                  ye[:, half * 512:(half + 1) * 512], start=True, stop=True).then_inc(e_full, 1)

            def expert(pair, p, e, first_step, use):
                n_e = pe.value_load(cnt[0:1, ds(e, 1)], min_val=0, max_val=T)

                def run(n):
                    if n < T:
                        gathered(e, p, first_step, use)
                        return
                    pe.wait_ge(x_added, e * 4 + 4)
                    pe.wait_ge(gx_back, e + 1)
                    pe.wait_ge(all_low, e + 1)
                    all_tokens(1, EXPERT_STEPS, first_step, use, p)
                    pe.sem_inc(e_full, 4)
                    pe.wait_ge(x_added, e * 4 + 8)
                    gather(e + 1, 1 - p)
                by_count(pe, n_e, run)
            gather(0, 0)
            pairs(pe, expert)

        @block.scalar
        def _(act):
            def norm(l, name):
                y = name == "y"
                for t in range(NT):
                    if y and t == 0:
                        act.wait_ge(pr_free[0], (l + 1) * (NPF // 2))
                        act.wait_ge(pr_free[1], (l + 1) * (NPF // 2))
                    elif y:
                        act.wait_ge(sc_free, (l + 1) * NSU)
                    elif l:
                        act.wait_ge(x_added, 2 * (t + 1))
                    else:
                        act.wait_ge(s_x[t], 16)
                    act.activation(squares[y][t], x[:, t, :], ACT.Square, accum_out=ssx[:, t:t + 1]).then_inc(ssx_ready, 1)
                act.wait_ge(gains, 1)
                parts = y and l == 0
                for i in range(4) if parts else (1, 3):
                    t = i // 2
                    filled(act, l, (name, i))
                    for b in range(4):
                        k = 4 * (i % 2) + b
                        c = (G_FFN if y else G_MIX) + l * KD + k
                        ins = act.activation((xh_r if parts else hT)[:, k, t * P:(t + 1) * P],
                                             bank((name, i))[:, b * P:(b + 1) * P], ACT.Copy, scale=gT[:, c:c + 1])
                    ins.then_inc(xh_ready if parts else tr_free[1], 1)

            def read_unit(l, gi, g, u):
                m = PUNIT[g, u]
                act.wait_ge(pr_full, l * NPF + m + 1)
                if u >= 2:
                    if gi >= 2:
                        filled(act, l, (ORDER[gi - 2], "o"))
                    if g == "D":
                        act.activation(fraw[:, u - 2, :], pbank(m)[:, GW:GW + H], ACT.Copy)
                    act.activation(vbuf[:, gi % 2, u - 2, :], pbank(m)[:, 0:GW], ACT.Copy).then_inc(pr_free[m % 2], 1)
                elif g != "A":
                    cols = 384 if g == "B" else 512
                    n = NORMED[g, u] + l * len(NORMED)
                    if n:
                        act.wait_ge(ssq_ready, n)
                    act.activation(sq[:, 0:cols], pbank(m)[:, 0:cols], ACT.Square).then_inc(sq_ready, 1)

            def forget(l):
                act.wait_ge(f_dve, 3 * l + 1)
                act.activation(fa[:], fu[:], ACT.Abs).then_inc(f_act, 1)
                act.wait_ge(f_act, 3 * l + 1)
                act.activation(fe[:], fa[:], ACT.Exp, scale=-1.0).then_inc(f_act, 1)
                act.wait_ge(f_act, 3 * l + 2)
                act.activation(fl[:], fe[:], ACT.Ln, bias=1.0).then_inc(f_act, 1)

            def read_qk(l, gi, g):
                scale_qk(act, l, gi, g, 1)

            def softmax(l, gi, g):
                act.wait_ge(m_ready, 3 * l + SOFT.index(g) + 1)
                for h in range(H):
                    for t in range(NT):
                        c0, c1 = (0, P) if t == 0 else (P, SC)
                        n = t * H + h
                        ins = act.activation(Lbufs[l][:, h, c0:c1], Lbufs[l][:, h, c0:c1], ACT.Exp, bias=nm[:, n:n + 1],
                                             accum_out=rsum[:, n:n + 1])
                    ins.then_inc(p_ready, 1)
                if g == "B":
                    act.wait_ge(mx_part, 2 * (l + 1))
                    act.activation(esink[:], esink[:], ACT.Exp).then_inc(es_ready, 1)

            def stick_softplus(l):
                act.wait_ge(a_relu, l + 1)
                act.activation(Lbufs[l][:], ps[:, 2:2 + H, 0:SC], ACT.Abs).then_inc(sc_free, 1)
                act.wait_ge(sc_free, l * NSU + SUSE["Az"] + 1)
                act.activation(Lbufs[l][:], Lbufs[l][:], ACT.Exp, scale=-1.0).then_inc(a_abs, 1)
                act.wait_ge(a_abs, 2 * l + 1)
                act.activation(Lbufs[l][:], Lbufs[l][:], ACT.Ln, bias=1.0).then_inc(a_abs, 1)

            def stick_exp(l, gi):
                act.wait_ge(sc_free, l * NSU + SUSE["Aw"] + 1)
                act.activation(Lbufs[l][:], Lbufs[l][:], ACT.Exp).then_inc(p_ready, H)

            def read_p(l, g):
                for h in (1, 3):
                    filled(act, l, (g, "p", h))
                    act.activation(pTs[l][:, h, :], bank((g, "p", h))[:, 0:SC], ACT.Copy).then_inc(tr_free[FILL[g, "p", h] % 2], 1)

            def read_oT(l, g):
                filled(act, l, (g, "oT"))
                for kk in range(2):
                    k = 2 * CAT[g] + kk
                    c = G_OUT + l * 8 + k
                    ins = act.activation(oT[:, :, k * P:(k + 1) * P],
                                         bank((g, "oT"))[:, kk * T:(kk + 1) * T].rearrange("p (a c) -> p a c", a=NT),
                                         ACT.Copy, scale=gT[:, c:c + 1])
                ins.then_inc(tr_free[FILL[g, "oT"] % 2], 1)

            def attention(l):
                norm(l, "x")
                for u in range(4):
                    read_unit(l, 0, "D", u)
                forget(l)
                read_unit(l, 1, "A", 0)
                read_qk(l, 0, "D")
                softmax(l, 0, "D")
                read_unit(l, 1, "A", 1)
                read_unit(l, 1, "A", 2)
                read_p(l, "D")
                read_unit(l, 1, "A", 3)
                read_unit(l, 2, "C", 0)
                read_qk(l, 1, "A")
                read_oT(l, "D")
                stick_softplus(l)
                read_unit(l, 2, "C", 1)
                read_unit(l, 2, "C", 2)
                stick_exp(l, 1)
                read_unit(l, 2, "C", 3)
                read_qk(l, 2, "C")
                softmax(l, 2, "C")
                read_unit(l, 3, "B", 0)
                read_oT(l, "A")
                read_unit(l, 3, "B", 1)
                read_p(l, "C")
                first_high(l)
                read_qk(l, 3, "B")
                read_oT(l, "C")
                softmax(l, 3, "B")
                read_p(l, "B")
                read_oT(l, "B")
                norm(l, "y")

            def high(l, i, kind, step, use, cols=FT, first=False):
                act.wait_ge(s_raw[i][kind], (use + 1) * 16)
                if not first:
                    act.wait_ge((g_full, u_full, d_full)[kind], step * 2)
                for q in range(QUARTERS):
                    act.activation(quarter_r(HIGH[l][kind], q, cols), quarter(SETS[l][i][kind], q, cols),
                                   ACT.Copy).then_inc(hi_ready[kind], 1)

            def first_high(l):
                act.wait_ge(pr_full, l * NPF + PUNIT["B", 1] + 1)
                act.wait_ge(s_tabm, l + 1)
                for kind in range(2 - l):
                    high(l, 0, kind, l * DENSE_STEPS, l * (DENSE_STEPS // 2), hidden_cols(0, l == 0), first=True)

            def silu(bufs, done, count, cols):
                act.wait_ge(g_full, done)
                act.activation(hid[bufs][:, 0:cols], ps[:, 2 * bufs, 0:cols], ACT.Silu).then_inc(silu_ready, count)

            def hidden_high(bufs, done, count, cols):
                act.wait_ge(t_full, done)
                act.activation(hh_r[:, bufs, 0:cols], ps[:, 2 * bufs, 0:cols], ACT.Copy).then_inc(hh_ready, count)

            def all_tokens(l, n, first_step, use, parity):
                def one(s, i, step, use_, loop):
                    cols = hidden_cols(s, l == 0)
                    silu(0, step * 2 + 1, 1, cols)
                    high(l, i, 2, step, use_, cols, first=(s == 0 and l == 0))
                    hidden_high(0, step * 2 + 1, 1, cols)
                    unless_last(act, s, n, loop, lambda: high(l, 1 - i, 0, step + 1, use_ + i))
                    silu(1, step * 2 + 2, 1, cols)
                    unless_last(act, s, n, loop, lambda: high(l, 1 - i, 1, step + 1, use_ + i))
                    hidden_high(1, step * 2 + 2, 1, cols)
                steps(act, one, n, first_step, use, parity)

            attention(0)
            all_tokens(0, DENSE_STEPS, 0, 0, 0)

            attention(1)
            act.wait_ge(r_dve, R_DIFF)
            act.activation(em[:], dm[:], ACT.Exp).then_inc(r_act, 1)
            act.wait_ge(r_dve, R_ALL)

            def expert(pair, p, e, first_step, use):
                n_e = act.value_load(cnt[0:1, ds(e, 1)], min_val=0, max_val=T)

                def up_high():
                    high(1, p, 1, first_step, use)

                def next_gate_high():
                    next_expert(act, pair, p, lambda: high(1, 1 - p, 0, first_step + EXPERT_STEPS, use + (EXPERT_STEPS + p) // 2))

                def run(n):
                    if n == T:
                        act.wait_ge(gx_dve, e * KD + KD)
                        act.wait_ge(u_full, first_step * 2)
                        act.activation(xh_r, hT[:], ACT.Copy).then_inc(all_high, 1)
                        up_high()
                        all_tokens(1, EXPERT_STEPS, first_step, use, p)
                        act.wait_ge(whole, e + 1)
                        gather_high(e + 1)
                        next_gate_high()
                        act.sem_inc(ye_act, 1)
                        return
                    up_high()

                    def one(s, i, step, use_, loop):
                        silu(i, step * 2 + 2, 2, FT)

                        def next_high():
                            for kind in range(2):
                                high(1, 1 - i, kind, step + 1, use_ + i)
                        unless_last(act, s, EXPERT_STEPS, loop, next_high)
                        hidden_high(i, step * 2 + 2, 2, FT)
                        high(1, i, 2, step, use_)
                    steps(act, one, EXPERT_STEPS, first_step, use, p)
                    gather_high(e + 1)
                    act.wait_ge(d_full, first_step * 2 + 2 * EXPERT_STEPS)
                    act.activation(ye[:, 512:1024], ps[:, 7, :], ACT.Copy).then_inc(ye_act, 1)
                    next_gate_high()
                    act.sem_inc(all_high, 1)
                by_count(act, n_e, run)
            def gather_high(e):
                for k in range(KD):
                    if k % 4 == 0:
                        act.wait_ge(gx_full, e * 3 + (k // 4 + 1))
                    c = G_FFN + KD + k
                    act.activation(xeh_r[:, k, :], ps[:, 4 + k // 4, (k % 4) * P:(k % 4 + 1) * P], ACT.Copy,
                                   scale=gT[:, c:c + 1]).then_inc(gx_act, 1)

            gather_high(0)
            pairs(act, expert)

        @block.gpsimd
        def _(pool):
            pool.memset(mhalf[:], -0.5).then_inc(rx_part, 1)
            done = [1]

            def rstd(mean, total, scale, out_, part, ready, value):
                pool.tensor_scalar(mean, total, scale, EPS, ALU.mult, ALU.add).then_inc(part, 1)
                pool.wait_ge(part, value)
                n = mean.shape[-1]
                pool.tensor_tensor(out_, mean, mhalf[:, 0:n], ALU.pow).then_inc(ready, 1)

            def norm(l, name):
                n = 2 * l + (name == "y")
                for t in range(NT):
                    pool.wait_ge(ssx_ready, NT * n + t + 1)
                    if not n:
                        pool.wait_ge(rx_part, 1)
                    rstd(rx0[:, t:t + 1], ssx[:, t:t + 1], 1.0 / D, rx[:, t:t + 1], rx_part, rx_ready, NT * n + t + 2)

            def unit_rstd(l, g, u):
                n = NORMED[g, u] + l * len(NORMED)
                k = 6 if g == "B" else 8
                pool.wait_ge(ssq_ready, n + 1)
                rstd(rq0[:, u, 0:k], ssq[:, u, 0:k], 1.0 / HD, rq[:, u, 0:k], rq_part, rq_ready, n + 1)

            def group_rstd(l, gi):
                n = 4 * l + gi
                pool.wait_ge(sso_ready, NT * (n + 1))
                rstd(ro0[:], sso[:], 1.0 / GW, ro[:], ro_part, ro_ready, n + 1)

            for l in range(L):
                norm(l, "x")
                for gi, g in enumerate(ORDER + [None]):
                    if g is not None and g != "A":
                        unit_rstd(l, g, 0)
                    if g is not None and g != "A":
                        unit_rstd(l, g, 1)
                    if gi:
                        group_rstd(l, gi - 1)
                    if gi == 1:
                        pool.wait_ge(s_tabc, 16 * (l + 1))
                        pool.wait_ge(s_con, 16)
                        pool.wait_ge(pr_full, l * NPF + PUNIT["D", 3] + 1)
                        for h in range(H):
                            for c0, c1 in ((0, P), (P, SC)):
                                keys = c1 - c0
                                backward = bass.AP(tensor=hankels[l].tensor, offset=hankels[l].offset + h * T + keys - 1,
                                                   ap=[list(hankels[l].ap[0]), [-1, keys]])
                                ins = pool.tensor_tensor(tabCs[l][:, h, c0:c1], backward,
                                                         con[:, C_BLOCK + c0:C_BLOCK + c1], ALU.add)
                        ins.then_inc(s_tabm, 1)
                norm(l, "y")

        @block.vector
        def _(dve):
            def norm_scale(l, name, t):
                dve.wait_ge(rx_ready, NT * (2 * l + (name == "y")) + t + 1)
                dve.tensor_scalar(xs[:, t, :], x[:, t, :], rx[:, t:t + 1], None, ALU.mult).then_inc(xs_ready, 1)

            def norm_read(l, name):
                c0 = (G_FFN if name == "y" else G_MIX) + l * KD
                if name == "y" and l == 0:
                    for i in range(4):
                        t = i // 2
                        dve.wait_ge(xh_ready, i + 1)
                        for b in range(4):
                            k = 4 * (i % 2) + b
                            ins = dve.scalar_tensor_tensor(
                                out=hT_r[:, k, t * P:(t + 1) * P], in0=bank((name, i))[:, b * P:(b + 1) * P],
                                scalar=gT[:, c0 + k:c0 + k + 1], in1=xh_r[:, k, t * P:(t + 1) * P],
                                op0=ALU.mult, op1=ALU.subtract)
                        ins.then_inc(tr_free[i % 2], 1)
                    return
                for i in (0, 2):
                    t = i // 2
                    filled(dve, l, (name, i))
                    dve.tensor_tensor(hT[:, 0:4, t * P:(t + 1) * P], bank((name, i)).rearrange("p (b c) -> p b c", c=P),
                                      spread(gT[:, c0:c0 + 4], 4, P), ALU.mult).then_inc(tr_free[0], 1)

            def spread(ap, n, width):
                return ap.unsqueeze(2).broadcast_to([P, n, width])

            def read_unit(l, gi, g, u):
                if u >= 2:
                    return
                m = PUNIT[g, u]
                dve.wait_ge(pr_full, l * NPF + m + 1)
                if g == "A":
                    filled(dve, l, (ORDER[gi - 1], "qk", u))
                    dve.tensor_copy(stage[:, u, :], pbank(m)[:, :]).then_inc(pr_free[m % 2], 1)
                    return
                n = NORMED[g, u] + l * len(NORMED)
                k = 6 if g == "B" else 8
                dve.wait_ge(sq_ready, n + 1)
                dve.tensor_reduce(ssq[:, u, 0:k], sq[:, 0:k * HD].rearrange("p (h c) -> p h c", c=HD), AX.X, ALU.add) \
                    .then_inc(ssq_ready, 1)
                if gi:
                    filled(dve, l, (ORDER[gi - 1], "qk", u))
                dve.wait_ge(rq_ready, n + 1)
                if g == "B":
                    for half in range(2):
                        src = pbank(m)[:, half * P:(half + 1) * P].rearrange("p (b c) -> p b c", c=HD)
                        dst = stage[:, u, 0:2 * P].rearrange("p (b a c) -> p b a c", b=2, a=2)[:, :, half, :]
                        dve.tensor_tensor(dst, src, spread(rq[:, u, 2 * half:2 * half + 2], 2, HD), ALU.mult)
                    dve.tensor_tensor(stage[:, u, 2 * P:3 * P].rearrange("p (h c) -> p h c", c=HD),
                                      pbank(m)[:, 2 * P:3 * P].rearrange("p (h c) -> p h c", c=HD),
                                      spread(rq[:, u, 4:6], 2, HD), ALU.mult)
                    filled(dve, l, (ORDER[gi - 2], "o"))
                    dve.tensor_copy(vbuf[:, gi % 2, u, 0:P], pbank(m)[:, 3 * P:4 * P]).then_inc(pr_free[m % 2], 1)
                else:
                    dve.tensor_tensor(stage[:, u, :].rearrange("p (h c) -> p h c", c=HD),
                                      pbank(m)[:, :].rearrange("p (h c) -> p h c", c=HD),
                                      spread(rq[:, u, :], 8, HD), ALU.mult).then_inc(pr_free[m % 2], 1)

            def forget(l):
                if not l:
                    dve.wait_ge(s_small, 16 * 3)
                    dve.tensor_scalar(nsink[:], sink[:], -1.0, None, ALU.mult).then_inc(gains, 1)
                    dve.wait_ge(gains, 3)
                for m in (2, 3):
                    dve.wait_ge(pr_free[m % 2], l * (NPF // 2) + 2)
                dve.tensor_tensor(fu[:], fraw[:], bfr[:, l:l + 1, :].broadcast_to([P, NT, H]), ALU.add).then_inc(f_dve, 1)
                dve.wait_ge(f_dve, 3 * l + 1)
                dve.tensor_scalar(fr[:], fu[:], -1.0, 0.0, ALU.mult, ALU.max).then_inc(f_dve, 1)
                dve.wait_ge(f_dve, 3 * l + 2)
                dve.wait_ge(f_act, 3 * l + 3)
                dve.tensor_tensor(fsp[:], fr[:], fl[:], ALU.add).then_inc(f_dve, 1)
                dve.wait_ge(f_dve, 3 * l + 3)
                dve.tensor_copy(spbs[l], spread(fsp[:].rearrange("p a b -> p (a b)"), NT * H, P)).then_inc(spb_ready, 1)

            def table_d(l):
                dve.wait_ge(s_con, 16)
                dve.wait_ge(sc_full, l * NSU + SUSE["Dsum"] + 1)
                for c0, c1 in ((0, P), (P, SC)):
                    ins = dve.tensor_tensor(L2s[l][:, :, c0:c1], ps[:, 2:2 + H, 0:c1 - c0],
                                            con[:, C_CAUSAL + c0:C_CAUSAL + c1].unsqueeze(1).broadcast_to([P, H, c1 - c0]),
                                            ALU.add)
                ins.then_inc(sc_free, 1)
                dve.wait_ge(sc_free, l * NSU + SUSE["Dsum"] + 1)

            def softmax(l, gi, g):
                dve.wait_ge(sc_full, l * NSU + SUSE[g] + 1)
                if g == "C":
                    dve.wait_ge(s_tabm, l + 1)
                if g == "B":
                    table = con[:, C_ALIBI:C_ALIBI + H * SC].rearrange("p (h c) -> p h c", h=H)
                else:
                    table = {"D": L2s[l], "C": tabCs[l]}[g]
                if gi:
                    filled(dve, l, (ORDER[gi - 1], "o"))
                dve.tensor_tensor(Lbufs[l], ps[:, 2:2 + H, 0:SC], table, ALU.add).then_inc(sc_free, 1)
                dve.wait_ge(sc_free, l * NSU + SUSE[g] + 1)
                dve.tensor_reduce(nm[:, 0:H], Lbufs[l][:, :, 0:P], AX.X, ALU.max, negate=True)
                ins = dve.tensor_reduce(nm[:, H:2 * H], Lbufs[l][:, :, P:SC], AX.X, ALU.max, negate=True)
                if g == "B":
                    ins.then_inc(mx_part, 1)
                    dve.wait_ge(mx_part, 2 * l + 1)
                    ns = nsink[:, l, :, :].rearrange("p a b -> p (a b)")
                    dve.tensor_tensor(nm[:], nm[:], ns, ALU.min).then_inc(m_ready, 1)
                    dve.wait_ge(m_ready, 3 * l + 3)
                    dve.tensor_tensor(esink[:], nm[:], sink[:, l, :, :].rearrange("p a b -> p (a b)"), ALU.add) \
                        .then_inc(mx_part, 1)
                else:
                    ins.then_inc(m_ready, 1)

            def stick_relu(l):
                dve.wait_ge(sc_full, l * NSU + SUSE["Az"] + 1)
                dve.tensor_scalar(L2s[l], ps[:, 2:2 + H, 0:SC], 0.0, None, ALU.max).then_inc(a_relu, 1)

            def read_p(l, g):
                for h in (0, 2):
                    filled(dve, l, (g, "p", h))
                    dve.tensor_copy(pTs[l][:, h, :], bank((g, "p", h))[:, 0:SC]).then_inc(tr_free[FILL[g, "p", h] % 2], 1)

            def inverse(l, g):
                n = 3 * l + SOFT.index(g)
                dve.wait_ge(p_ready, 4 * (4 * l + ORDER.index(g)) + H)
                if g == "B":
                    dve.wait_ge(es_ready, l + 1)
                    dve.tensor_tensor(rsum[:], rsum[:], esink[:], ALU.add).then_inc(rs_part, 1)
                    dve.wait_ge(rs_part, l + 1)
                dve.reciprocal(rinv[:], rsum[:]).then_inc(ri_ready, 1)
                dve.wait_ge(ri_ready, n + 1)

            def group_out(l, gi, g, meanwhile=None):
                filled(dve, l, (g, "o"))
                if gi:
                    filled(dve, l, (ORDER[gi - 1], "oT"))
                o = obuf[:].rearrange("p a (h c) -> p (a h) c", c=HD)
                b = FILL[g, "o"] % 2
                src = bank((g, "o"))[:, :].rearrange("p (n c) -> p n c", c=HD)
                if g == "A":
                    dve.tensor_copy(o, src).then_inc(tr_free[b], 1)
                else:
                    dve.tensor_tensor(o, src, spread(rinv[:], 8, HD), ALU.mult).then_inc(tr_free[b], 1)
                emptied(dve, l, (g, "o"))
                for t in range(NT):
                    dve.tensor_tensor_reduce(out=osq[:, t, :], in0=obuf[:, t, :], in1=obuf[:, t, :], scale=1.0, scalar=0.0,
                                             op0=ALU.mult, op1=ALU.add, accum_out=sso[:, t:t + 1]).then_inc(sso_ready, 1)
                if meanwhile:
                    meanwhile()
                dve.wait_ge(ro_ready, 4 * l + gi + 1)
                for t in range(NT):
                    ins = dve.tensor_scalar(obuf[:, t, :], obuf[:, t, :], ro[:, t:t + 1], None, ALU.mult)
                ins.then_inc(o_ready, 1)

            def add_out(l, t):
                if t:
                    dve.wait_ge(sc_full, (l + 1) * NSU)
                for half in range(2):
                    if not t:
                        dve.wait_ge(pr_full, l * NPF + NPU + half + 1)
                    xt = x[:, t, half * 512:(half + 1) * 512]
                    ins = dve.tensor_tensor(xt, ps[:, 2 * t + half, :], xt, ALU.add)
                    if not t:
                        ins.then_inc(pr_free[half], 1)
                if t:
                    ins.then_inc(sc_free, 1)

            def attention(l):
                norm_read(l, "x")
                read_unit(l, 0, "D", 0)
                read_unit(l, 0, "D", 1)
                forget(l)
                table_d(l)
                scale_qk(dve, l, 0, "D", 0)
                softmax(l, 0, "D")
                read_unit(l, 1, "A", 0)
                read_unit(l, 1, "A", 1)
                read_p(l, "D")
                inverse(l, "D")
                group_out(l, 0, "D")
                scale_qk(dve, l, 1, "A", 0)
                stick_relu(l)
                read_unit(l, 2, "C", 0)
                stick_softplus(l)
                read_unit(l, 2, "C", 1)
                stick_logits(l, 1)
                group_out(l, 1, "A", meanwhile=lambda: scale_qk(dve, l, 2, "C", 0))
                softmax(l, 2, "C")
                read_unit(l, 3, "B", 0)
                read_p(l, "C")
                inverse(l, "C")
                read_unit(l, 3, "B", 1)
                group_out(l, 2, "C")
                scale_qk(dve, l, 3, "B", 0)
                softmax(l, 3, "B")
                for kind in range(2 - l):
                    low(l, 0, kind, l * DENSE_STEPS, hidden_cols(0, l == 0))
                read_p(l, "B")
                inverse(l, "B")
                group_out(l, 3, "B")
                for t in range(NT):
                    add_out(l, t)
                    norm_scale(l, "y", t)
                norm_read(l, "y")

            def stick_softplus(l):
                m = con[:, C_AMASK:C_AMASK + SC].unsqueeze(1).broadcast_to([P, H, SC])
                dve.wait_ge(a_abs, 2 * (l + 1))
                dve.tensor_tensor(L2s[l], L2s[l], Lbufs[l], ALU.add).then_inc(a_sp, 1)
                dve.wait_ge(a_sp, 2 * l + 1)
                dve.tensor_tensor(L2s[l], L2s[l], m, ALU.mult).then_inc(a_sp, 1)

            def stick_logits(l, gi):
                m = con[:, C_ANEG:C_ANEG + SC].unsqueeze(1).broadcast_to([P, H, SC])
                dve.wait_ge(sc_full, l * NSU + SUSE["Aw"] + 1)
                dve.tensor_tensor(Lbufs[l], ps[:, 2:2 + H, 0:SC], m, ALU.add).then_inc(sc_free, 1)
                dve.wait_ge(sc_free, l * NSU + SUSE["Aw"] + 1)

            def low(l, i, kind, step, cols=FT):
                for q in range(QUARTERS):
                    dve.wait_ge(hi_ready[kind], step * QUARTERS + (q + 1))
                    u = SETS[l][i][kind]
                    dve.tensor_tensor(quarter_r(u, q, cols), quarter(u, q, cols),
                                      quarter_r(HIGH[l][kind], q, cols), ALU.subtract).then_inc(lo_ready[kind], 1)

            def hidden(bufs, done, count, cols):
                dve.wait_ge(silu_ready, done)
                dve.wait_ge(u_full, done)
                dve.tensor_tensor(hid[bufs][:, 0:cols], ps[:, 2 * bufs + 1, 0:cols], hid[bufs][:, 0:cols], ALU.mult) \
                    .then_inc(h_ready, count)

            def hidden_low(bufs, done, count, cols):
                dve.wait_ge(hh_ready, done)
                dve.tensor_tensor(hl_r[:, bufs, 0:cols], ps[:, 2 * bufs, 0:cols], hh_r[:, bufs, 0:cols],
                                  ALU.subtract).then_inc(hl_ready, count)

            def all_tokens(l, n, first_step, use, parity):
                def one(s, i, step, use_, loop):
                    cols = hidden_cols(s, l == 0)
                    hidden(0, step * 2 + 1, 1, cols)
                    low(l, i, 2, step, cols)
                    hidden_low(0, step * 2 + 1, 1, cols)
                    unless_last(dve, s, n, loop, lambda: low(l, 1 - i, 0, step + 1))
                    hidden(1, step * 2 + 2, 1, cols)
                    unless_last(dve, s, n, loop, lambda: low(l, 1 - i, 1, step + 1))
                    hidden_low(1, step * 2 + 2, 1, cols)
                steps(dve, one, n, first_step, use, parity)

            def router():
                rev = con[:, C_REV:C_REV + E].unsqueeze(1).broadcast_to([P, NT, E])
                count = [0]

                def done(ins):
                    count[0] += 1
                    ins.then_inc(r_dve, 1)
                    dve.wait_ge(r_dve, count[0])

                def first_largest(values, top, onehot):
                    done(dve.tensor_reduce(top[:], values[:], AX.X, ALU.max))
                    done(dve.tensor_tensor(tmp[:], values[:], spread(top[:], NT, E), ALU.is_equal))
                    done(dve.tensor_tensor(tmp[:], tmp[:], rev, ALU.mult))
                    done(dve.tensor_reduce(r1[:], tmp[:], AX.X, ALU.max))
                    done(dve.tensor_tensor(onehot[:], rev, spread(r1[:], NT, E), ALU.is_equal))

                dve.wait_ge(r_pe, 1)
                done(dve.tensor_copy(lg[:], ps[:, 0, 0:NT * E].rearrange("p (a e) -> p a e", e=E)))
                first_largest(lg, m1, one1)
                done(dve.tensor_scalar(tmp[:], one1[:], NEG, None, ALU.mult))
                done(dve.tensor_tensor(lg2[:], lg[:], tmp[:], ALU.add))
                first_largest(lg2, m2, one2)
                done(dve.tensor_tensor(dm[:], m2[:], m1[:], ALU.subtract))
                assert count[0] == R_DIFF
                done(dve.tensor_tensor(mask[:], one1[:], one2[:], ALU.add))
                assert count[0] == R_MASK
                dve.wait_ge(r_act, 1)
                done(dve.tensor_scalar(em1[:], em[:], 1.0, None, ALU.add))
                done(dve.reciprocal(p1[:], em1[:]))
                done(dve.tensor_tensor(p2[:], em[:], p1[:], ALU.mult))
                done(dve.tensor_tensor(gates[:, :, 0:E], one1[:], spread(p1[:], NT, E), ALU.mult))
                done(dve.tensor_tensor(tmp[:], one2[:], spread(p2[:], NT, E), ALU.mult))
                done(dve.tensor_tensor(gates[:, :, 0:E], gates[:, :, 0:E], tmp[:], ALU.add))
                dve.wait_ge(r_pe, 2)
                done(dve.scalar_tensor_tensor(out=slot[:, :, 0:E], in0=ps[:, 1, 0:NT * E].rearrange("p (a e) -> p a e", e=E),
                                              scalar=1.0, in1=mask[:], op0=ALU.add, op1=ALU.mult))
                done(dve.tensor_scalar(slot[:, :, 0:E], slot[:, :, 0:E], -1.0, None, ALU.add))
                done(dve.memset(slot[:, :, E:E + 1], -1.0))
                done(dve.memset(gates[:, :, E:E + 1], 0.0))
                done(dve.tensor_copy(cnt[:], ps[:, 1, NT * E:(NT + 1) * E]))
                assert count[0] == R_ALL

            dve.wait_ge(gains_T, 1)
            dve.tensor_copy(gT[:], ps[:, 0, 0:G_ALL]).then_inc(gains, 1)
            dve.wait_ge(gains, 1)
            dve.tensor_scalar(gT[:, G_Q:G_K], gT[:, G_Q:G_K], SCALE, None, ALU.mult).then_inc(gains, 1)
            dve.wait_ge(gains, 2)
            for t in range(NT):
                norm_scale(0, "x", t)

            attention(0)
            all_tokens(0, DENSE_STEPS, 0, 0, 0)
            for t in range(NT):
                dve.wait_ge(d_full, 2 * DENSE_STEPS - 1 + t)
                for half in range(2):
                    xt = x[:, t, half * 512:(half + 1) * 512]
                    dve.tensor_tensor(xt, ps[:, YB[t] + half, :], xt, ALU.add).then_inc(x_added, 1)
                norm_scale(1, "x", t)

            attention(1)
            router()

            def select(e):
                iota = con[:, C_IOTA:C_IOTA + P]
                for t in range(NT):
                    at, gate = slot[:, t, ds(e, 1)], gates[:, t, ds(e, 1)]
                    dve.tensor_scalar(sel[:, t, :], iota, at, None, ALU.is_equal)
                    ins = dve.tensor_scalar(selg[:, t, :], iota, at, gate, ALU.is_equal, ALU.mult)
                ins.then_inc(sel_ready, 1)

            def gather_low(e, p):
                for k in range(KD):
                    c = G_FFN + KD + k
                    if k % 4 == 0:
                        dve.wait_ge(gx_act, e * KD + (k + 4))
                    dve.scalar_tensor_tensor(out=xel_r[:, k, :], in0=ps[:, 4 + k // 4, (k % 4) * P:(k % 4 + 1) * P],
                                             scalar=gT[:, c:c + 1], in1=xeh_r[:, k, :], op0=ALU.mult, op1=ALU.subtract) \
                        .then_inc(gx_dve, 1)
                dve.wait_ge(gx_full, e * 3 + 3)
                dve.tensor_copy(back[p], ps[:, 2 * p + 1, 0:T]).then_inc(gx_back, 1)

            select(0)
            gather_low(0, 0)

            def expert(pair, p, e, first_step, use):
                n_e = dve.value_load(cnt[0:1, ds(e, 1)], min_val=0, max_val=T)

                def up_low():
                    low(1, p, 1, first_step)

                def next_gate_low():
                    next_expert(dve, pair, p, lambda: low(1, 1 - p, 0, first_step + EXPERT_STEPS))

                select(e + 1)

                def run(n):
                    if n == T:
                        dve.wait_ge(all_high, e + 1)
                        dve.tensor_tensor(hT_r[:], hT[:], xh_r, ALU.subtract).then_inc(all_low, 1)
                        up_low()
                        all_tokens(1, EXPERT_STEPS, first_step, use, p)
                        dve.wait_ge(u_full, first_step * 2 + 2 * EXPERT_STEPS)
                        dve.tensor_tensor(hT[:], hT_r[:], xh_r, ALU.add).then_inc(whole, 1)
                        dve.sem_inc(ye_dve, 1)
                        for t in range(NT):
                            dve.wait_ge(d_full, first_step * 2 + (2 * EXPERT_STEPS - 1 + t))
                            for half in range(2):
                                xt = x[:, t, half * 512:(half + 1) * 512]
                                dve.scalar_tensor_tensor(out=xt, in0=ps[:, YB[t] + half, :], scalar=gates[:, t, ds(e, 1)],
                                                         in1=xt, op0=ALU.mult, op1=ALU.add).then_inc(x_added, 1)
                        gather_low(e + 1, 1 - p)
                        next_gate_low()
                        return
                    up_low()

                    def one(s, i, step, use_, loop):
                        hidden(i, step * 2 + 2, 2, FT)

                        def next_low():
                            for kind in range(2):
                                low(1, 1 - i, kind, step + 1)
                        unless_last(dve, s, EXPERT_STEPS, loop, next_low)
                        hidden_low(i, step * 2 + 2, 2, FT)
                        low(1, i, 2, step)
                    steps(dve, one, EXPERT_STEPS, first_step, use, p)
                    gather_low(e + 1, 1 - p)
                    dve.wait_ge(d_full, first_step * 2 + 2 * EXPERT_STEPS)
                    dve.tensor_copy(ye[:, 0:512], ps[:, 6, :]).then_inc(ye_dve, 1)
                    next_gate_low()
                    for t in range(NT):
                        for half in range(2):
                            k = 2 * t + half
                            xt = x[:, t, half * 512:(half + 1) * 512]
                            dve.wait_ge(e_full, e * 4 + (k + 1))
                            dve.tensor_tensor(xt, ps[:, (4, 2 * p)[t] + half, :], xt, ALU.add).then_inc(x_added, 1)
                    dve.sem_inc(whole, 1)
                    dve.sem_inc(all_low, 1)
                by_count(dve, n_e, run)
            pairs(dve, expert)


_INS = ["x", "g_mix", "w_in", "b_f", "g_q", "g_k", "swa_sinks", "rel_bias", "g_out", "w_out", "g_ffn",
        "w_ff_gate", "w_ff_up", "w_ff_down", "w_router", "w_exp_gate", "w_exp_up", "w_exp_down"]
_OUTS = [((1, 256, 1024), "float32")]


def kernel(**inputs):
    import numpy as _np
    import concourse.bacc as _bacc
    from concourse import mybir as _mybir
    from concourse.bass_utils import run_bass_kernel_spmd as _run

    nc = _bacc.Bacc("TRN2", target_bir_lowering=False, num_devices=1)
    arrays, args = {}, []
    given = {name: inputs[name] for name in _INS}
    given["consts"] = shape_constants()
    for name, value in given.items():
        a = _np.ascontiguousarray(value)
        arrays[f"in_{name}_dram"] = a
        args.append(nc.dram_tensor(f"in_{name}_dram", a.shape, _mybir.dt.from_np(a.dtype), kind="ExternalInput").ap())
    for i, (shape, dtype) in enumerate(_OUTS):
        dt = _mybir.dt.from_np(_np.dtype(dtype))
        args.append(nc.dram_tensor(f"out_{i}_dram", shape, dt, kind="ExternalOutput").ap())
    trunk(nc, *args)
    r = _run(nc, [arrays], core_ids=[0])
    got = tuple(r.results[0][f"out_{i}_dram"] for i in range(len(_OUTS)))
    return got[0]
```
